# Optimizing a Trainium2 kernel written in Bass

```python
import jax, jax.numpy as jnp
from jax import lax
import numpy as np

D_MODEL = 1024
BATCH = 1
SEQ = 128
DEPTH = 2
DEC_BATCH = 1
DEC_SEQ = 512
PAST_LEN = 128

GRID_W = 64
N_EVEN = (DEPTH + 1) // 2
N_ODD = DEPTH // 2
EPS = 1e-6
CONV_DIM = D_MODEL // 2
CONV_WIDTH = 31
RET_HEADS = 4
RET_DK = D_MODEL // 8
RET_DV = 2 * RET_DK
RET_CHUNK = 128
N_Q_HEADS = 8
N_KV_HEADS = 2
HEAD_DIM = D_MODEL // N_Q_HEADS
ROPE_THETA = 10000.0
Q_BLOCK = 128
D_FF = 4 * D_MODEL
EVEN_SPLIT_SIZES = (CONV_DIM, CONV_DIM, RET_HEADS * RET_DK, RET_HEADS * RET_DK,
                    RET_HEADS * RET_DV, RET_HEADS * RET_DV)
IN_EVEN = sum(EVEN_SPLIT_SIZES)
MIX_EVEN = CONV_DIM + RET_HEADS * RET_DV
QKV_DIM = (N_Q_HEADS + 2 * N_KV_HEADS) * HEAD_DIM

kernel_name = 'hybrid_conv_retention_gqa_dit_step'

def rmsnorm(x, g):
    xf = x.astype(jnp.float32)
    y = xf * lax.rsqrt(jnp.mean(xf * xf, axis=-1, keepdims=True) + EPS)
    return (y * g.astype(jnp.float32)).astype(x.dtype)

def layernorm_f32(x):
    mu = jnp.mean(x, axis=-1, keepdims=True)
    xc = x - mu
    return xc * lax.rsqrt(jnp.mean(xc * xc, axis=-1, keepdims=True) + EPS)

def conformer_conv(u_val, u_gate, w_dw, b_dw, ln_g, ln_b):
    z = u_val * jax.nn.sigmoid(u_gate)
    z = lax.conv_general_dilated(
        z, w_dw.astype(z.dtype)[:, None, :], window_strides=(1,),
        padding=[(CONV_WIDTH // 2, CONV_WIDTH // 2)],
        dimension_numbers=('NWC', 'WIO', 'NWC'), feature_group_count=CONV_DIM) + b_dw
    zf = layernorm_f32(z.astype(jnp.float32)) * ln_g.astype(jnp.float32) + ln_b.astype(jnp.float32)
    return jax.nn.silu(zf).astype(u_val.dtype)

def retention_scan(q, k, v, log_gamma, s0):
    B, L = q.shape[0], q.shape[1]
    n = L // RET_CHUNK

    def to_chunks(a):
        return a.reshape((B, n, RET_CHUNK) + a.shape[2:]).swapaxes(0, 1)

    pos = jnp.arange(RET_CHUNK, dtype=jnp.float32)
    rel = pos[:, None] - pos[None, :]
    intra = jnp.exp(jnp.maximum(rel, 0.0)[None] * log_gamma[:, None, None]) * (rel >= 0)[None]
    q_decay = jnp.exp((pos + 1.0)[:, None] * log_gamma[None, :])
    k_decay = jnp.exp((RET_CHUNK - 1.0 - pos)[:, None] * log_gamma[None, :])
    chunk_decay = jnp.exp(RET_CHUNK * log_gamma)

    def step(s, qkv):
        qc, kc, vc = qkv
        scores = jnp.einsum('bihd,bjhd->bhij', qc, kc) * intra
        o = (jnp.einsum('bhij,bjhe->bihe', scores, vc)
             + jnp.einsum('bihd,bhde->bihe', qc * q_decay[:, :, None], s))
        s = (s * chunk_decay[None, :, None, None]
             + jnp.einsum('bjhd,bjhe->bhde', kc * k_decay[:, :, None], vc))
        return s, o

    s_fin, o = lax.scan(step, s0, (to_chunks(q), to_chunks(k), to_chunks(v)))
    return o.swapaxes(0, 1).reshape(B, L, RET_HEADS, RET_DV), s_fin

def bi_retention(q, k, v, log_gamma2, s0):
    o_f, s_f = retention_scan(q, k, v, log_gamma2[0], s0[:, 0])
    o_b, s_b = retention_scan(q[:, ::-1], k[:, ::-1], v[:, ::-1], log_gamma2[1], s0[:, 1])
    return o_f + o_b[:, ::-1], jnp.stack([s_f, s_b], axis=1)

def even_mixer(h, w_in, w_out, w_dw, b_dw, ln_g, ln_b, log_decay, s0):
    B, L, _ = h.shape
    idx = np.cumsum(EVEN_SPLIT_SIZES)[:-1].tolist()
    u_val, u_gate, q, k, v, g = jnp.split(h @ w_in, idx, axis=-1)
    conv_out = conformer_conv(u_val, u_gate, w_dw, b_dw, ln_g, ln_b)
    qf = q.reshape(B, L, RET_HEADS, RET_DK).astype(jnp.float32) * (RET_DK ** -0.5)
    kf = k.reshape(B, L, RET_HEADS, RET_DK).astype(jnp.float32)
    vf = v.reshape(B, L, RET_HEADS, RET_DV).astype(jnp.float32)
    log_gamma = -jnp.exp(log_decay.astype(jnp.float32))
    o, s_fin = bi_retention(qf, kf, vf, log_gamma, s0.astype(jnp.float32))
    o = layernorm_f32(o).reshape(B, L, RET_HEADS * RET_DV)
    ret_out = (jax.nn.silu(g.astype(jnp.float32)) * o).astype(h.dtype)
    y = jnp.concatenate([conv_out, ret_out], axis=-1) @ w_out
    return y, s_fin.astype(h.dtype)

def gqa_project(h, w_qkv, q_g, k_g):
    B, L, _ = h.shape
    q, k, v = jnp.split(h @ w_qkv, [N_Q_HEADS * HEAD_DIM, (N_Q_HEADS + N_KV_HEADS) * HEAD_DIM], axis=-1)
    q = rmsnorm(q.reshape(B, L, N_Q_HEADS, HEAD_DIM), q_g)
    k = rmsnorm(k.reshape(B, L, N_KV_HEADS, HEAD_DIM), k_g)
    return q, k, v.reshape(B, L, N_KV_HEADS, HEAD_DIM)

def axial_rope_tables(L):
    n_rows = L // GRID_W
    rows = jnp.repeat(jnp.arange(n_rows), GRID_W).astype(jnp.float32)
    cols = jnp.tile(jnp.arange(GRID_W), n_rows).astype(jnp.float32)
    half = HEAD_DIM // 2
    inv = ROPE_THETA ** (-jnp.arange(0, half, 2, dtype=jnp.float32) / half)
    ang = jnp.concatenate([rows[:, None] * inv, cols[:, None] * inv], axis=-1)
    return jnp.cos(ang), jnp.sin(ang)

def apply_rope(x, cos, sin):
    xf = x.astype(jnp.float32).reshape(x.shape[:-1] + (HEAD_DIM // 2, 2))
    x1, x2 = xf[..., 0], xf[..., 1]
    c, s = cos[None, :, None, :], sin[None, :, None, :]
    out = jnp.stack([x1 * c - x2 * s, x1 * s + x2 * c], axis=-1)
    return out.reshape(x.shape).astype(x.dtype)

def blocked_attention(q, k, v):
    B, Sq = q.shape[0], q.shape[1]
    G = N_Q_HEADS // N_KV_HEADS
    nb = Sq // Q_BLOCK
    qb = q.reshape(B, nb, Q_BLOCK, N_KV_HEADS, G, HEAD_DIM).swapaxes(0, 1)
    scale = HEAD_DIM ** -0.5

    def one_block(qi):
        s = jnp.einsum('bqhgd,bkhd->bhgqk', qi, k, preferred_element_type=jnp.float32) * scale
        p = jax.nn.softmax(s, axis=-1)
        return jnp.einsum('bhgqk,bkhd->bqhgd', p.astype(v.dtype), v)

    o = lax.map(one_block, qb)
    return o.swapaxes(0, 1).reshape(B, Sq, N_Q_HEADS * HEAD_DIM)

def trunk(x, cond, ctx_ret, ctx_k, ctx_v, weights):
    (ada_w, ada_b, norm_g, final_g, even_w_in, even_w_out, conv_dw_w, conv_dw_b,
     conv_ln_g, conv_ln_b, ret_log_decay, odd_w_qkv, odd_q_g, odd_k_g, odd_w_o,
     mlp_w1, mlp_w2) = weights
    is_ctx = ctx_ret is None
    B, L, _ = x.shape
    if not is_ctx:
        cos, sin = axial_rope_tables(L)
    new_ret, new_k, new_v = [], [], []
    for layer in range(DEPTH):
        m = jax.nn.silu(cond) @ ada_w[layer] + ada_b[layer]
        m = m.reshape(m.shape[:-1] + (1, 6, D_MODEL))
        sh1, sc1, g1, sh2, sc2, g2 = (m[..., i, :] for i in range(6))
        h = rmsnorm(x, norm_g[layer, 0]) * (1 + sc1) + sh1
        li = layer // 2
        if layer % 2 == 0:
            if is_ctx:
                s0 = jnp.zeros((B, 2, RET_HEADS, RET_DK, RET_DV), jnp.float32)
            else:
                s0 = ctx_ret[:, li]
            y, s_fin = even_mixer(h, even_w_in[li], even_w_out[li], conv_dw_w[li], conv_dw_b[li],
                                  conv_ln_g[li], conv_ln_b[li], ret_log_decay[li], s0)
            new_ret.append(s_fin)
        else:
            q, k, v = gqa_project(h, odd_w_qkv[li], odd_q_g[li], odd_k_g[li])
            if is_ctx:
                new_k.append(k)
                new_v.append(v)
                keys, vals = k, v
            else:
                q = apply_rope(q, cos, sin)
                k = apply_rope(k, cos, sin)
                keys = jnp.concatenate([ctx_k[:, li].astype(k.dtype), k], axis=1)
                vals = jnp.concatenate([ctx_v[:, li].astype(v.dtype), v], axis=1)
            y = blocked_attention(q, keys, vals) @ odd_w_o[li]
        x = x + g1 * y
        h = rmsnorm(x, norm_g[layer, 1]) * (1 + sc2) + sh2
        x = x + g2 * (jnp.square(jax.nn.relu(h @ mlp_w1[layer])) @ mlp_w2[layer])
    return rmsnorm(x, final_g), new_ret, new_k, new_v

def setup_inputs(seed: int = 0) -> dict:
    key = jax.random.key(seed)
    ks = jax.random.split(key, 32)
    f32 = jnp.float32

    def nrm(k, shape, fan_in):
        return jax.random.normal(k, shape, f32) * (fan_in ** -0.5)

    def noise(k, shape, s):
        return jax.random.normal(k, shape, f32) * s

    base_decay = jnp.log(-jnp.log1p(-(2.0 ** (-5.0 - jnp.arange(RET_HEADS, dtype=f32)))))
    return {
        'x_prompt': jax.random.normal(ks[0], (BATCH, SEQ, D_MODEL), f32),
        'x_sample': jax.random.normal(ks[1], (DEC_BATCH, DEC_SEQ, D_MODEL), f32),
        'state_ret': jax.random.normal(ks[2], (DEC_BATCH, N_EVEN, 2, RET_HEADS, RET_DK, RET_DV), f32),
        'cache_k': jax.random.normal(ks[3], (DEC_BATCH, N_ODD, PAST_LEN, N_KV_HEADS, HEAD_DIM), f32),
        'cache_v': jax.random.normal(ks[4], (DEC_BATCH, N_ODD, PAST_LEN, N_KV_HEADS, HEAD_DIM), f32),
        'c': jax.random.normal(ks[5], (DEC_BATCH, D_MODEL), f32),
        'c_ctx': jax.random.normal(ks[6], (D_MODEL,), f32),
        'ada_w': nrm(ks[7], (DEPTH, D_MODEL, 6 * D_MODEL), D_MODEL) * 0.5,
        'ada_b': noise(ks[8], (DEPTH, 6 * D_MODEL), 0.01),
        'norm_g': 1.0 + noise(ks[9], (DEPTH, 2, D_MODEL), 0.05),
        'final_g': 1.0 + noise(ks[10], (D_MODEL,), 0.05),
        'even_w_in': nrm(ks[11], (N_EVEN, D_MODEL, IN_EVEN), D_MODEL),
        'even_w_out': nrm(ks[12], (N_EVEN, MIX_EVEN, D_MODEL), MIX_EVEN),
        'conv_dw_w': nrm(ks[13], (N_EVEN, CONV_WIDTH, CONV_DIM), CONV_WIDTH),
        'conv_dw_b': noise(ks[14], (N_EVEN, CONV_DIM), 0.01),
        'conv_ln_g': 1.0 + noise(ks[15], (N_EVEN, CONV_DIM), 0.05),
        'conv_ln_b': noise(ks[16], (N_EVEN, CONV_DIM), 0.01),
        'ret_log_decay': base_decay[None, None, :] + noise(ks[17], (N_EVEN, 2, RET_HEADS), 0.1),
        'odd_w_qkv': nrm(ks[18], (N_ODD, D_MODEL, QKV_DIM), D_MODEL),
        'odd_q_g': 1.0 + noise(ks[19], (N_ODD, HEAD_DIM), 0.05),
        'odd_k_g': 1.0 + noise(ks[20], (N_ODD, HEAD_DIM), 0.05),
        'odd_w_o': nrm(ks[21], (N_ODD, N_Q_HEADS * HEAD_DIM, D_MODEL), N_Q_HEADS * HEAD_DIM),
        'mlp_w1': nrm(ks[22], (DEPTH, D_MODEL, D_FF), D_MODEL),
        'mlp_w2': nrm(ks[23], (DEPTH, D_FF, D_MODEL), D_FF),
    }

def reference(x_prompt, x_sample, state_ret, cache_k, cache_v, c, c_ctx,
              ada_w, ada_b, norm_g, final_g, even_w_in, even_w_out, conv_dw_w, conv_dw_b,
              conv_ln_g, conv_ln_b, ret_log_decay, odd_w_qkv, odd_q_g, odd_k_g, odd_w_o,
              mlp_w1, mlp_w2):
    weights = (ada_w, ada_b, norm_g, final_g, even_w_in, even_w_out, conv_dw_w, conv_dw_b,
               conv_ln_g, conv_ln_b, ret_log_decay, odd_w_qkv, odd_q_g, odd_k_g, odd_w_o,
               mlp_w1, mlp_w2)
    y_prompt, ret_list, k_list, v_list = trunk(x_prompt, c_ctx, None, None, None, weights)
    new_state_ret = jnp.stack(ret_list, axis=1)
    new_cache_k = jnp.stack(k_list, axis=1)
    new_cache_v = jnp.stack(v_list, axis=1)
    y_sample, _, _, _ = trunk(x_sample, c, state_ret, cache_k, cache_v, weights)
    return (y_prompt, y_sample, new_state_ret, new_cache_k, new_cache_v)


_drawn_inputs = setup_inputs


def setup_inputs(seed=0):
    import zlib

    import numpy as np

    out = dict(_drawn_inputs(seed))
    spreads = {}
    factors = {'state_ret': 8.0,
     'cache_k': 8.0,
     'cache_v': 6.737,
     'conv_dw_b': 8.0,
     'conv_ln_g': 8.0,
     'conv_ln_b': 8.0,
     'odd_q_g': 8.0}
    for name, (base, spread) in spreads.items():
        noise = np.random.default_rng([zlib.crc32(name.encode()), seed]).standard_normal(out[name].shape)
        drawn = base * np.exp(spread * noise) if base else spread * noise
        out[name] = __import__('jax').numpy.asarray(drawn.astype(out[name].dtype))
    for name, factor in factors.items():
        out[name] = (out[name] * factor).astype(out[name].dtype)
    return out
```

```python
from contextlib import ExitStack

import numpy as np

import concourse.bass as bass
from concourse import mybir

F32, F32R = mybir.dt.float32, mybir.dt.float32r
ALU, ACT = mybir.AluOpType, mybir.ActivationFunctionType
AX_X = mybir.AxisListType.X

P = 128
D = 1024
KC = D // P
LAT, CTX = 512, 128
T = LAT + CTX
HALF = T // 2
NT = T // P
CTX_TILE = 2
LAT_TILES = (0, 1, 3, 4)
EPS = 1e-6
CONV, WIDTH = 512, 31
CC = CONV // P
PAD = WIDTH // 2
ZW = PAD + LAT + PAD + CTX + PAD
CW = LAT + PAD + CTX
RH, RV = 4, 256
QH, KVH = 8, 2
GRP = QH // KVH
FF = 4 * D
FG = FF // D
GRID_W = 64
ATT_SCALE = float(P) ** -0.5
RET_SCALE = float(P) ** -0.5
KEYS = P + LAT

PAIRS = {"half": [(h, p) for h in range(2) for p in range(4)],
         "tile": [(h, p) for p in range(4) for h in range(2)],
         "wc": [(h, 2 * t + p) for t in range(2) for h in range(2) for p in range(2)]}
SUM_AT = {k: [sum(1 if p == 0 else 2 for _, p in v[:n + 1]) for n in range(8)] for k, v in PAIRS.items()}
SUMS = 14
CONV_MAP = ((0, 0, 256), (LAT + PAD, 256, CTX), (256, 384, 256))

SEGS = (((0, 256, 0), (256, 64, 1)), ((320, 64, 1), (384, 256, 0)))

T_GATE, T_VAL, T_HEADS = 0, 2, 4
T_WR = T_HEADS + 12
T_WC = T_WR + 4
T_MLP0 = T_WC + 2
T_QKV = T_MLP0 + 8 * FG
T_WO = T_QKV + 6
T_MLP1 = T_WO + 4
N_TILES = T_MLP1 + 8 * FG

G_X = 0
G_GATE = 16
G_VAL = G_GATE + 8
G_HEADS = G_VAL + 8
G_PAIR = 28
G_RT = G_HEADS + 2 * G_PAIR
G_WR = G_RT + 16
G_WC = G_WR + 16
G_MLP0 = G_WC + 16
G_QKV = G_MLP0 + 32 * FG
G_WO = G_QKV + 30
G_MLP1 = G_WO + 16
A_HEADS, A_MLP0 = 8, 8 + 2 * G_PAIR
A_QKV = A_MLP0 + 16 * FG
A_MLP1 = A_QKV + 30
V_VAL, V_RT, V_WR, V_WC, V_MLP0 = 16, 24, 40, 56, 72
V_WO = V_MLP0 + 16 * FG
V_MLP1 = V_WO + 16
NAT_BANKS = (0, 1, 2, 3, 7)

N_MOD = 96
SH1, SC1, G1, SH2, SC2, G2 = (8 * s for s in range(6))
MOD1 = 48

R_C, R_NORM, R_FINAL, R_CB, R_LG, R_LB, R_END = 0, 16, 48, 56, 60, 64, 68

C_ID, C_PF, C_PB, C_QF, C_QB, C_KP, C_SEL = 0, 128, 256, 384, 512, 640, 642
C_END = 644


def shape_constants():
    c = np.zeros((P, C_END), np.float32)
    i, j = np.arange(P)[None, :], np.arange(P)[:, None]
    c[:, C_ID:C_ID + P] = np.eye(P)
    c[:, C_PF:C_PF + P] = np.maximum(i - j, 0)
    c[:, C_PB:C_PB + P] = np.maximum(j - i, 0)
    c[:, C_QF:C_QF + P] = i + 1
    c[:, C_QB:C_QB + P] = P - i
    c[:, C_KP] = P - 1 - np.arange(P)
    c[:, C_KP + 1] = np.arange(P)
    for s in range(4):
        c[32 * s, C_SEL] = c[32 * s + 1, C_SEL + 1] = 1
    half = P // 2
    pos = np.arange(LAT)
    inv = (np.float32(10000.0) ** (-np.arange(0, half, 2, dtype=np.float32) / half)).astype(np.float32)
    ang = np.concatenate([(pos // GRID_W).astype(np.float32)[:, None] * inv,
                          (pos % GRID_W).astype(np.float32)[:, None] * inv], axis=1)
    rope = np.zeros((P, 2, NT, half), np.float32)
    rope[:, 0, CTX_TILE] = 1.0
    for n, tile in enumerate(LAT_TILES):
        rope[:, 0, tile] = np.cos(ang[n * P:(n + 1) * P].astype(np.float64))
        rope[:, 1, tile] = np.sin(ang[n * P:(n + 1) * P].astype(np.float64))
    return c, rope


def hybrid_step(nc, x_prompt, x_sample, state_ret, cache_k, cache_v, c, c_ctx, ada_w, ada_b, norm_g,
                final_g, even_w_in, even_w_out, conv_dw_w, conv_dw_b, conv_ln_g, conv_ln_b,
                ret_log_decay, odd_w_qkv, odd_q_g, odd_k_g, odd_w_o, mlp_w1, mlp_w2,
                shape_const, rope_const, y_prompt, y_sample, new_state, new_k, new_v):
    ctx = ExitStack()
    with ctx:
        here = [(nc.sbuf_base + 31) // 32 * 32]

        def place(name, shape, dt=F32):
            at = here[0]
            here[0] += (int(np.prod(shape[1:])) * 4 + 31) // 32 * 32
            return nc.alloc_sbuf_tensor_at(name, shape, dt, offset=at)

        xT = place("xT", [P, KC, T])
        hH = place("hH", [P, KC, T], F32R)
        hL = place("hL", [P, KC, T], F32R)
        raw = place("raw", [P, 2, 1024])
        wH = place("wH", [P, 2, 2048], F32R)
        wL = place("wL", [P, 2, 2048], F32R)
        ada = place("ada", [P, 2, KC, P])
        const = place("const", [P, C_END])
        ones = place("ones", [P, P])
        eps = place("eps", [P, 1])
        vecT = place("vecT", [P, 3, P])
        siluc = place("siluc", [P, KC, 32])
        ada_sb = place("ada_sb", [P, P])
        modT = place("modT", [P, N_MOD, 2])
        coef = place("coef", [P, 4, KC, 2])
        norm_buffers = here[0]
        ssum = place("ssum", [P, 2, HALF])
        rstd = place("rstd", [P, 2, HALF])
        ub = place("ub", [P, 2, HALF])
        sqb = place("sqb", [P, 2, HALF])
        tb = place("tb", [P, 2, HALF])
        lg = place("lg", [P, 2, RH])
        kdec = place("kdec", [P, 2, RH])
        cdec = place("cdec", [P, 2, RH])
        arena = here[0]

        x_nat = place("x_nat", [P, NT, D])
        rows = place("rows", [P, 3, P])
        here[0] = arena
        ret = place("ret", [P, NT, RH * RV])
        zp = place("zp", [P, CC, ZW])
        cacc = place("cacc", [P, CC, CW])
        head_arena = here[0]
        qT = place("qT", [P, 2, T])
        kT = place("kT", [P, 2, T])
        v_nat = place("v_nat", [P, NT, RV])
        gate = place("gate", [P, NT, RV])
        qdec = place("qdec", [P, 2, T])
        kd_nat = place("kd_nat", [P, 2, NT, P])
        S = place("S", [P, 2, 4, RV])
        here[0] = norm_buffers
        dmat = place("dmat", [P, 2, P])
        qtab = place("qtab", [P, 2, P])
        here[0] = norm_buffers + 4 * T
        state_out = place("state_out", [P, 2, RV])
        bst = place("bst", [P, NT, 6])
        bmv = place("bmv", [P, NT, 2])
        brs = place("brs", [P, NT, 1])
        here[0] = norm_buffers + 8 * T
        prob = place("prob", [P, T])
        sgate = nc.alloc_sbuf_tensor_at("sgate", [P, CC, T], F32, offset=arena)
        here[0] = head_arena
        cH = place("cH", [P, CC, T], F32R)
        cL = place("cL", [P, CC, T], F32R)
        cst = place("cst", [P, 2, T])
        cmp_ = place("cmp", [P, 2, T])
        here[0] = arena
        fH = place("fH", [P, KC, T], F32R)
        fL = place("fL", [P, KC, T], F32R)
        fr = place("fr", [P, 2, HALF])
        fs = place("fs", [P, 2, HALF])
        here[0] = arena
        q_nat = place("q_nat", [P, 2, NT, RV])
        k_nat = place("k_nat", [P, NT, RV])
        va = place("va", [P, NT + 1, RV])
        kc_nat = place("kc_nat", [P, RV])
        kro = place("kro", [P, NT, RV])
        qro = place("qro", [P, NT, RV])
        rtmp = place("rtmp", [P, 2, NT, 2, 64])
        rn = place("rn", [P, NT, RV])
        rss = place("rss", [P, NT * 2])
        tabs = place("tabs", [P, 2, 4, NT, 64])
        rope_sb = nc.alloc_sbuf_tensor_at("rope_sb", [P, 2, NT, 64], F32, offset=here[0])
        gqk = nc.alloc_sbuf_tensor_at("gqk", [P, 2, P], F32, offset=here[0] + 2 * NT * 64 * 4)
        kTa = place("kTa", [P, KVH, P + KEYS])
        qTa = place("qTa", [P, QH, T])
        here[0] = arena
        pr = place("pr", [P, 2, KEYS])
        pT = nc.alloc_sbuf_tensor_at("pT", [P, NT, LAT], F32,
                                     offset=arena + 2 * NT * RV * 4 + NT * RV * 4 + (NT + 1) * RV * 4 + RV * 4)
        amx = place("amx", [P, 2, 4])
        asum = place("asum", [P, 2, 4])
        here[0] = arena
        y_nat = place("y_nat", [P, NT, D])

        ident = const[:, C_ID:C_ID + P]
        sel = const[:, C_SEL:C_SEL + 2]

        ps = ctx.enter_context(nc.psum_tensor("ps", [P, 8, 512], F32))
        B_ADA = 4

        def sem(name):
            return ctx.enter_context(nc.semaphore(name))

        rows_in, const_in, x_in = sem("rows_in"), sem("const_in"), sem("x_in")
        raw_in = [sem("raw_in0"), sem("raw_in1")]
        ada_in = [sem("ada_in0"), sem("ada_in1")]
        s0_in, att_in, store = sem("s0_in"), sem("att_in"), sem("store")
        act_dma, k_st, v_st = sem("act_dma"), sem("k_st"), sem("v_st")
        wh_done, wl_done = sem("wh_done"), sem("wl_done")
        acc_full, act_free, dve_free = sem("acc_full"), sem("act_free"), sem("dve_free")
        set_up, rows_full, rows_out, siluc_ready = sem("set_up"), sem("rows_full"), sem("rows_out"), sem("siluc_ready")
        ada_strips, ada_ev, ada_fin, mod_done = sem("ada_strips"), sem("ada_ev"), sem("ada_fin"), sem("mod_done")
        coef_done = sem("coef_done")
        sq_done, sum_done, stat_full, std_done = sem("sq_done"), sem("sum_done"), sem("stat_full"), sem("std_done")
        rstd_done, u_done, t_done, hh_done, h_ready = (sem("rstd_done"), sem("u_done"), sem("t_done"),
                                                       sem("hh_done"), sem("h_ready"))
        conv_done, cn_sum, csum_done, crec_done = sem("conv_done"), sem("cn_sum"), sem("csum_done"), sem("crec_done")
        cstat_in, cstat_full, csq_done, cstd_done = sem("cstat_in"), sem("cstat_full"), sem("csq_done"), sem("cstd_done")
        cx_done, cn_done, csilu_done, ch_done, cl_done = (sem("cx_done"), sem("cn_done"), sem("csilu_done"),
                                                          sem("ch_done"), sem("cl_done"))
        lg_raw, lg_done, dec_done = sem("lg_raw"), sem("lg_done"), sem("dec_done")
        dexp_done, dm_done = sem("dexp_done"), sem("dm_done")
        st_full, prob_done, qdec_done, kd_done = sem("st_full"), sem("prob_done"), sem("qdec_done"), sem("kd_done")
        u_full, s_done, so_done, o_full, o_out = sem("u_full"), sem("s_done"), sem("so_done"), sem("o_full"), sem("o_out")
        bn_done, bstd_done, brs_done, on_done, ret_done = (sem("bn_done"), sem("bstd_done"), sem("brs_done"),
                                                           sem("on_done"), sem("ret_done"))
        rth_done = sem("rth_done")
        fr_done, fs_done, fh_done, f_ready = sem("fr_done"), sem("fs_done"), sem("fh_done"), sem("f_ready")
        tab_done, rsq_done, rss_done, rstd2, rrec = sem("tab_done"), sem("rsq_done"), sem("rss_done"), sem("rstd2"), sem("rrec")
        rn_done, rm_done, ro_done = sem("rn_done"), sem("rm_done"), sem("ro_done")
        tr_full, tr_out = sem("tr_full"), sem("tr_out")
        sc_full, mx_done, nmx_done, ex_done = sem("sc_full"), sem("mx_done"), sem("nmx_done"), sem("ex_done")
        rc_done, pn_done, pt_full, pt_act, pt_dve = (sem("rc_done"), sem("pn_done"), sem("pt_full"),
                                                     sem("pt_act"), sem("pt_dve"))
        pv_full, ah_done, attn_ready = sem("pv_full"), sem("ah_done"), sem("attn_ready")
        y_done, y_full, y_act, y_dve = sem("y_done"), sem("y_full"), sem("y_act"), sem("y_dve")

        block = ctx.enter_context(nc.Block())

        @block.sync
        def _(sp):
            def cols(w, k0, nk, c0, n):
                return w[k0 * P:(k0 + nk) * P, bass.ds(c0, n)].rearrange("(k p) n -> p k n", p=P)

            def load_tile(t, halves, first=False):
                for j, src in enumerate(halves):
                    if not first:
                        sp.wait_ge(wl_done, 2 * t - 1 + j)
                    n = src.shape[2]
                    sp.dma_start(raw[:, j, :].rearrange("p (k n) -> p k n", n=n), src).then_inc(raw_in[j], 16)

            def k8(w, c0, row0=0):
                return [w[row0 + 512 * j:row0 + 512 * (j + 1), bass.ds(c0, 256)]
                        .rearrange("(k p) n -> p k n", p=P) for j in range(2)]

            def load_ada(n, slot, layer, col, first=False):
                if not first:
                    sp.wait_ge(ada_strips, n - 1)
                sp.dma_start(ada[:, slot], ada_w[layer, :, bass.ds(col, P)]
                             .rearrange("(k p) n -> p k n", p=P)).then_inc(ada_in[slot], 16)

            vec = lambda a: a.rearrange("(r p) -> r p", p=P)
            sp.dma_start(rows[0:8, 0, :], vec(c[0])).then_inc(rows_in, 16)
            sp.dma_start(rows[8:16, 0, :], vec(c_ctx)).then_inc(rows_in, 16)
            sp.dma_start(rows[R_NORM:R_FINAL, 0, :], norm_g.rearrange("l i (r p) -> (l i r) p", p=P)).then_inc(rows_in, 16)
            sp.dma_start(rows[R_FINAL:R_CB, 0, :], vec(final_g)).then_inc(rows_in, 16)
            sp.dma_start(rows[R_CB:R_LG, 0, :], vec(conv_dw_b[0])).then_inc(rows_in, 16)
            sp.dma_start(rows[R_LG:R_LB, 0, :], vec(conv_ln_g[0])).then_inc(rows_in, 16)
            sp.dma_start(rows[R_LB:R_END, 0, :], vec(conv_ln_b[0])).then_inc(rows_in, 16)
            sp.dma_start(rows[0:N_MOD, 1, :], ada_b.rearrange("l (r p) -> (l r) p", p=P)).then_inc(rows_in, 16)
            sp.dma_start(rows[0:WIDTH * CC, 2, :], conv_dw_w[0].rearrange("w (r p) -> (w r) p", p=P)).then_inc(rows_in, 16)
            sp.dma_start(const[:], shape_const).then_inc(const_in, 16)
            load_ada(0, 0, 0, 0, first=True)
            load_ada(1, 1, 0, P, first=True)
            for n, tile in enumerate(LAT_TILES):
                sp.dma_start(x_nat[:, tile, :], x_sample[0, n * P:(n + 1) * P, :]).then_inc(x_in, 16)
            sp.dma_start(x_nat[:, CTX_TILE, :], x_prompt[0]).then_inc(x_in, 16)
            for n in range(2, 16):
                load_ada(n, n % 2, 0, n * P)
                if n == 8:
                    load_tile(0, k8(even_w_in[0], CONV), first=True)
            for t in range(4):
                if t:
                    load_tile(t, k8(even_w_in[0], (CONV, CONV + 256, 0, 256)[t]))
                for a in range(2):
                    load_ada(16 + 2 * t + a, a, 0, (16 + 2 * t + a) * P)
            with sp.Fori(0, 2) as i:
                for b in range(6):
                    col = (1024 + 256 * i, 1536 + 256 * i, 2048 + 512 * i, 3072 + 512 * i,
                           2304 + 512 * i, 3328 + 512 * i)[b]
                    load_tile(T_HEADS + 6 * i + b, k8(even_w_in[0], col))
                    for a in range(2):
                        n = 24 + 12 * i + 2 * b + a
                        load_ada(n, a, 0, n * P)
                    if b in (2, 5):
                        head = 2 * i + (b == 5)
                        sp.wait_ge(acc_full, G_HEADS + G_PAIR * i + (17 if b == 5 else -1))
                        for r in range(2):
                            sp.dma_start(S[:, r, 3 * r, :], state_ret[0, 0, r, bass.ds(head, 1)]
                                         .rearrange("a d e -> (a d) e")).then_inc(s0_in, 16)
            for t in range(4):
                load_tile(T_WR + t, k8(even_w_out[0], 256 * t, CONV))
            for t in range(2):
                load_tile(T_WC + t, [even_w_out[0, 256 * j:256 * (j + 1), 512 * t:512 * (t + 1)]
                                     .rearrange("(k p) n -> p k n", p=P) for j in range(2)])

            def load_mlp(layer, first_tile):
                with sp.Fori(0, FG) as g:
                    for b in range(8):
                        if b < 4:
                            halves = k8(mlp_w1[layer], 1024 * g + 256 * b)
                        else:
                            halves = [mlp_w2[layer, bass.ds(1024 * g + 512 * j, 512), 256 * (b - 4):256 * (b - 3)]
                                      .rearrange("(k p) n -> p k n", p=P) for j in range(2)]
                        load_tile(first_tile + 8 * g + b, halves)
                        if layer == 0:
                            for q in ((2 * b, 2 * b + 1) if b < 4 else (4 + b,)):
                                load_ada(MOD1 + 12 * g + q, q % 2, 1, (12 * g + q) * P)

            load_mlp(0, T_MLP0)
            sp.dma_start(rope_sb[:], rope_const).then_inc(att_in, 16)
            sp.dma_start(gqk[:, 0, :], odd_q_g[0].partition_broadcast(P)).then_inc(att_in, 16)
            sp.dma_start(gqk[:, 1, :], odd_k_g[0].partition_broadcast(P)).then_inc(att_in, 16)
            load_tile(T_QKV, k8(odd_w_qkv[0], 1024))
            load_tile(T_QKV + 1, k8(odd_w_qkv[0], 0))
            sp.wait_ge(acc_full, G_QKV)
            sp.dma_start(kc_nat[:], cache_k[0, 0].rearrange("t h d -> t (h d)")).then_inc(att_in, 16)
            sp.dma_start(va[:, NT, :], cache_v[0, 0].rearrange("t h d -> t (h d)")).then_inc(att_in, 16)
            for t in range(2, 6):
                load_tile(T_QKV + t, k8(odd_w_qkv[0], (256, 512, 768, 1280)[t - 2]))
            for t in range(2):
                load_tile(T_WO + t, k8(odd_w_o[0], 256 * t))
            sp.wait_ge(ro_done, 2)
            sp.dma_start(new_k[0, 0].rearrange("t h d -> t (h d)"), kro[:, CTX_TILE, :]).then_inc(k_st, 16)
            sp.wait_ge(act_free, A_QKV + 30)
            sp.dma_start(new_v[0, 0].rearrange("t h d -> t (h d)"), va[:, CTX_TILE, :]).then_inc(v_st, 16)
            for t in range(2, 4):
                load_tile(T_WO + t, k8(odd_w_o[0], 256 * t))
            load_mlp(1, T_MLP1)
            for tile in range(NT):
                sp.wait_ge(y_act, tile + 1)
                sp.wait_ge(y_dve, tile + 1)
                if tile == CTX_TILE:
                    dst = y_prompt[0]
                else:
                    n = LAT_TILES.index(tile)
                    dst = y_sample[0, n * P:(n + 1) * P, :]
                sp.dma_start(dst, y_nat[:, tile, :]).then_inc(store, 16)
            sp.wait_ge(store, 16 * NT)
            sp.wait_ge(k_st, 16)
            sp.wait_ge(v_st, 16)
            sp.wait_ge(act_dma, 16 * (RH + 1))

        @block.tensor
        def _(pe):
            def product(bank, lhs, rhs, nk, waits=None, width=HALF):
                last = None
                for k in range(nk):
                    if waits:
                        waits(k)
                    (aH, aL), (bH, bL) = lhs(k), rhs(k)
                    for p_, (a_, b_) in enumerate(((aH, bH), (aH, bL), (aL, bH))):
                        last = nc.tensor.matmul(ps[:, bank, 0:width], a_, b_, start=(k == 0 and p_ == 0),
                                                stop=(k == nk - 1 and p_ == 2))
                last.then_inc(acc_full, 1)

            def w_wait(t, k, nk):
                if k == 0:
                    pe.wait_ge(wl_done, 2 * t + 1)
                elif k == nk // 2:
                    pe.wait_ge(wl_done, 2 * t + 2)

            def tile_t(t, slot, xH, xL, free, x_wait=None, hooks=None, nk=KC, nm=2, bank0=0):
                for half in range(2):
                    for m in range(nm):
                        n = half * nm + m
                        free(n)

                        def waits(k, n=n, half=half, m=m):
                            if n == 0:
                                w_wait(t, k, nk)
                            if x_wait and m == 0:
                                x_wait(half, k)
                        wv = [w[:, slot, :].rearrange("p (k n) -> p k n", k=nk) for w in (wH, wL)]
                        product((bank0 + n) % 4, lambda k: [w[:, k, m * P:(m + 1) * P] for w in wv],
                                lambda k: [x[:, k, half * HALF:(half + 1) * HALF] for x in (xH, xL)], nk, waits)
                        if hooks and n in hooks:
                            for hook in hooks[n]:
                                hook()

            def tile_n(t, slot, free, banks, x_wait=None, hooks=None):
                wv = [w[:, slot, :].rearrange("p (k n) -> p k n", k=KC) for w in (wH, wL)]
                for n in range(NT):
                    free(n)

                    def waits(k, n=n):
                        if n == 0:
                            w_wait(t, k, KC)
                        if x_wait and n in (0, 2):
                            x_wait(n // 2, k)
                    product(banks[n], lambda k: [x[:, k, n * P:(n + 1) * P] for x in (hH, hL)],
                            lambda k: [w[:, k, :] for w in wv], KC, waits, width=256)
                    if hooks and n in hooks:
                        for hook in hooks[n]:
                            hook()

            def strips(n, slot, full):
                pe.wait_ge(ada_in[slot], full)
                if not (isinstance(n, int) and n == 0):
                    pe.wait_ge(mod_done, n)
                for k in range(KC):
                    j = k % 4
                    last = nc.tensor.matmul(ps[32 * j:32 * j + 32, B_ADA, 0:P], siluc[:, k, :], ada[:, slot, k, :],
                                            start=(k < 4), stop=(k >= 4), tile_position=(0, 32 * j))
                last.then_inc(ada_strips, 1)

            def finish(n):
                pe.wait_ge(ada_ev, n + 1)
                nc.tensor.matmul(ps[:, B_ADA, 256:258], ada_sb[:], sel, start=True, stop=True).then_inc(ada_fin, 1)

            def ada_hooks(n, count=2, full=None):
                full = full or (lambda q: 16 * (q // 2 + 1))
                out = {}
                for a in range(count):
                    out.setdefault(2 * a, []).append(lambda a=a: strips(n + a, a, full(a)))
                    out.setdefault(2 * a + 1, []).append(lambda a=a: finish(n + a))
                return out

            def stat(norm, half, count):
                pe.wait_ge(sum_done, SUMS * norm + count)
                nc.tensor.matmul(ps[:, 5 + half, 0:HALF], ones[:], ssum[:, half, :], start=True,
                                 stop=True).then_inc(stat_full, 1)

            def h_wait(norm):
                return lambda half, k: pe.wait_ge(h_ready, 16 * norm + 8 * half + k + 1)

            def turn(bank, src, col0):
                def one(tile, p0, np_, at, last=False):
                    return nc.tensor.transpose(ps[:, bank, at:at + np_], src[p0:p0 + np_, tile, col0:col0 + P],
                                               ident[p0:p0 + np_, p0:p0 + np_])
                return one

            def turn_half(bank, src, col0, half):
                one = turn(bank, src, col0)
                if half == 0:
                    one(0, 0, P, 0)
                    one(1, 0, P, P)
                    last = one(CTX_TILE, 0, 64, 256)
                else:
                    one(CTX_TILE, 64, 64, 0)
                    one(3, 0, P, 64)
                    last = one(4, 0, P, 192)
                last.then_inc(acc_full, 1)

            pe.wait_ge(const_in, 16)
            pe.wait_ge(rows_in, 9 * 16)
            for r, nr in enumerate((R_END, N_MOD, WIDTH * CC)):
                nc.tensor.transpose(ps[:, 5 + r, 0:nr], rows[0:nr, r, :], ident[0:nr, 0:nr]).then_inc(rows_full, 1)
            pe.wait_ge(siluc_ready, 1)
            pe.wait_ge(x_in, 16 * NT)

            def x_group(n):
                if n >= 4:
                    pe.wait_ge(dve_free, n - 3)
                turn_half(n % 4, x_nat, (n % 8) * P, n // 8)

            for n in range(16):
                strips(n, n % 2, 16 * (n // 2 + 1))
                x_group(n)
                finish(n)
            stat(0, 0, SUM_AT["half"][3])
            stat(0, 1, SUM_AT["half"][7])

            for t in range(4):
                if t < 2:
                    free = lambda n, t=t: (pe.wait_ge(dve_free, 13 + n) if t == 0 else pe.wait_ge(act_free, n + 1))
                else:
                    free = lambda n, t=t: (pe.wait_ge(act_free, 5 + n) if t == 2
                                           else pe.wait_ge(dve_free, V_VAL + n + 1))
                tile_t(t, t % 2, hH, hL, free, h_wait(0) if t == 0 else None,
                       ada_hooks(16 + 2 * t, full=lambda a, t=t: 16 * (9 + t)))

            def scores(i, e):
                pe.wait_ge(act_free, A_HEADS + G_PAIR * i + (18 if e else 8))
                k_of = lambda tile: kT[:, e, tile * P:(tile + 1) * P]
                q_of = lambda tile: qT[:, e, tile * P:(tile + 1) * P]
                for n, tile in enumerate(LAT_TILES):
                    last = nc.tensor.matmul(ps[:, 5, n * P:(n + 1) * P], k_of(tile), q_of(tile), start=True, stop=True)
                last.then_inc(st_full, 1)
                nc.tensor.matmul(ps[:, 7, 0:P], k_of(CTX_TILE), q_of(CTX_TILE), start=True, stop=True)
                nc.tensor.transpose(ps[:, 7, P:2 * P], k_of(CTX_TILE), ident).then_inc(st_full, 1)
                for n, tile in enumerate(LAT_TILES):
                    last = nc.tensor.transpose(ps[:, 6, n * P:(n + 1) * P], k_of(tile), ident)
                last.then_inc(st_full, 1)

            def update(bank, at, r, tile):
                return nc.tensor.matmul(ps[:, bank, at:at + RV], kd_nat[:, r, tile, :], v_nat[:, tile, :],
                                        start=True, stop=True)

            def updates_1(i, e):
                head = 2 * i + e
                pe.wait_ge(kd_done, 4 * head + 4)
                pe.wait_ge(prob_done, 2 * head + 2)
                pe.wait_ge(act_free, A_HEADS + G_PAIR * i + 13 + 10 * e)
                for bank, (a_, b_) in ((5, ((0, 0), (0, 1))), (6, ((0, 3), (0, CTX_TILE))), (7, ((1, 4), (1, 3)))):
                    update(bank, 0, *a_)
                    update(bank, RV, *b_).then_inc(u_full, 1)

            def updates_2(i, e):
                pe.wait_ge(s_done, 6 * (2 * i + e) + 2)
                update(5, 0, 1, 1)
                update(5, RV, 1, CTX_TILE).then_inc(u_full, 1)

            def outputs(i, e):
                head = 2 * i + e
                pe.wait_ge(s_done, 6 * head + 6)
                pe.wait_ge(so_done, 2 * head + 2)
                pe.wait_ge(qdec_done, 4 * head + 4)
                for tile in range(NT):
                    out = ps[:, 5 + tile // 2, (tile % 2) * RV:(tile % 2 + 1) * RV]
                    cs = slice(tile * P, (tile + 1) * P)
                    ctx_ = tile == CTX_TILE
                    last = nc.tensor.matmul(out, prob[:, cs], v_nat[:, tile, :], start=True, stop=ctx_)
                    if not ctx_:
                        n = LAT_TILES.index(tile)
                        for r in range(2):
                            last = nc.tensor.matmul(out, qdec[:, r, cs], S[:, r, n, :], start=False, stop=(r == 1))
                    if tile in (1, 3, 4):
                        last.then_inc(o_full, 1)

            with pe.Fori(0, 2) as i:
                at = 0
                for b in range(6):
                    t = T_HEADS + 6 * i + b
                    hooks = ada_hooks(24 + 12 * i + 2 * b, full=lambda a, b=b: 16 * (13 + 6 * i + b))
                    free = lambda n, at=at: pe.wait_ge(act_free, A_HEADS + G_PAIR * i + at + n - 3)
                    if b == 0:
                        free0 = free

                        def free(n, free0=free0):
                            if n < 4:
                                pe.wait_ge(dve_free, V_RT - 3 + n)
                            free0(n)
                    if b < 2:
                        tile_t(t, b % 2, hH, hL, free, None, hooks)
                        at += 4
                        continue
                    e = (b - 2) // 2
                    if b % 2 == 0:
                        hooks[0].append(lambda e=e: scores(i, e))
                    else:
                        hooks[0].append(lambda e=e: updates_1(i, e))
                        hooks[1].append(lambda e=e: updates_2(i, e))
                        hooks[2].append(lambda e=e: outputs(i, e))
                    tile_n(t, b % 2, free, [(at + n) % 4 for n in range(NT)], None, hooks)
                    at += 5

            for n in range(16):
                pe.wait_ge(ret_done, n // 4 + 1)
                if n < 4:
                    pe.wait_ge(act_free, A_MLP0 - 3 + n)
                else:
                    pe.wait_ge(dve_free, V_RT + n - 3)
                turn_half(n % 4, ret, (n // 2) * P, n % 2)

            def channel_stat(which):
                pe.wait_ge(cstat_in, which + 1)
                nc.tensor.matmul(ps[:, 5, 0:LAT], ones[:], cst[:, which, 0:LAT], start=True, stop=True)
                nc.tensor.matmul(ps[:, 6, 0:CTX], ones[:], cst[:, which, LAT:T], start=True,
                                 stop=True).then_inc(cstat_full, 1)

            for t in range(4):
                tile_t(T_WR + t, t % 2, hH, hL, lambda n, t=t: pe.wait_ge(dve_free, V_WR + 4 * t + n - 3),
                       (lambda half, k: pe.wait_ge(dve_free, V_RT + 2 * k + half + 1)) if t == 0 else None,
                       {0: {0: [lambda: channel_stat(0)]}, 1: {2: [lambda: channel_stat(1)]}}.get(t))
            pe.wait_ge(cl_done, 2 * CC)
            for t in range(2):
                tile_t(T_WC + t, t % 2, cH, cL, lambda n, t=t: pe.wait_ge(dve_free, V_WC + 8 * t + n - 3),
                       nk=CC, nm=4, hooks={6: [lambda: stat(1, 0, SUM_AT["wc"][5])]} if t else None)
            stat(1, 1, SUM_AT["wc"][7])

            def mlp_group(g, layer, norm, last):
                t0, a0, v0, f0 = ((T_MLP0, A_MLP0, V_MLP0, 0), (T_MLP1, A_MLP1, V_MLP1, 64))[layer]
                for b in range(4):
                    hooks = None
                    if layer == 0:
                        hooks = ada_hooks(MOD1 + 12 * g + 2 * b, full=lambda a, b=b: 16 * (25 + 6 * g + b))
                    tile_t(t0 + 8 * g + b, b % 2, hH, hL,
                           lambda n, b=b: (pe.wait_ge(dve_free, v0 + 16 * g - 3 + n) if b == 0
                                           else pe.wait_ge(act_free, a0 + 16 * g + 4 * b + n - 3)),
                           h_wait(norm) if b == 0 else None, hooks)
                for b in range(4):
                    hooks = {}
                    if layer == 0:
                        n_ = MOD1 + 12 * g + 8 + b
                        hooks = {0: [lambda n_=n_, b=b: strips(n_, b % 2, 16 * (29 + 6 * g + b // 2))],
                                 1: [lambda n_=n_: finish(n_)]}
                    if last and b == 3:
                        hooks.setdefault(2, []).append(lambda: stat(norm + 1, 0, SUM_AT["tile"][6]))
                    tile_t(t0 + 8 * g + 4 + b, b % 2, fH, fL,
                           lambda n, b=b: (pe.wait_ge(act_free, a0 + 16 * g + 13 + n) if b == 0
                                           else pe.wait_ge(dve_free, v0 + 16 * g + 4 * b + n - 3)),
                           (lambda half, k: pe.wait_ge(f_ready, f0 + 16 * g + 4 * (k // 2) + 2 * half + k % 2 + 1))
                           if b == 0 else None, hooks)
                if last:
                    stat(norm + 1, 1, SUM_AT["tile"][7])

            with pe.Fori(0, FG - 1) as g:
                mlp_group(g, 0, 1, False)
            mlp_group(FG - 1, 0, 1, True)

            def turn_keys():
                pe.wait_ge(ro_done, 2)
                pe.wait_ge(att_in, 16 * 5)
                for h in range(KVH):
                    cs = slice(h * P, (h + 1) * P)
                    for n, tile in enumerate(LAT_TILES):
                        last = nc.tensor.transpose(ps[:, 4 + h, n * P:(n + 1) * P], kro[:, tile, cs], ident)
                    last.then_inc(tr_full, 1)
                    nc.tensor.transpose(ps[:, 6, 2 * h * P:(2 * h + 1) * P], kro[:, CTX_TILE, cs], ident)
                    last = nc.tensor.transpose(ps[:, 6, (2 * h + 1) * P:(2 * h + 2) * P], kc_nat[:, cs], ident)
                last.then_inc(tr_full, 1)

            def turn_queries(r):
                pe.wait_ge(ro_done, 2 * r + 4)
                pe.wait_ge(tr_out, 3 * (r + 1))
                for h in range(2):
                    cs = slice(h * P, (h + 1) * P)
                    for n, tile in enumerate(LAT_TILES):
                        last = nc.tensor.transpose(ps[:, 4 + h, n * P:(n + 1) * P], qro[:, tile, cs], ident)
                    last.then_inc(tr_full, 1)
                    last = nc.tensor.transpose(ps[:, 6, h * P:(h + 1) * P], qro[:, CTX_TILE, cs], ident)
                last.then_inc(tr_full, 1)

            for t in range(6):
                def free(n, t=t):
                    if t == 0:
                        if n < 4:
                            pe.wait_ge(dve_free, V_WO - 3 + n)
                    else:
                        pe.wait_ge(act_free, A_QKV + 5 * (t - 1) + n + 1)
                tile_n(T_QKV + t, t % 2, free, NAT_BANKS, h_wait(2) if t == 0 else None)
                if t == 1:
                    turn_keys()
                elif t > 1:
                    turn_queries(t - 2)

            def att_scores(n):
                if n >= 2:
                    pe.wait_ge(ex_done, n - 1)
                if n < 4 * QH:
                    h, i = n // 4, n % 4
                    for j in range(2):
                        last = nc.tensor.matmul(ps[:, 2 * (n % 2) + j, 0:HALF], qTa[:, h, i * P:(i + 1) * P],
                                                kTa[:, h // GRP, P + j * HALF:P + (j + 1) * HALF], start=True, stop=True)
                else:
                    kv = n - 4 * QH
                    for j in range(GRP):
                        last = nc.tensor.matmul(ps[:, 2 * (n % 2), j * P:(j + 1) * P], qTa[:, GRP * kv + j, LAT:T],
                                                kTa[:, kv, 0:P], start=True, stop=True)
                last.then_inc(sc_full, 1)

            def att_turn(n):
                pe.wait_ge(pn_done, n + 1)
                if n >= 2:
                    pe.wait_ge(pt_act, n - 1)
                bank = 4 if n % 2 == 0 else 7
                for j in range(4):
                    last = nc.tensor.transpose(ps[:, bank, j * P:(j + 1) * P], pr[:, n % 2, j * P:(j + 1) * P], ident)
                if n < 4 * QH:
                    if n >= 1:
                        pe.wait_ge(pt_dve, n)
                    last = nc.tensor.transpose(ps[:, 5, 0:P], pr[:, n % 2, 4 * P:5 * P], ident)
                last.then_inc(pt_full, 1)

            def att_values(h):
                if h >= 1:
                    pe.wait_ge(attn_ready, h)
                if h < QH:
                    pe.wait_ge(pt_act, 4 * h + 4)
                    pe.wait_ge(pt_dve, 4 * h + 4)
                    kv = h // GRP
                    for n, vt in enumerate((NT,) + LAT_TILES):
                        last = nc.tensor.matmul(ps[:, 6, :], va[:, vt, kv * P:(kv + 1) * P], pT[:, n, :],
                                                start=(n == 0), stop=(n == 4))
                else:
                    kv = h - QH
                    pe.wait_ge(pt_act, 4 * QH + kv + 1)
                    last = nc.tensor.matmul(ps[:, 6, :], va[:, CTX_TILE, kv * P:(kv + 1) * P], pT[:, kv, :],
                                            start=True, stop=True)
                last.then_inc(pv_full, 1)

            pe.wait_ge(tr_out, 15)
            pe.wait_ge(act_free, A_QKV + 30)
            N_ATT = 4 * QH + KVH
            att_scores(0)
            att_scores(1)
            for n in range(N_ATT):
                if n % 4 == 0 and n:
                    att_values(n // 4 - 1)
                att_turn(n)
                if n + 2 < N_ATT:
                    att_scores(n + 2)
            att_values(QH)
            att_values(QH + 1)

            for t in range(4):
                tile_t(T_WO + t, t % 2, hH, hL,
                       lambda n, t=t: (pe.wait_ge(attn_ready, QH + KVH) if t == 0
                                       else pe.wait_ge(dve_free, V_WO + 4 * t + n - 3)),
                       hooks={2: [lambda: stat(3, 0, SUM_AT["tile"][6])]} if t == 3 else None)
            stat(3, 1, SUM_AT["tile"][7])

            with pe.Fori(0, FG - 1) as g:
                mlp_group(g, 1, 3, False)
            mlp_group(FG - 1, 1, 3, True)

            for tile in range(NT):
                pe.wait_ge(y_done, 8 if tile < 2 else 16)
                for kq in range(2):
                    n = 2 * tile + kq
                    if n >= 4:
                        pe.wait_ge(y_dve if kq else y_act, tile - 1)
                    for j in range(4):
                        last = nc.tensor.transpose(ps[:, n % 4, j * P:(j + 1) * P],
                                                   xT[:, 4 * kq + j, tile * P:(tile + 1) * P], ident)
                    last.then_inc(y_full, 1)


        @block.scalar
        def _(act):
            def seg(x, half, s):
                c0, n, which = SEGS[half][s]
                return x[..., c0:c0 + n], which

            def split(t, slot, start=None):
                if start is not None:
                    act.wait_ge(acc_full, start)
                for j in range(2):
                    act.wait_ge(raw_in[j], 16 * (t + 1))
                    nc.scalar.activation(wH[:, slot, j * 1024:(j + 1) * 1024], raw[:, j, :], ACT.Copy).then_inc(wh_done, 1)

            def strips_out(n):
                act.wait_ge(ada_strips, n + 1)
                nc.scalar.activation(ada_sb[:], ps[:, B_ADA, 0:P], ACT.Copy).then_inc(ada_ev, 1)

            def add_bias(n):
                act.wait_ge(ada_fin, n + 1)
                act.wait_ge(rows_out, 2)
                nc.scalar.activation(modT[:, bass.ds(n, 1), :].rearrange("p a c -> p (a c)"), ps[:, B_ADA, 256:258],
                                     ACT.Identity, bias=vecT[:, 1, bass.ds(n, 1)]).then_inc(mod_done, 1)

            def square(norm, s, v0, order):
                half, p_ = PAIRS[order][s // 2]
                k = 2 * p_ + s % 2
                act.wait_ge(dve_free, v0 + s + 1)
                if s >= 2:
                    act.wait_ge(sum_done, SUMS * norm + SUM_AT[order][s // 2 - 1])
                nc.scalar.activation(sqb[:, s % 2, :], xT[:, k, half * HALF:(half + 1) * HALF], ACT.Square).then_inc(sq_done, 1)

            def std(norm, half):
                act.wait_ge(stat_full, 2 * norm + half + 1)
                nc.scalar.activation(rstd[:, half, :], ps[:, 5 + half, 0:HALF], ACT.Sqrt, bias=eps[:],
                                     scale=1.0 / D).then_inc(std_done, 1)

            def hi(norm, half, ks=range(KC)):
                for k in ks:
                    act.wait_ge(t_done, 16 * norm + 8 * half + k + 1)
                    nc.scalar.activation(hH[:, k, half * HALF:(half + 1) * HALF], tb[:, k % 2, :],
                                         ACT.Copy).then_inc(hh_done, 1)

            def h_hi(norm):
                for half in range(2):
                    std(norm, half)
                    hi(norm, half)

            def last_tile(norm, v0):
                square(norm, 12, v0, "tile")
                square(norm, 13, v0, "tile")
                std(norm, 0)
                square(norm, 14, v0, "tile")
                hi(norm, 0, range(0, 4))
                square(norm, 15, v0, "tile")
                hi(norm, 0, range(4, 8))
                std(norm, 1)
                hi(norm, 1)

            act.dma_start(lg[:].rearrange("p a b -> p (a b)"),
                          ret_log_decay.rearrange("a b c -> (a b c)").partition_broadcast(P)).then_inc(act_dma, 16)
            act.wait_ge(rows_out, 1)
            act.wait_ge(set_up, 3)
            nc.scalar.activation(siluc[:, :, 0:2].rearrange("p k c -> p c k"),
                                 vecT[:, 0, R_C:R_C + 16].rearrange("p (c k) -> p c k", c=2), ACT.Silu).then_inc(siluc_ready, 1)
            act.wait_ge(act_dma, 16)
            nc.scalar.activation(lg[:], lg[:], ACT.Exp).then_inc(lg_raw, 1)
            act.wait_ge(lg_done, 1)
            for r in range(2):
                nc.scalar.activation(kdec[:, r, :], lg[:, r, :], ACT.Exp, scale=const[:, C_KP + r:C_KP + r + 1]).then_inc(dec_done, 1)
            nc.scalar.activation(cdec[:], lg[:], ACT.Exp, scale=float(P)).then_inc(dec_done, 1)

            for n in range(16):
                strips_out(n)
                if n:
                    square(0, n - 1, 0, "half")
                add_bias(n)
            square(0, 15, 0, "half")
            split(0, 0)
            h_hi(0)

            for t in range(4):
                split(t + 1, (t + 1) % 2, 16 + 4 * t if t else None)
                for n in range(4):
                    g = G_GATE + 4 * t + n
                    if t < 2:
                        act.wait_ge(acc_full, g + 1)
                        nc.scalar.activation(sgate[:, 2 * t + n % 2, (n // 2) * HALF:(n // 2 + 1) * HALF],
                                             ps[:, n, 0:HALF], ACT.Sigmoid).then_inc(act_free, 1)
                    (strips_out if n % 2 == 0 else add_bias)(16 + 2 * t + n // 2)

            def decay_tables(head, e):
                act.wait_ge(dec_done, 3)
                for r, col in enumerate((C_PF, C_PB)):
                    nc.scalar.activation(dmat[:, r, :], const[:, col:col + P], ACT.Exp,
                                         scale=lg[:, r, bass.ds(head, 1)]).then_inc(dexp_done, 1)
                for r, col in enumerate((C_QF, C_QB)):
                    nc.scalar.activation(qtab[:, r, :], const[:, col:col + P], ACT.Exp,
                                         scale=lg[:, r, bass.ds(head, 1)]).then_inc(dexp_done, 1)

            def decayed_keys(head):
                act.wait_ge(st_full, 3 * head + 3)
                act.wait_ge(prob_done, 2 * head + 2)
                act.wait_ge(dec_done, 2)
                for r in range(2):
                    sc = kdec[:, r, bass.ds(head, 1)]
                    for a_, b_ in ((0, 0), (3, 2)):
                        nc.scalar.activation(kd_nat[:, r, a_:a_ + 2, :],
                                             ps[:, 6, b_ * P:(b_ + 2) * P].rearrange("p (a b) -> p a b", a=2),
                                             ACT.Copy, scale=sc)
                    nc.scalar.activation(kd_nat[:, r, CTX_TILE, :], ps[:, 7, P:2 * P], ACT.Copy, scale=sc).then_inc(kd_done, 2)

            def ret_std(head):
                act.wait_ge(bn_done, 10 * head + 10)
                nc.scalar.activation(brs[:, :, 0], bmv[:, :, 1], ACT.Sqrt, bias=eps[:]).then_inc(bstd_done, 1)

            with act.Fori(0, 2) as i:
                at = 0
                for b in range(6):
                    e = (b - 2) // 2
                    head = 2 * i + e
                    split(T_HEADS + 6 * i + b + 1, (b + 1) % 2, G_HEADS + G_PAIR * i + at)
                    if b == 0:
                        decay_tables(2 * i, 0)
                    if b == 3:
                        decay_tables(2 * i + 1, 1)
                    for n in range(4 if b < 2 else NT):
                        act.wait_ge(acc_full, G_HEADS + G_PAIR * i + at + n + 1)
                        bank = (at + n) % 4
                        if b < 2:
                            dst, src = (qT, kT)[b][:, n % 2, (n // 2) * HALF:(n // 2 + 1) * HALF], ps[:, bank, 0:HALF]
                        else:
                            dst, src = (v_nat, gate)[b % 2][:, n, :], ps[:, bank, 0:RV]
                        nc.scalar.activation(dst, src, ACT.Silu if b in (3, 5) else ACT.Copy).then_inc(act_free, 1)
                        m = 24 + 12 * i + 2 * b + n // 2
                        if n < 4:
                            (strips_out if n % 2 == 0 else add_bias)(m)
                        if b in (2, 4) and n == 1:
                            decayed_keys(head)
                        if b == 4 and n == 0:
                            ret_std(2 * i)
                        if b == 4 and n == 2:
                            act.wait_ge(so_done, 2 * (2 * i) + 2)
                            act.dma_start(new_state[0, 0, :, bass.ds(2 * i, 1)].rearrange("r a d e -> d (r a) e"),
                                          state_out[:]).then_inc(act_dma, 16)
                        if b in (3, 5) and n == 3:
                            for q in range(3):
                                act.wait_ge(o_full, 3 * head + q + 1)
                                act.wait_ge(dve_free, V_RT)
                                w_ = 2 if q < 2 else 1
                                nc.scalar.activation(ret[:, 2 * q:2 * q + w_, bass.ds(512 * i + 256 * e, RV)],
                                                     ps[:, 5 + q, 0:w_ * RV].rearrange("p (a b) -> p a b", a=w_),
                                                     ACT.Copy).then_inc(o_out, 1)
                    at += 4 if b < 2 else NT
                ret_std(2 * i + 1)
                act.wait_ge(so_done, 2 * (2 * i + 1) + 2)
                act.dma_start(new_state[0, 0, :, bass.ds(2 * i + 1, 1)].rearrange("r a d e -> d (r a) e"),
                              state_out[:]).then_inc(act_dma, 16)

            for n in range(16):
                act.wait_ge(acc_full, G_RT + n + 1)
                nc.scalar.activation(hH[:, n // 2, (n % 2) * HALF:(n % 2 + 1) * HALF], ps[:, n % 4, 0:HALF],
                                     ACT.Copy).then_inc(rth_done, 1)

            split(T_WR + 1, 1, G_WR)
            for ch in range(CC):
                act.wait_ge(cx_done, ch + 1)
                if ch >= 2:
                    act.wait_ge(csum_done, ch - 1)
                nc.scalar.activation(cmp_[:, ch % 2, 0:LAT], cacc[:, ch, 0:LAT], ACT.Square)
                nc.scalar.activation(cmp_[:, ch % 2, LAT:T], cacc[:, ch, LAT + PAD:CW], ACT.Square).then_inc(csq_done, 1)
            split(T_WR + 2, 0, G_WR + 4)
            split(T_WR + 3, 1, G_WR + 8)
            act.wait_ge(cstat_full, 2)
            nc.scalar.activation(cmp_[:, 0, 0:LAT], ps[:, 5, 0:LAT], ACT.Sqrt, bias=eps[:], scale=1.0 / CONV)
            nc.scalar.activation(cmp_[:, 0, LAT:T], ps[:, 6, 0:CTX], ACT.Sqrt, bias=eps[:], scale=1.0 / CONV).then_inc(cstd_done, 1)
            for ch in range(CC):
                act.wait_ge(cn_done, ch + 1)
                nc.scalar.activation(cacc[:, ch, :], cacc[:, ch, :], ACT.Silu, scale=vecT[:, 0, R_LG + ch:R_LG + ch + 1],
                                     bias=vecT[:, 0, R_LB + ch:R_LB + ch + 1]).then_inc(csilu_done, 1)
            for ch in range(CC):
                act.wait_ge(csilu_done, ch + 1)
                for a_, b_, n_ in CONV_MAP:
                    last = nc.scalar.activation(cH[:, ch, b_:b_ + n_], cacc[:, ch, a_:a_ + n_], ACT.Copy)
                last.then_inc(ch_done, 1)
            split(T_WC, 0, G_WR + 12)
            split(T_WC + 1, 1, G_WC)
            for s in range(8):
                square(1, s, V_WC, "wc")
            split(T_MLP0, 0, G_WC + 8)
            for s in range(8, 16):
                square(1, s, V_WC, "wc")
            act.wait_ge(act_dma, 16 * (RH + 1))
            h_hi(1)

            def mlp_group(g, layer, last):
                t0, g0, a0, v0, f0, norm = ((T_MLP0, G_MLP0, A_MLP0, V_MLP0, 0, 1),
                                            (T_MLP1, G_MLP1, A_MLP1, V_MLP1, 64, 3))[layer]

                def hidden_hi(n):
                    act.wait_ge(fs_done, f0 + 16 * g + n + 1)
                    k, half = 2 * (n // 4) + n % 2, n // 2 % 2
                    nc.scalar.activation(fH[:, k, half * HALF:(half + 1) * HALF], fs[:, n % 2, :], ACT.Copy).then_inc(fh_done, 1)

                for b in range(8):
                    if not (last and layer == 1 and b == 7):
                        split(t0 + 8 * g + b + 1, (b + 1) % 2, g0 + 32 * g + 4 * b)
                    if b < 4:
                        for n in range(4):
                            j = 4 * b + n
                            act.wait_ge(acc_full, g0 + 32 * g + j + 1)
                            if j >= 2:
                                act.wait_ge(fs_done, f0 + 16 * g + j - 1)
                            nc.scalar.activation(fr[:, j % 2, :], ps[:, n, 0:HALF], ACT.Relu).then_inc(act_free, 1)
                            if j:
                                hidden_hi(j - 1)
                            if layer == 0:
                                (strips_out if n % 2 == 0 else add_bias)(MOD1 + 12 * g + 2 * b + n // 2)
                        if b == 3:
                            hidden_hi(15)
                    else:
                        if layer == 0:
                            strips_out(MOD1 + 12 * g + 4 + b)
                            add_bias(MOD1 + 12 * g + 4 + b)
                        if last and b == 7 and layer == 0:
                            last_tile(2, v0 + 16 * g)
                        elif last:
                            for s in range(4 * (b - 4), 4 * (b - 3)):
                                square(norm + 1, s, v0 + 16 * g, "tile")

            with act.Fori(0, FG - 1) as g:
                mlp_group(g, 0, False)
            mlp_group(FG - 1, 0, True)

            def rope_std(r):
                act.wait_ge(rss_done, r + 1)
                nc.scalar.activation(rss[:], rss[:], ACT.Sqrt, bias=eps[:], scale=1.0 / P).then_inc(rstd2, 1)

            def turned_out(r):
                for h in range(2):
                    act.wait_ge(tr_full, 3 * r + h + 1)
                    dst = kTa[:, h, 2 * P:] if r == 0 else qTa[:, 2 * (r - 1) + h, 0:LAT]
                    nc.scalar.activation(dst, ps[:, 4 + h, :], ACT.Copy).then_inc(tr_out, 1)
                act.wait_ge(tr_full, 3 * r + 3)
                if r == 0:
                    nc.scalar.activation(kTa[:, :, 0:2 * P], ps[:, 6, :].rearrange("p (h n) -> p h n", h=2),
                                         ACT.Copy).then_inc(tr_out, 1)
                else:
                    nc.scalar.activation(qTa[:, 2 * (r - 1):2 * r, LAT:T], ps[:, 6, 0:2 * P].rearrange("p (h n) -> p h n", h=2),
                                         ACT.Copy).then_inc(tr_out, 1)

            for t in range(6):
                split(T_QKV + t + 1, (t + 1) % 2, G_QKV + 5 * t)
                for n in range(NT):
                    act.wait_ge(acc_full, G_QKV + 5 * t + n + 1)
                    if t == 0:
                        dst = k_nat[:, n, :]
                    elif t < 5:
                        if t > 2:
                            act.wait_ge(rn_done, t - 1)
                        dst = q_nat[:, (t - 1) % 2, n, :]
                    else:
                        dst = va[:, n, :]
                    nc.scalar.activation(dst, ps[:, NAT_BANKS[n], 0:RV], ACT.Copy).then_inc(act_free, 1)
                    if n == 1 and t:
                        rope_std(t - 1)
                    if n == 1 and t > 1:
                        turned_out(t - 2)
            turned_out(4)

            def att_exp(n):
                act.wait_ge(nmx_done, n + 1)
                if n >= 2:
                    act.wait_ge(pt_full, n - 1)
                if n < 4 * QH:
                    last = nc.scalar.activation(pr[:, n % 2, :].rearrange("p (a b) -> p a b", a=2),
                                                ps[:, 2 * (n % 2):2 * (n % 2) + 2, 0:HALF], ACT.Exp,
                                                bias=amx[:, n % 2, 0:1], scale=ATT_SCALE, accum_out=asum[:, n % 2, 0:1])
                else:
                    for j in range(GRP):
                        last = nc.scalar.activation(pr[:, n % 2, j * P:(j + 1) * P], ps[:, 2 * (n % 2), j * P:(j + 1) * P],
                                                    ACT.Exp, bias=amx[:, n % 2, j:j + 1], scale=ATT_SCALE,
                                                    accum_out=asum[:, n % 2, j:j + 1])
                last.then_inc(ex_done, 1)

            def att_turned(n):
                act.wait_ge(pt_full, n + 1)
                bank = ps[:, 4 if n % 2 == 0 else 7, :]
                if n == 0:
                    act.wait_ge(k_st, 16)
                if n < 4 * QH:
                    nc.scalar.activation(pT[:, 0:4, (n % 4) * P:(n % 4 + 1) * P], bank.rearrange("p (a b) -> p a b", a=4),
                                         ACT.Copy).then_inc(pt_act, 1)
                else:
                    nc.scalar.activation(pT[:, n - 4 * QH, :], bank, ACT.Copy).then_inc(pt_act, 1)

            def att_hi(h):
                act.wait_ge(pv_full, h + 1)
                if h < QH:
                    nc.scalar.activation(hH[:, h, 0:256], ps[:, 6, 0:256], ACT.Copy)
                    nc.scalar.activation(hH[:, h, 384:640], ps[:, 6, 256:512], ACT.Copy).then_inc(ah_done, 1)
                else:
                    kv = h - QH
                    nc.scalar.activation(hH[:, GRP * kv:GRP * (kv + 1), 256:384],
                                         ps[:, 6, :].rearrange("p (a b) -> p a b", a=GRP), ACT.Copy).then_inc(ah_done, 1)

            att_exp(0)
            att_exp(1)
            for n in range(4 * QH + KVH):
                if n % 4 == 0 and n:
                    att_hi(n // 4 - 1)
                att_turned(n)
                if n + 2 < 4 * QH + KVH:
                    att_exp(n + 2)
            att_hi(QH)
            att_hi(QH + 1)

            for t in range(4):
                split(T_WO + t + 1, (t + 1) % 2, G_WO + 4 * t)
                if t < 3:
                    for s in range(4 * t, 4 * t + 4):
                        square(3, s, V_WO, "tile")
            last_tile(3, V_WO)
            with act.Fori(0, FG - 1) as g:
                mlp_group(g, 1, False)
            mlp_group(FG - 1, 1, True)
            std(4, 0)
            std(4, 1)
            for tile in range(NT):
                act.wait_ge(y_full, 2 * tile + 1)
                nc.scalar.activation(y_nat[:, tile, 0:512], ps[:, (2 * tile) % 4, :], ACT.Copy).then_inc(y_act, 1)

        @block.gpsimd
        def _(pool):
            def lo(t, slot):
                for j in range(2):
                    pool.wait_ge(wh_done, 2 * t + j + 1)
                    cs = slice(j * 1024, (j + 1) * 1024)
                    nc.gpsimd.tensor_tensor(wL[:, slot, cs], raw[:, j, :], wH[:, slot, cs].bitcast(F32),
                                            ALU.subtract).then_inc(wl_done, 1)

            def h_lo(norm):
                for half in range(2):
                    for k in range(KC):
                        pool.wait_ge(hh_done, 16 * norm + 8 * half + k + 1)
                        cs = slice(half * HALF, (half + 1) * HALF)
                        nc.gpsimd.tensor_tensor(hL[:, k, cs], tb[:, k % 2, :], hH[:, k, cs].bitcast(F32),
                                                ALU.subtract).then_inc(h_ready, 1)

            lo(0, 0)
            h_lo(0)
            for t in range(4):
                lo(t + 1, (t + 1) % 2)
            with pool.Fori(0, 2) as i:
                for b in range(6):
                    lo(T_HEADS + 6 * i + b + 1, (b + 1) % 2)
            for t in range(T_WR + 1, T_MLP0 + 1):
                lo(t, t % 2)
            for norm, first, n_tiles in ((1, T_MLP0, 8 * FG), (2, T_QKV, 6 + 4), (3, T_MLP1, 8 * FG - 1)):
                h_lo(norm)
                with pool.Fori(0, n_tiles // 2) as i:
                    for j in range(2):
                        lo(first + 2 * i + j + 1, (j + 1) % 2)
            lo(N_TILES - 1, 1)

        @block.vector
        def _(dve):
            def halfcols(half):
                return slice(half * HALF, (half + 1) * HALF)

            def residual(g, v0, n, half, k, gate_at):
                dve.wait_ge(acc_full, g + n + 1)
                for c0, w_, which in SEGS[half]:
                    x = xT[:, k, c0:c0 + w_]
                    last = nc.vector.scalar_tensor_tensor(out=x, in0=ps[:, n % 4, c0 - half * HALF:c0 - half * HALF + w_],
                                                          scalar=modT[:, gate_at + k, which:which + 1], in1=x,
                                                          op0=ALU.mult, op1=ALU.add)
                last.then_inc(dve_free, 1)

            def add_squares(norm, q, order):
                half, p_ = PAIRS[order][q]
                base = SUMS * norm
                dve.wait_ge(sq_done, 16 * norm + 2 * q + 2)
                out = ssum[:, half, :]
                if p_ == 0:
                    nc.vector.tensor_tensor(out, sqb[:, 0, :], sqb[:, 1, :], ALU.add).then_inc(sum_done, 1)
                else:
                    before = base + SUM_AT[order][q] - 2
                    dve.wait_ge(sum_done, before)
                    nc.vector.tensor_tensor(out, out, sqb[:, 0, :], ALU.add).then_inc(sum_done, 1)
                    dve.wait_ge(sum_done, before + 1)
                    nc.vector.tensor_tensor(out, out, sqb[:, 1, :], ALU.add).then_inc(sum_done, 1)

            def reciprocal_std(norm, half):
                dve.wait_ge(std_done, 2 * norm + half + 1)
                nc.vector.reciprocal(rstd[:, half, :], rstd[:, half, :]).then_inc(rstd_done, 1)
                dve.wait_ge(rstd_done, 2 * norm + half + 1)

            def h_values(norm, half, ks):
                shift_at = (SH1, SH2, MOD1 + SH1, MOD1 + SH2)[norm]
                i0 = 16 * norm + 8 * half

                def normed(k):
                    if i0 + k >= 2:
                        dve.wait_ge(t_done, i0 + k - 1)
                    nc.vector.tensor_tensor(ub[:, k % 2, :], xT[:, k, halfcols(half)], rstd[:, half, :],
                                            ALU.mult).then_inc(u_done, 1)
                normed(ks[0])
                for k in ks:
                    if k != ks[-1]:
                        normed(k + 1)
                    dve.wait_ge(u_done, i0 + k + 1)
                    if i0 + k >= 2:
                        dve.wait_ge(h_ready, i0 + k - 1)
                    for c0, w_, which in SEGS[half]:
                        a_ = c0 - half * HALF
                        last = nc.vector.tensor_scalar(tb[:, k % 2, a_:a_ + w_], ub[:, k % 2, a_:a_ + w_],
                                                       coef[:, norm, k, which:which + 1],
                                                       modT[:, shift_at + k, which:which + 1], ALU.mult, ALU.add)
                    last.then_inc(t_done, 1)

            def coefficients(norm):
                scale_at = (SC1, SC2, MOD1 + SC1, MOD1 + SC2)[norm]
                dve.wait_ge(mod_done, scale_at + KC)
                g = vecT[:, 0, R_NORM + KC * norm:R_NORM + KC * (norm + 1)]
                nc.vector.scalar_tensor_tensor(out=coef[:, norm], in0=modT[:, scale_at:scale_at + KC, :], scalar=1.0,
                                               in1=g[:, :, None].to_broadcast([P, KC, 2]), op0=ALU.add,
                                               op1=ALU.mult).then_inc(coef_done, 1)
                dve.wait_ge(coef_done, norm + 1)

            nc.vector.memset(ones[:], 1.0).then_inc(set_up, 1)
            nc.vector.memset(eps[:], EPS).then_inc(set_up, 1)
            nc.vector.memset(siluc[:], 0.0).then_inc(set_up, 1)
            for r, nr in enumerate((R_END, N_MOD, WIDTH * CC)):
                dve.wait_ge(rows_full, r + 1)
                nc.vector.tensor_copy(vecT[:, r, 0:nr], ps[:, 5 + r, 0:nr]).then_inc(rows_out, 1)
            dve.wait_ge(lg_raw, 1)
            nc.vector.tensor_scalar(lg[:], lg[:], -1.0, None, ALU.mult).then_inc(lg_done, 1)

            for n in range(16):
                dve.wait_ge(acc_full, n + 1)
                nc.vector.tensor_copy(xT[:, n % 8, halfcols(n // 8)], ps[:, n % 4, 0:HALF]).then_inc(dve_free, 1)
                if n % 2 == 1 and n > 1:
                    add_squares(0, n // 2 - 1, "half")
            add_squares(0, 7, "half")
            for a_, b_ in ((0, PAD), (PAD + LAT, 2 * PAD + LAT), (ZW - PAD, ZW)):
                last = nc.vector.memset(zp[:, :, a_:b_], 0.0)
            last.then_inc(set_up, 1)
            coefficients(0)
            for half in range(2):
                reciprocal_std(0, half)
                h_values(0, half, range(KC))

            dve.wait_ge(act_free, 8)
            for t in range(2):
                for n in range(4):
                    half, ch = n // 2, 2 * t + n % 2
                    dve.wait_ge(acc_full, G_VAL + 4 * t + n + 1)
                    for c0, w_, which in SEGS[half]:
                        a_ = c0 - half * HALF
                        z0 = (2 * PAD + LAT + c0 - 256) if which else (PAD + c0 - (P if half else 0))
                        last = nc.vector.tensor_tensor(zp[:, ch, z0:z0 + w_], ps[:, n, a_:a_ + w_],
                                                       sgate[:, ch, c0:c0 + w_], ALU.mult)
                    last.then_inc(dve_free, 1)

            dve.wait_ge(set_up, 4)
            dve.wait_ge(dve_free, V_RT)
            dve.wait_ge(rows_out, 3)
            with dve.Fori(0, 2) as i:
                def taps(w0, w1):
                    for w in range(w0, w1):
                        for ch in range(2):
                            src = zp[:, bass.ds(2 * i + ch, 1), w:w + CW].rearrange("p a n -> p (a n)")
                            acc = cacc[:, bass.ds(2 * i + ch, 1), :].rearrange("p a n -> p (a n)")
                            wt = vecT[:, 2, bass.ds(2 * i + 4 * w + ch, 1)]
                            if w == 0:
                                nc.vector.tensor_scalar(acc, src, wt, vecT[:, 0, bass.ds(R_CB + 2 * i + ch, 1)],
                                                        ALU.mult, ALU.add).then_inc(conv_done, 1)
                            else:
                                dve.wait_ge(conv_done, 2 * WIDTH * i + 2 * w + ch - 1)
                                nc.vector.scalar_tensor_tensor(out=acc, in0=src, scalar=wt, in1=acc, op0=ALU.mult,
                                                               op1=ALU.add).then_inc(conv_done, 1)

                for e in range(2):
                    head = 2 * i + e
                    w0 = 16 * e
                    taps(w0, w0 + 4)
                    dve.wait_ge(dexp_done, 4 * head + 4)
                    nc.vector.tensor_tensor(dmat[:, 0, :], dmat[:, 0, :], dmat[:, 1, :], ALU.mult).then_inc(dm_done, 1)
                    dve.wait_ge(act_free, A_HEADS + G_PAIR * i + 4)
                    for r in range(2):
                        for c0 in (0, 384):
                            nc.vector.scalar_tensor_tensor(
                                out=qdec[:, r, c0:c0 + 256].rearrange("p (a b) -> p a b", a=2),
                                in0=qT[:, e, c0:c0 + 256].rearrange("p (a b) -> p a b", a=2), scalar=RET_SCALE,
                                in1=qtab[:, r, None, :].to_broadcast([P, 2, P]), op0=ALU.mult,
                                op1=ALU.mult).then_inc(qdec_done, 1)
                    dve.wait_ge(dm_done, 2 * head + 1)
                    nc.vector.tensor_tensor(dmat[:, 0, :], dmat[:, 0, :], ident, ALU.add).then_inc(dm_done, 1)
                    dve.wait_ge(dm_done, 2 * head + 2)
                    dve.wait_ge(st_full, 3 * head + 2)
                    for a_, b_ in ((0, 0), (3, 2)):
                        last = nc.vector.scalar_tensor_tensor(
                            out=prob[:, a_ * P:(a_ + 2) * P].rearrange("p (a b) -> p a b", a=2),
                            in0=ps[:, 5, b_ * P:(b_ + 2) * P].rearrange("p (a b) -> p a b", a=2), scalar=RET_SCALE,
                            in1=dmat[:, 0, None, :].to_broadcast([P, 2, P]), op0=ALU.mult, op1=ALU.mult)
                    last.then_inc(prob_done, 1)
                    nc.vector.scalar_tensor_tensor(out=prob[:, 2 * P:3 * P], in0=ps[:, 7, 0:P], scalar=RET_SCALE,
                                                   in1=dmat[:, 0, :], op0=ALU.mult, op1=ALU.mult).then_inc(prob_done, 1)
                    taps(w0 + 4, w0 + 11)
                    dve.wait_ge(s0_in, 32 * (head + 1))
                    dve.wait_ge(dec_done, 3)

                    def advance(r, n, to, bank, at, count):
                        if count:
                            dve.wait_ge(s_done, 6 * head + count)
                        nc.vector.scalar_tensor_tensor(out=S[:, r, to, :], in0=S[:, r, n, :],
                                                       scalar=cdec[:, r, bass.ds(head, 1)], in1=ps[:, bank, at:at + RV],
                                                       op0=ALU.mult, op1=ALU.add).then_inc(s_done, 1)

                    dve.wait_ge(u_full, 4 * head + 1)
                    advance(0, 0, 1, 5, 0, 0)
                    advance(0, 1, 2, 5, RV, 1)
                    dve.wait_ge(u_full, 4 * head + 2)
                    advance(0, 2, 3, 6, 0, 2)
                    dve.wait_ge(act_dma, 16 * (head + 1))
                    nc.vector.tensor_copy(state_out[:, 0, :], ps[:, 6, RV:2 * RV]).then_inc(so_done, 1)
                    dve.wait_ge(u_full, 4 * head + 3)
                    advance(1, 3, 2, 7, 0, 3)
                    advance(1, 2, 1, 7, RV, 4)
                    dve.wait_ge(u_full, 4 * head + 4)
                    advance(1, 1, 0, 5, 0, 5)
                    nc.vector.tensor_copy(state_out[:, 1, :], ps[:, 5, RV:2 * RV]).then_inc(so_done, 1)
                    taps(w0 + 11, w0 + 13)
                    hc = bass.ds(512 * i + 256 * e, RV)
                    for n in range(NT):
                        dve.wait_ge(o_out, 3 * head + n // 2 + 1)
                        nc.vector.bn_stats(bst[:, n, :], ret[:, n, hc]).then_inc(bn_done, 1)
                    dve.wait_ge(bn_done, 10 * head + 5)
                    taps(w0 + 13, w0 + 14)
                    for n in range(NT):
                        nc.vector.bn_aggr(bmv[:, n, :], bst[:, n, :]).then_inc(bn_done, 1)
                    taps(w0 + 14, w0 + 15)
                    dve.wait_ge(bstd_done, head + 1)
                    nc.vector.reciprocal(brs[:, :, 0], brs[:, :, 0]).then_inc(brs_done, 1)
                    taps(w0 + 15, min(w0 + 16, WIDTH))
                    dve.wait_ge(brs_done, head + 1)
                    for n in range(NT):
                        nc.vector.tensor_scalar(ret[:, n, hc], ret[:, n, hc], bmv[:, n, 0:1], brs[:, n, 0:1],
                                                ALU.subtract, ALU.mult).then_inc(on_done, 1)
                    dve.wait_ge(act_free, A_HEADS + G_PAIR * i + 18 + 10 * e)
                    for n in range(NT):
                        dve.wait_ge(on_done, NT * head + n + 1)
                        last = nc.vector.tensor_tensor(ret[:, n, hc], ret[:, n, hc], gate[:, n, :], ALU.mult)
                    last.then_inc(ret_done, 1)

            def compact(ch):
                return ((cacc[:, ch, 0:LAT], slice(0, LAT)), (cacc[:, ch, LAT + PAD:CW], slice(LAT, T)))

            dve.wait_ge(conv_done, 4 * WIDTH)
            for src, cs in compact(0):
                other = dict((c.start, s) for s, c in compact(1))[cs.start]
                last = nc.vector.tensor_tensor(cst[:, 0, cs], src, other, ALU.add)
            last.then_inc(cn_sum, 1)
            for ch in (2, 3):
                dve.wait_ge(cn_sum, ch - 1)
                for src, cs in compact(ch):
                    last = nc.vector.tensor_tensor(cst[:, 0, cs], cst[:, 0, cs], src, ALU.add)
                last.then_inc(cn_sum, 1)
            dve.wait_ge(cn_sum, 3)
            nc.vector.tensor_scalar(cst[:, 0, :], cst[:, 0, :], 1.0 / CONV, None, ALU.mult).then_inc(cstat_in, 1)

            for n in range(16):
                dve.wait_ge(rth_done, n + 1)
                cs = halfcols(n % 2)
                nc.vector.tensor_tensor(hL[:, n // 2, cs], ps[:, n % 4, 0:HALF], hH[:, n // 2, cs].bitcast(F32),
                                        ALU.subtract).then_inc(dve_free, 1)

            def wr(n):
                t, m = n // 4, n % 4
                residual(G_WR, V_WR, n, m // 2, 2 * t + m % 2, G1)

            dve.wait_ge(mod_done, MOD1)
            wr(0)
            wr(1)
            dve.wait_ge(cstat_full, 1)
            for ch in range(CC):
                for (src, cs), bank in zip(compact(ch), (5, 6)):
                    last = nc.vector.tensor_tensor(src, src, ps[:, bank, 0:cs.stop - cs.start], ALU.subtract)
                last.then_inc(cx_done, 1)
            for n in range(2, 5):
                wr(n)
            dve.wait_ge(csq_done, 2)
            nc.vector.tensor_tensor(cst[:, 1, :], cmp_[:, 0, :], cmp_[:, 1, :], ALU.add).then_inc(csum_done, 2)
            for ch in (2, 3):
                dve.wait_ge(csq_done, ch + 1)
                dve.wait_ge(csum_done, ch)
                nc.vector.tensor_tensor(cst[:, 1, :], cst[:, 1, :], cmp_[:, ch % 2, :], ALU.add).then_inc(
                    csum_done if ch == 2 else cstat_in, 1)
            for n in range(5, 10):
                wr(n)
            dve.wait_ge(cstd_done, 1)
            nc.vector.reciprocal(cmp_[:, 0, :], cmp_[:, 0, :]).then_inc(crec_done, 1)
            dve.wait_ge(crec_done, 1)
            for ch in range(CC):
                dve.wait_ge(cx_done, ch + 1)
                for src, cs in compact(ch):
                    last = nc.vector.tensor_tensor(src, src, cmp_[:, 0, cs], ALU.mult)
                last.then_inc(cn_done, 1)
            for n in range(10, 16):
                wr(n)
            for ch in range(CC):
                dve.wait_ge(ch_done, ch + 1)
                for a_, b_, n_ in CONV_MAP:
                    last = nc.vector.tensor_tensor(cL[:, ch, b_:b_ + n_], cacc[:, ch, a_:a_ + n_],
                                                   cH[:, ch, b_:b_ + n_].bitcast(F32), ALU.subtract)
                last.then_inc(cl_done, 2)
            coefficients(1)

            def last_tile(norm, order, update, first):
                update(first)
                update(first + 1)
                add_squares(norm, first // 2, order)
                update(first + 2)
                reciprocal_std(norm, 0)
                h_values(norm, 0, range(0, 4))
                update(first + 3)
                add_squares(norm, first // 2 + 1, order)
                h_values(norm, 0, range(4, 8))
                reciprocal_std(norm, 1)
                h_values(norm, 1, range(KC))

            def wc(n):
                t, m = n // 8, n % 8
                residual(G_WC, V_WC, n, m // 4, 4 * t + m % 4, G1)

            for n in range(13):
                wc(n)
                if n % 2 == 1:
                    add_squares(1, n // 2, "wc")
            wc(13)
            add_squares(1, 6, "wc")
            wc(14)
            wc(15)
            add_squares(1, 7, "wc")
            for half in range(2):
                reciprocal_std(1, half)
                h_values(1, half, range(KC))

            def mlp_group(g, layer, last):
                g0, a0, v0, f0, norm, gate_at = ((G_MLP0, A_MLP0, V_MLP0, 0, 1, G2),
                                                 (G_MLP1, A_MLP1, V_MLP1, 64, 3, MOD1 + G2))[layer]

                def hidden_lo(n):
                    dve.wait_ge(fh_done, f0 + 16 * g + n + 1)
                    k, half = 2 * (n // 4) + n % 2, n // 2 % 2
                    nc.vector.tensor_tensor(fL[:, k, halfcols(half)], fs[:, n % 2, :], fH[:, k, halfcols(half)].bitcast(F32),
                                            ALU.subtract).then_inc(f_ready, 1)

                for n in range(16):
                    dve.wait_ge(act_free, a0 + 16 * g + n + 1)
                    if n >= 2:
                        dve.wait_ge(f_ready, f0 + 16 * g + n - 1)
                    nc.vector.tensor_tensor(fs[:, n % 2, :], fr[:, n % 2, :], fr[:, n % 2, :], ALU.mult).then_inc(fs_done, 1)
                    if n:
                        hidden_lo(n - 1)
                hidden_lo(15)

                def update(n):
                    b, m = n // 4, n % 4
                    residual(g0 + 32 * g + 16, v0, n, m // 2, 2 * b + m % 2, gate_at)

                for n in range(12 if last else 16):
                    update(n)
                    if last and n % 2 == 1:
                        add_squares(norm + 1, n // 2, "tile")
                return update

            with dve.Fori(0, FG - 1) as g:
                mlp_group(g, 0, False)
            update = mlp_group(FG - 1, 0, True)
            dve.wait_ge(mod_done, N_MOD)
            coefficients(2)
            last_tile(2, "tile", update, 12)
            coefficients(3)

            dve.wait_ge(att_in, 16 * 3)
            for qk in range(2):
                for j, (cs_, par) in enumerate(((0, 0), (1, 1), (1, 0), (0, 1))):
                    last = nc.vector.tensor_tensor(tabs[:, qk, j], rope_sb[:, cs_],
                                                   gqk[:, qk, None, par::2].to_broadcast([P, NT, 64]), ALU.mult)
            last.then_inc(tab_done, 1)
            dve.wait_ge(tab_done, 1)

            def rope(r):
                src = k_nat[:] if r == 0 else q_nat[:, (r - 1) % 2]
                out = kro if r == 0 else qro
                tab = tabs[:, 1 if r == 0 else 0]
                dve.wait_ge(act_free, A_QKV + 5 * r + 5)
                nc.vector.tensor_tensor(rn[:], src, src, ALU.mult).then_inc(rsq_done, 1)
                dve.wait_ge(rsq_done, r + 1)
                nc.vector.tensor_reduce(rss[:], rn[:].rearrange("p n (h d) -> p (n h) d", h=2), AX_X,
                                        ALU.add).then_inc(rss_done, 1)
                dve.wait_ge(rstd2, r + 1)
                nc.vector.reciprocal(rss[:], rss[:]).then_inc(rrec, 1)
                dve.wait_ge(rrec, r + 1)
                nc.vector.tensor_tensor(rn[:].rearrange("p n (h d) -> p (n h) d", h=2),
                                        src.rearrange("p n (h d) -> p (n h) d", h=2),
                                        rss[:, :, None].to_broadcast([P, 2 * NT, P]), ALU.mult).then_inc(rn_done, 1)
                dve.wait_ge(rn_done, r + 1)
                if r > 1:
                    dve.wait_ge(tr_full, 3 * r)
                x = [rn[:].rearrange("p n (h d) -> p n h d", h=2)[..., par::2] for par in range(2)]
                y = [out[:].rearrange("p n (h d) -> p n h d", h=2)[..., par::2] for par in range(2)]
                for j, (dst, a_) in enumerate(((y[0], 0), (rtmp[:, 0], 1), (y[1], 0), (rtmp[:, 1], 1))):
                    nc.vector.tensor_tensor(dst, x[a_], tab[:, j, :, None, :].to_broadcast([P, NT, 2, 64]),
                                            ALU.mult).then_inc(rm_done, 1)
                for j in range(2):
                    dve.wait_ge(rm_done, 4 * r + 2 * j + 2)
                    nc.vector.tensor_tensor(y[j], y[j], rtmp[:, j], ALU.add if j else ALU.subtract).then_inc(ro_done, 1)

            for r in range(5):
                rope(r)

            def att_max(n):
                dve.wait_ge(sc_full, n + 1)
                if n >= 2:
                    dve.wait_ge(ex_done, n - 1)
                if n < 4 * QH:
                    m = amx[:, n % 2, 0:1]
                    nc.vector.tensor_reduce(m, ps[:, 2 * (n % 2):2 * (n % 2) + 2, 0:HALF], mybir.AxisListType.XY,
                                            ALU.max).then_inc(mx_done, 1)
                else:
                    m = amx[:, n % 2, :]
                    nc.vector.tensor_reduce(m, ps[:, 2 * (n % 2), :].rearrange("p (a b) -> p a b", a=GRP), AX_X,
                                            ALU.max).then_inc(mx_done, 1)
                dve.wait_ge(mx_done, n + 1)
                nc.vector.tensor_scalar(m, m, -ATT_SCALE, None, ALU.mult).then_inc(nmx_done, 1)

            def att_normalise(n):
                dve.wait_ge(ex_done, n + 1)
                w_ = 1 if n < 4 * QH else GRP
                s = asum[:, n % 2, 0:w_]
                nc.vector.reciprocal(s, s).then_inc(rc_done, 1)
                dve.wait_ge(rc_done, n + 1)
                if w_ == 1:
                    nc.vector.tensor_scalar(pr[:, n % 2, :], pr[:, n % 2, :], s, None, ALU.mult).then_inc(pn_done, 1)
                else:
                    p_ = pr[:, n % 2, 0:512].rearrange("p (a b) -> p a b", a=GRP)
                    nc.vector.tensor_tensor(p_, p_, s[:, :, None].to_broadcast([P, GRP, P]), ALU.mult).then_inc(pn_done, 1)

            def att_lo(h):
                dve.wait_ge(ah_done, h + 1)
                if h < QH:
                    for a_, b_ in ((0, 0), (384, 256)):
                        last = nc.vector.tensor_tensor(hL[:, h, a_:a_ + 256], ps[:, 6, b_:b_ + 256],
                                                       hH[:, h, a_:a_ + 256].bitcast(F32), ALU.subtract)
                else:
                    hs = slice(GRP * (h - QH), GRP * (h - QH + 1))
                    last = nc.vector.tensor_tensor(hL[:, hs, 256:384], ps[:, 6, :].rearrange("p (a b) -> p a b", a=GRP),
                                                   hH[:, hs, 256:384].bitcast(F32), ALU.subtract)
                last.then_inc(attn_ready, 1)

            att_max(0)
            att_max(1)
            for n in range(4 * QH + KVH):
                att_normalise(n)
                if n % 4 == 0 and n:
                    att_lo(n // 4 - 1)
                if n + 2 < 4 * QH + KVH:
                    att_max(n + 2)
                if n < 4 * QH:
                    dve.wait_ge(pt_full, n + 1)
                    nc.vector.tensor_copy(pT[:, 4, (n % 4) * P:(n % 4 + 1) * P], ps[:, 5, 0:P]).then_inc(pt_dve, 1)
            att_lo(QH)
            att_lo(QH + 1)

            def wo(n):
                t, m = n // 4, n % 4
                residual(G_WO, V_WO, n, m // 2, 2 * t + m % 2, MOD1 + G1)

            for n in range(12):
                wo(n)
                if n % 2 == 1:
                    add_squares(3, n // 2, "tile")
            last_tile(3, "tile", wo, 12)

            with dve.Fori(0, FG - 1) as g:
                mlp_group(g, 1, False)
            update = mlp_group(FG - 1, 1, True)
            for n in range(12, 16):
                update(n)
                if n % 2 == 1:
                    add_squares(4, n // 2, "tile")
            for half in range(2):
                reciprocal_std(4, half)
                for k in range(KC):
                    x = xT[:, k, halfcols(half)]
                    nc.vector.scalar_tensor_tensor(out=x, in0=x, scalar=vecT[:, 0, R_FINAL + k:R_FINAL + k + 1],
                                                   in1=rstd[:, half, :], op0=ALU.mult, op1=ALU.mult).then_inc(y_done, 1)
            for tile in range(NT):
                dve.wait_ge(y_full, 2 * tile + 2)
                nc.vector.tensor_copy(y_nat[:, tile, 512:1024], ps[:, (2 * tile + 1) % 4, :]).then_inc(y_dve, 1)


_INS = ["x_prompt", "x_sample", "state_ret", "cache_k", "cache_v", "c", "c_ctx", "ada_w", "ada_b", "norm_g",
        "final_g", "even_w_in", "even_w_out", "conv_dw_w", "conv_dw_b", "conv_ln_g", "conv_ln_b",
        "ret_log_decay", "odd_w_qkv", "odd_q_g", "odd_k_g", "odd_w_o", "mlp_w1", "mlp_w2"]
_OUTS = [("y_prompt", (1, CTX, D)), ("y_sample", (1, LAT, D)), ("new_state", (1, 1, 2, RH, P, RV)),
         ("new_k", (1, 1, CTX, KVH, P)), ("new_v", (1, 1, CTX, KVH, P))]


def kernel(**inputs):
    import concourse.bacc as bacc
    from concourse.bass_utils import run_bass_kernel_spmd

    nc = bacc.Bacc("TRN2", target_bir_lowering=False, num_devices=1)
    shape_const, rope_const = shape_constants()
    arrays, args = {}, []
    for name in _INS + ["shape_const", "rope_const"]:
        a = {"shape_const": shape_const, "rope_const": rope_const}.get(name)
        a = np.ascontiguousarray(inputs[name]) if a is None else a
        arrays[f"in_{name}"] = a
        args.append(nc.dram_tensor(f"in_{name}", a.shape, mybir.dt.from_np(a.dtype), kind="ExternalInput").ap())
    for name, shape in _OUTS:
        args.append(nc.dram_tensor(f"out_{name}", shape, F32, kind="ExternalOutput").ap())
    hybrid_step(nc, *args)
    r = run_bass_kernel_spmd(nc, [arrays], core_ids=[0])
    return tuple(r.results[0][f"out_{name}"] for name, _ in _OUTS)
```

```python
from contextlib import ExitStack

import numpy as np

import concourse.bass as bass
from concourse import mybir

F32, F32R = mybir.dt.float32, mybir.dt.float32r
ALU, ACT = mybir.AluOpType, mybir.ActivationFunctionType
AX_X = mybir.AxisListType.X

P = 128
D = 1024
KC = D // P
LAT, CTX = 512, 128
T = LAT + CTX
HALF = T // 2
NT = T // P
CTX_TILE = 2
LAT_TILES = (0, 1, 3, 4)
EPS = 1e-6
CONV, WIDTH = 512, 31
CC = CONV // P
PAD = WIDTH // 2
ZW = PAD + LAT + PAD + CTX + PAD
CW = LAT + PAD + CTX
RH, RV = 4, 256
QH, KVH = 8, 2
GRP = QH // KVH
FF = 4 * D
FG = FF // D
GRID_W = 64
ATT_SCALE = float(P) ** -0.5
RET_SCALE = float(P) ** -0.5
KEYS = P + LAT

PAIRS = {"half": [(h, p) for h in range(2) for p in range(4)],
         "tile": [(h, p) for p in range(4) for h in range(2)],
         "wc": [(h, 2 * t + p) for t in range(2) for h in range(2) for p in range(2)]}
SUM_AT = {k: [sum(1 if p == 0 else 2 for _, p in v[:n + 1]) for n in range(8)] for k, v in PAIRS.items()}
SUMS = 14
CONV_MAP = ((0, 0, 256), (LAT + PAD, 256, CTX), (256, 384, 256))

SEGS = (((0, 256, 0), (256, 64, 1)), ((320, 64, 1), (384, 256, 0)))

T_GATE, T_VAL, T_HEADS = 0, 2, 4
T_WR = T_HEADS + 12
T_WC = T_WR + 4
T_MLP0 = T_WC + 2
T_QKV = T_MLP0 + 8 * FG
T_WO = T_QKV + 6
T_MLP1 = T_WO + 4
N_TILES = T_MLP1 + 8 * FG

G_X = 0
G_GATE = 16
G_VAL = G_GATE + 8
G_HEADS = G_VAL + 8
G_PAIR = 28
G_WR = G_HEADS + 2 * G_PAIR
G_WC = G_WR + 16
G_MLP0 = G_WC + 16
G_QKV = G_MLP0 + 32 * FG
G_WO = G_QKV + 30
G_MLP1 = G_WO + 16
A_HEADS, A_MLP0 = 8, 8 + 2 * G_PAIR
A_QKV = A_MLP0 + 16 * FG
A_MLP1 = A_QKV + 30
V_VAL, V_WR, V_WC, V_MLP0 = 16, 24, 40, 56
V_WO = V_MLP0 + 16 * FG
V_MLP1 = V_WO + 16
N_ATT = KVH + 4 * QH
VALUES_AT = {2: 0, 4: 1, **{KVH + 4 * h + 4: KVH + h for h in range(QH - 1)}}
NAT_BANKS = (0, 1, 2, 3, 7)

N_PRE = 16
N_MOD = 96
SH1, SC1, G1, SH2, SC2, G2 = (8 * s for s in range(6))
MOD1 = 48

R_C, R_NORM, R_FINAL, R_CB, R_LG, R_LB, R_END = 0, 16, 48, 56, 60, 64, 68

C_ID, C_PF, C_PB, C_QF, C_QB, C_KP, C_SEL = 0, 128, 256, 384, 512, 640, 642
C_END = 644


def shape_constants():
    c = np.zeros((P, C_END), np.float32)
    i, j = np.arange(P)[None, :], np.arange(P)[:, None]
    c[:, C_ID:C_ID + P] = np.eye(P)
    c[:, C_PF:C_PF + P] = np.maximum(i - j, 0)
    c[:, C_PB:C_PB + P] = np.maximum(j - i, 0)
    c[:, C_QF:C_QF + P] = i + 1
    c[:, C_QB:C_QB + P] = P - i
    c[:, C_KP] = P - 1 - np.arange(P)
    c[:, C_KP + 1] = np.arange(P)
    for s in range(4):
        c[32 * s, C_SEL] = c[32 * s + 1, C_SEL + 1] = 1
    half = P // 2
    pos = np.arange(LAT)
    inv = (np.float32(10000.0) ** (-np.arange(0, half, 2, dtype=np.float32) / half)).astype(np.float32)
    ang = np.concatenate([(pos // GRID_W).astype(np.float32)[:, None] * inv,
                          (pos % GRID_W).astype(np.float32)[:, None] * inv], axis=1)
    rope = np.zeros((P, 2, NT, half), np.float32)
    rope[:, 0, CTX_TILE] = 1.0
    for n, tile in enumerate(LAT_TILES):
        rope[:, 0, tile] = np.cos(ang[n * P:(n + 1) * P].astype(np.float64))
        rope[:, 1, tile] = np.sin(ang[n * P:(n + 1) * P].astype(np.float64))
    return c, rope


def by_feature_chunk(inputs):
    out = np.zeros((P, 3, P), np.float32)
    for b, at, names in ((0, R_C, ("c", "c_ctx", "norm_g", "final_g", "conv_dw_b", "conv_ln_g", "conv_ln_b")),
                         (1, 0, ("ada_b",)), (2, 0, ("conv_dw_w",))):
        for name in names:
            a = np.asarray(inputs[name]).reshape(-1, P)
            out[:, b, at:at + len(a)] = a.T
            at += len(a)
    return out


def hybrid_step(nc, x_prompt, x_sample, state_ret, cache_k, cache_v, ada_w, even_w_in, even_w_out,
                ret_log_decay, odd_w_qkv, odd_q_g, odd_k_g, odd_w_o, mlp_w1, mlp_w2, feature_vectors,
                shape_const, rope_const, y_prompt, y_sample, new_state, new_k, new_v):
    ctx = ExitStack()
    with ctx:
        here = [(nc.sbuf_base + 31) // 32 * 32]

        def place(name, shape, dt=F32):
            at = here[0]
            here[0] += (int(np.prod(shape[1:])) * 4 + 31) // 32 * 32
            return nc.alloc_sbuf_tensor_at(name, shape, dt, offset=at)

        xT = place("xT", [P, KC, T])
        h_at = here[0]
        hH = place("hH", [P, KC, T], F32R)
        hL = place("hL", [P, KC, T], F32R)
        raw = place("raw", [P, 2, 1024])
        wH = place("wH", [P, 2, 2048], F32R)
        wL = place("wL", [P, 2, 2048], F32R)
        ada = place("ada", [P, 2, KC, P])
        const = place("const", [P, C_END])
        ones = place("ones", [P, P])
        eps = place("eps", [P, 1])
        vecT = place("vecT", [P, 3, P])
        siluc = place("siluc", [P, KC, 32])
        ada_sb = place("ada_sb", [P, P])
        modT = place("modT", [P, N_MOD, 2])
        coef = place("coef", [P, 4, KC, 2])
        norm_buffers = here[0]
        ssum = place("ssum", [P, 2, HALF])
        rstd = place("rstd", [P, 2, HALF])
        ub = place("ub", [P, 2, HALF])
        sqb = place("sqb", [P, 2, HALF])
        tb = place("tb", [P, 2, HALF])
        lg = place("lg", [P, 2, RH])
        kdec = place("kdec", [P, 2, RH])
        cdec = place("cdec", [P, 2, RH])
        arena = here[0]

        x_nat = place("x_nat", [P, NT, D])
        pre_over_h = nc.alloc_sbuf_tensor_at("pre_over_h", [P, 2, KC, 4 * P], F32, offset=h_at)
        pre_sb = nc.alloc_sbuf_tensor_at("pre_sb", [P, 2, 4 * P], F32, offset=h_at + 2 * KC * 4 * P * 4)
        pre_arena = place("pre_arena", [P, 2, KC, 4 * P])
        here[0] = arena
        ret = place("ret", [P, NT, RH * RV])
        zp = place("zp", [P, CC, ZW])
        cacc = place("cacc", [P, CC, CW])
        head_arena = here[0]
        qT = place("qT", [P, 2, T])
        kT = place("kT", [P, 2, T])
        v_nat = place("v_nat", [P, NT, RV])
        gate = place("gate", [P, NT, RV])
        qdec = place("qdec", [P, 2, T])
        kd_nat = place("kd_nat", [P, 2, NT, P])
        S = place("S", [P, 2, 4, RV])
        here[0] = norm_buffers
        dmat = place("dmat", [P, 2, P])
        qtab = place("qtab", [P, 2, P])
        here[0] = norm_buffers + 4 * T
        state_out = place("state_out", [P, 2, RV])
        bst = place("bst", [P, NT, 6])
        bmv = place("bmv", [P, NT, 2])
        brs = place("brs", [P, NT, 1])
        here[0] = norm_buffers + 8 * T
        prob = place("prob", [P, T])
        sgate = nc.alloc_sbuf_tensor_at("sgate", [P, CC, T], F32, offset=arena)
        here[0] = head_arena
        cH = place("cH", [P, CC, T], F32R)
        cL = place("cL", [P, CC, T], F32R)
        cst = place("cst", [P, 2, T])
        cmp_ = place("cmp", [P, 2, T])
        here[0] = arena
        fH = place("fH", [P, KC, T], F32R)
        fL = place("fL", [P, KC, T], F32R)
        fr = place("fr", [P, 2, HALF])
        fs = place("fs", [P, 2, HALF])
        here[0] = arena
        q_nat = place("q_nat", [P, 2, NT, RV])
        k_nat = place("k_nat", [P, NT, RV])
        va = place("va", [P, NT + 1, RV])
        kc_nat = place("kc_nat", [P, RV])
        behind_values = here[0]
        kro = place("kro", [P, NT, RV])
        qro = place("qro", [P, NT, RV])
        rtmp = place("rtmp", [P, 2, NT, 2, 64])
        rn = place("rn", [P, NT, RV])
        rss = place("rss", [P, NT * 2])
        tabs = place("tabs", [P, 2, 4, NT, 64])
        rope_sb = nc.alloc_sbuf_tensor_at("rope_sb", [P, 2, NT, 64], F32, offset=here[0])
        gqk = nc.alloc_sbuf_tensor_at("gqk", [P, 2, P], F32, offset=here[0] + 2 * NT * 64 * 4)
        kTa = place("kTa", [P, KVH, P + KEYS])
        qTa = place("qTa", [P, QH, T])
        here[0] = arena
        pr = place("pr", [P, 2, KEYS])
        pT = nc.alloc_sbuf_tensor_at("pT", [P, 2, NT, LAT], F32, offset=behind_values)
        amx = place("amx", [P, 2, 4])
        asum = place("asum", [P, 2, 4])
        here[0] = arena
        y_nat = place("y_nat", [P, NT, D])

        ident = const[:, C_ID:C_ID + P]
        sel = const[:, C_SEL:C_SEL + 2]

        ps = ctx.enter_context(nc.psum_tensor("ps", [P, 8, 512], F32))
        B_ADA = 4

        def sem(name):
            return ctx.enter_context(nc.semaphore(name))

        vec_in, const_in = sem("vec_in"), sem("const_in")
        x_in = [sem("x_in0"), sem("x_in1")]
        pre_in = [sem(f"pre_in{j}") for j in range(N_PRE // 4)]
        raw_in = [sem("raw_in0"), sem("raw_in1")]
        ada_in = [sem("ada_in0"), sem("ada_in1")]
        s0_in, att_in, store = sem("s0_in"), sem("att_in"), sem("store")
        act_dma, k_st, v_st = sem("act_dma"), sem("k_st"), sem("v_st")
        wh_done, wl_done = sem("wh_done"), sem("wl_done")
        acc_full, act_free, dve_free = sem("acc_full"), sem("act_free"), sem("dve_free")
        set_up, siluc_ready = sem("set_up"), sem("siluc_ready")
        pre_strips, pre_ev, pre_fin, pre_mod = sem("pre_strips"), sem("pre_ev"), sem("pre_fin"), sem("pre_mod")
        ada_strips, ada_ev, ada_fin, mod_done = sem("ada_strips"), sem("ada_ev"), sem("ada_fin"), sem("mod_done")
        coef_done = sem("coef_done")
        sq_done, sum_done, stat_full, std_done = sem("sq_done"), sem("sum_done"), sem("stat_full"), sem("std_done")
        rstd_done, u_done, t_done, hh_done, h_ready = (sem("rstd_done"), sem("u_done"), sem("t_done"),
                                                       sem("hh_done"), sem("h_ready"))
        conv_done, cn_sum, csum_done, crec_done = sem("conv_done"), sem("cn_sum"), sem("csum_done"), sem("crec_done")
        cstat_in, cstat_full, csq_done, cstd_done = sem("cstat_in"), sem("cstat_full"), sem("csq_done"), sem("cstd_done")
        cx_done, cn_done, csilu_done, ch_done, cl_done = (sem("cx_done"), sem("cn_done"), sem("csilu_done"),
                                                          sem("ch_done"), sem("cl_done"))
        lg_raw, lg_done, dec_done = sem("lg_raw"), sem("lg_done"), sem("dec_done")
        dexp_done, dm_done = sem("dexp_done"), sem("dm_done")
        st_full, prob_done, qdec_done, kd_done = sem("st_full"), sem("prob_done"), sem("qdec_done"), sem("kd_done")
        u_full, s_done, so_done, o_full, o_out = sem("u_full"), sem("s_done"), sem("so_done"), sem("o_full"), sem("o_out")
        bn_done, bstd_done, brs_done, on_done, ret_done = (sem("bn_done"), sem("bstd_done"), sem("brs_done"),
                                                           sem("on_done"), sem("ret_done"))
        rt_full, rth_done, rtl_done = sem("rt_full"), sem("rth_done"), sem("rtl_done")
        fr_done, fs_done, fh_done, f_ready = sem("fr_done"), sem("fs_done"), sem("fh_done"), sem("f_ready")
        tab_done, rsq_done, rss_done, rstd2, rrec = sem("tab_done"), sem("rsq_done"), sem("rss_done"), sem("rstd2"), sem("rrec")
        rn_done, rm_done, ro_done = sem("rn_done"), sem("rm_done"), sem("ro_done")
        tr_full, tr_out = sem("tr_full"), sem("tr_out")
        sc_full, mx_done, nmx_done, ex_done = sem("sc_full"), sem("mx_done"), sem("nmx_done"), sem("ex_done")
        rc_done, pn_done, pt_full, pt_act, pt_dve = (sem("rc_done"), sem("pn_done"), sem("pt_full"),
                                                     sem("pt_act"), sem("pt_dve"))
        pv_full, ah_done, attn_ready = sem("pv_full"), sem("ah_done"), sem("attn_ready")
        y_done, y_full, y_act, y_dve = sem("y_done"), sem("y_full"), sem("y_act"), sem("y_dve")

        pre_w = [pre_over_h[:, 0], pre_over_h[:, 1], pre_arena[:, 0], pre_arena[:, 1]]

        block = ctx.enter_context(nc.Block())

        @block.sync
        def _(sp):
            def cols(w, k0, nk, c0, n):
                return w[k0 * P:(k0 + nk) * P, bass.ds(c0, n)].rearrange("(k p) n -> p k n", p=P)

            def load_tile(t, halves, first=False):
                for j, src in enumerate(halves):
                    if not first:
                        sp.wait_ge(wl_done, 2 * t - 1 + j)
                    n = src.shape[2]
                    sp.dma_start(raw[:, j, :].rearrange("p (k n) -> p k n", n=n), src).then_inc(raw_in[j], 16)

            def k8(w, c0, row0=0):
                return [w[row0 + 512 * j:row0 + 512 * (j + 1), bass.ds(c0, 256)]
                        .rearrange("(k p) n -> p k n", p=P) for j in range(2)]

            def load_ada(n, slot, layer, col, first=False):
                if not first:
                    sp.wait_ge(ada_strips, n - N_PRE - 1)
                sp.dma_start(ada[:, slot], ada_w[layer, :, bass.ds(col, P)]
                             .rearrange("(k p) n -> p k n", p=P)).then_inc(ada_in[slot], 16)

            sp.dma_start(vecT[:], feature_vectors).then_inc(vec_in, 16)
            sp.dma_start(const[:], shape_const).then_inc(const_in, 16)

            def load_x(half, tiles):
                for tile in tiles:
                    src = x_prompt[0] if tile == CTX_TILE else x_sample[0, LAT_TILES.index(tile) * P:][:P]
                    sp.dma_start(x_nat[:, tile, :], src).then_inc(x_in[half], 16)

            def load_pre(j):
                sp.dma_start(pre_w[j], ada_w[0, :, 4 * j * P:4 * (j + 1) * P].rearrange("(k p) n -> p k n", p=P)).then_inc(pre_in[j], 16)

            load_x(0, (0, 1, CTX_TILE))
            load_pre(0)
            load_x(1, (3, 4))
            load_pre(1)
            load_pre(2)
            load_tile(0, k8(even_w_in[0], CONV), first=True)
            load_pre(3)
            for t in range(4):
                if t:
                    load_tile(t, k8(even_w_in[0], (CONV, CONV + 256, 0, 256)[t]))
                for a in range(2):
                    load_ada(16 + 2 * t + a, a, 0, (16 + 2 * t + a) * P, first=(t == 0))
            with sp.Fori(0, 2) as i:
                for b in range(6):
                    col = (1024 + 256 * i, 1536 + 256 * i, 2048 + 512 * i, 3072 + 512 * i,
                           2304 + 512 * i, 3328 + 512 * i)[b]
                    load_tile(T_HEADS + 6 * i + b, k8(even_w_in[0], col))
                    for a in range(2):
                        n = 24 + 12 * i + 2 * b + a
                        load_ada(n, a, 0, n * P)
                    if b in (2, 5):
                        head = 2 * i + (b == 5)
                        sp.wait_ge(acc_full, G_HEADS + G_PAIR * i + (17 if b == 5 else -1))
                        for r in range(2):
                            sp.dma_start(S[:, r, 3 * r, :], state_ret[0, 0, r, bass.ds(head, 1)]
                                         .rearrange("a d e -> (a d) e")).then_inc(s0_in, 16)
            for t in range(4):
                load_tile(T_WR + t, k8(even_w_out[0], 256 * t, CONV))
            for t in range(2):
                load_tile(T_WC + t, [even_w_out[0, 256 * j:256 * (j + 1), 512 * t:512 * (t + 1)]
                                     .rearrange("(k p) n -> p k n", p=P) for j in range(2)])

            def load_mlp(layer, first_tile):
                with sp.Fori(0, FG) as g:
                    for b in range(8):
                        if b < 4:
                            halves = k8(mlp_w1[layer], 1024 * g + 256 * b)
                        else:
                            halves = [mlp_w2[layer, bass.ds(1024 * g + 512 * j, 512), 256 * (b - 4):256 * (b - 3)]
                                      .rearrange("(k p) n -> p k n", p=P) for j in range(2)]
                        load_tile(first_tile + 8 * g + b, halves)
                        if layer == 0:
                            for q in ((2 * b, 2 * b + 1) if b < 4 else (4 + b,)):
                                load_ada(MOD1 + 12 * g + q, q % 2, 1, (12 * g + q) * P)

            load_mlp(0, T_MLP0)
            sp.dma_start(rope_sb[:], rope_const).then_inc(att_in, 16)
            sp.dma_start(gqk[:, 0, :], odd_q_g[0].partition_broadcast(P)).then_inc(att_in, 16)
            sp.dma_start(gqk[:, 1, :], odd_k_g[0].partition_broadcast(P)).then_inc(att_in, 16)
            load_tile(T_QKV, k8(odd_w_qkv[0], 1024))
            load_tile(T_QKV + 1, k8(odd_w_qkv[0], 0))
            sp.wait_ge(acc_full, G_QKV)
            sp.dma_start(kc_nat[:], cache_k[0, 0].rearrange("t h d -> t (h d)")).then_inc(att_in, 16)
            sp.dma_start(va[:, NT, :], cache_v[0, 0].rearrange("t h d -> t (h d)")).then_inc(att_in, 16)
            for t in range(2, 6):
                load_tile(T_QKV + t, k8(odd_w_qkv[0], (256, 512, 768, 1280)[t - 2]))
            for t in range(2):
                load_tile(T_WO + t, k8(odd_w_o[0], 256 * t))
            sp.wait_ge(ro_done, 2)
            sp.dma_start(new_k[0, 0].rearrange("t h d -> t (h d)"), kro[:, CTX_TILE, :]).then_inc(k_st, 16)
            sp.wait_ge(act_free, A_QKV + 30)
            sp.dma_start(new_v[0, 0].rearrange("t h d -> t (h d)"), va[:, CTX_TILE, :]).then_inc(v_st, 16)
            for t in range(2, 4):
                load_tile(T_WO + t, k8(odd_w_o[0], 256 * t))
            load_mlp(1, T_MLP1)
            for tile in range(NT):
                sp.wait_ge(y_act, tile + 1)
                sp.wait_ge(y_dve, tile + 1)
                if tile == CTX_TILE:
                    dst = y_prompt[0]
                else:
                    n = LAT_TILES.index(tile)
                    dst = y_sample[0, n * P:(n + 1) * P, :]
                sp.dma_start(dst, y_nat[:, tile, :]).then_inc(store, 16)
            sp.wait_ge(store, 16 * NT)
            sp.wait_ge(k_st, 16)
            sp.wait_ge(v_st, 16)
            sp.wait_ge(act_dma, 16 * (RH + 1))

        @block.tensor
        def _(pe):
            def product(bank, lhs, rhs, nk, waits=None, width=HALF):
                last = None
                for k in range(nk):
                    if waits:
                        waits(k)
                    (aH, aL), (bH, bL) = lhs(k), rhs(k)
                    for p_, (a_, b_) in enumerate(((aH, bH), (aH, bL), (aL, bH))):
                        last = nc.tensor.matmul(ps[:, bank, 0:width], a_, b_, start=(k == 0 and p_ == 0),
                                                stop=(k == nk - 1 and p_ == 2))
                last.then_inc(acc_full, 1)

            def w_wait(t, k, nk):
                if k == 0:
                    pe.wait_ge(wl_done, 2 * t + 1)
                elif k == nk // 2:
                    pe.wait_ge(wl_done, 2 * t + 2)

            def tile_t(t, slot, xH, xL, free, x_wait=None, hooks=None, nk=KC, nm=2, bank0=0):
                for half in range(2):
                    for m in range(nm):
                        n = half * nm + m
                        free(n)

                        def waits(k, n=n, half=half, m=m):
                            if n == 0:
                                w_wait(t, k, nk)
                            if x_wait and m == 0:
                                x_wait(half, k)
                        wv = [w[:, slot, :].rearrange("p (k n) -> p k n", k=nk) for w in (wH, wL)]
                        product((bank0 + n) % 4, lambda k: [w[:, k, m * P:(m + 1) * P] for w in wv],
                                lambda k: [x[:, k, half * HALF:(half + 1) * HALF] for x in (xH, xL)], nk, waits)
                        if hooks and n in hooks:
                            for hook in hooks[n]:
                                hook()

            def tile_n(t, slot, free, banks, x_wait=None, hooks=None):
                wv = [w[:, slot, :].rearrange("p (k n) -> p k n", k=KC) for w in (wH, wL)]
                for n in range(NT):
                    free(n)

                    def waits(k, n=n):
                        if n == 0:
                            w_wait(t, k, KC)
                        if x_wait and n in (0, 2):
                            x_wait(n // 2, k)
                    product(banks[n], lambda k: [x[:, k, n * P:(n + 1) * P] for x in (hH, hL)],
                            lambda k: [w[:, k, :] for w in wv], KC, waits, width=256)
                    if hooks and n in hooks:
                        for hook in hooks[n]:
                            hook()

            def strips(n, slot, full):
                pe.wait_ge(ada_in[slot], full)
                if not (isinstance(n, int) and n == N_PRE):
                    pe.wait_ge(mod_done, n - N_PRE)
                for k in range(KC):
                    j = k % 4
                    last = nc.tensor.matmul(ps[32 * j:32 * j + 32, B_ADA, 0:P], siluc[:, k, :], ada[:, slot, k, :],
                                            start=(k < 4), stop=(k >= 4), tile_position=(0, 32 * j))
                last.then_inc(ada_strips, 1)

            def finish(n):
                pe.wait_ge(ada_ev, n - N_PRE + 1)
                nc.tensor.matmul(ps[:, B_ADA, 256:258], ada_sb[:], sel, start=True, stop=True).then_inc(ada_fin, 1)

            def ada_hooks(n, full, count=2):
                out = {}
                for a in range(count):
                    out.setdefault(2 * a, []).append(lambda a=a: strips(n + a, a, full(a)))
                    out.setdefault(2 * a + 1, []).append(lambda a=a: finish(n + a))
                return out

            def stat(norm, half, count):
                pe.wait_ge(sum_done, SUMS * norm + count)
                nc.tensor.matmul(ps[:, 5 + half, 0:HALF], ones[:], ssum[:, half, :], start=True,
                                 stop=True).then_inc(stat_full, 1)

            def h_wait(norm):
                return lambda half, k: pe.wait_ge(h_ready, 16 * norm + 8 * half + k + 1)

            def turn(bank, src, col0):
                def one(tile, p0, np_, at, last=False):
                    return nc.tensor.transpose(ps[:, bank, at:at + np_], src[p0:p0 + np_, tile, col0:col0 + P],
                                               ident[p0:p0 + np_, p0:p0 + np_])
                return one

            def turn_half(bank, src, col0, half, full):
                one = turn(bank, src, col0)
                if half == 0:
                    one(0, 0, P, 0)
                    one(1, 0, P, P)
                    last = one(CTX_TILE, 0, 64, 256)
                else:
                    one(CTX_TILE, 64, 64, 0)
                    one(3, 0, P, 64)
                    last = one(4, 0, P, 192)
                last.then_inc(full, 1)

            pe.wait_ge(const_in, 16)

            def x_group(n):
                if n == 0:
                    pe.wait_ge(x_in[0], 3 * 16)
                elif n == 8:
                    pe.wait_ge(x_in[1], 2 * 16)
                if n >= 4:
                    pe.wait_ge(dve_free, n - 3)
                turn_half(n % 4, x_nat, (n % 8) * P, n // 8, acc_full)

            def pre_strip(j):
                pe.wait_ge(pre_in[j], 16)
                if j:
                    pe.wait_ge(pre_ev, j)
                for k in range(KC):
                    q = k % 4
                    last = nc.tensor.matmul(ps[32 * q:32 * q + 32, B_ADA, :], siluc[:, k, :], pre_w[j][:, k, :],
                                            start=(k < 4), stop=(k >= 4), tile_position=(0, 32 * q))
                last.then_inc(pre_strips, 1)

            def pre_finish(j):
                pe.wait_ge(pre_ev, j + 1)
                if j >= 2:
                    pe.wait_ge(pre_mod, j - 1)
                for q in range(4):
                    last = nc.tensor.matmul(ps[:, 6 + j % 2, 2 * q:2 * q + 2], pre_sb[:, j % 2, q * P:(q + 1) * P], sel,
                                            start=True, stop=True)
                last.then_inc(pre_fin, 1)

            for n in range(6):
                x_group(n)
            pe.wait_ge(siluc_ready, 1)
            for j, (n0, n1) in enumerate(((6, 9), (9, 13), (13, 16), (16, 16))):
                if j == 3:
                    stat(0, 0, SUM_AT["half"][3])
                    pe.wait_ge(pre_mod, 3)
                    stat(0, 1, SUM_AT["half"][7])
                pre_strip(j)
                for n in range(n0, n1):
                    x_group(n)
                pre_finish(j)

            for t in range(4):
                if t < 2:
                    free = lambda n, t=t: (pe.wait_ge(dve_free, 13 + n) if t == 0 else pe.wait_ge(act_free, n + 1))
                else:
                    free = lambda n, t=t: (pe.wait_ge(act_free, 5 + n) if t == 2
                                           else pe.wait_ge(dve_free, V_VAL + n + 1))
                tile_t(t, t % 2, hH, hL, free, h_wait(0) if t == 0 else None,
                       ada_hooks(16 + 2 * t, lambda a, t=t: 16 * (1 + t)))

            def scores(i, e):
                pe.wait_ge(act_free, A_HEADS + G_PAIR * i + (18 if e else 8))
                k_of = lambda tile: kT[:, e, tile * P:(tile + 1) * P]
                q_of = lambda tile: qT[:, e, tile * P:(tile + 1) * P]
                for n, tile in enumerate(LAT_TILES):
                    last = nc.tensor.matmul(ps[:, 5, n * P:(n + 1) * P], k_of(tile), q_of(tile), start=True, stop=True)
                last.then_inc(st_full, 1)
                nc.tensor.matmul(ps[:, 7, 0:P], k_of(CTX_TILE), q_of(CTX_TILE), start=True, stop=True)
                nc.tensor.transpose(ps[:, 7, P:2 * P], k_of(CTX_TILE), ident).then_inc(st_full, 1)
                for n, tile in enumerate(LAT_TILES):
                    last = nc.tensor.transpose(ps[:, 6, n * P:(n + 1) * P], k_of(tile), ident)
                last.then_inc(st_full, 1)

            def update(bank, at, r, tile):
                return nc.tensor.matmul(ps[:, bank, at:at + RV], kd_nat[:, r, tile, :], v_nat[:, tile, :],
                                        start=True, stop=True)

            def updates_1(i, e):
                head = 2 * i + e
                pe.wait_ge(kd_done, 4 * head + 4)
                pe.wait_ge(prob_done, 2 * head + 2)
                pe.wait_ge(act_free, A_HEADS + G_PAIR * i + 13 + 10 * e)
                for bank, (a_, b_) in ((5, ((0, 0), (0, 1))), (6, ((0, 3), (0, CTX_TILE))), (7, ((1, 4), (1, 3)))):
                    update(bank, 0, *a_)
                    update(bank, RV, *b_).then_inc(u_full, 1)

            def updates_2(i, e):
                pe.wait_ge(s_done, 6 * (2 * i + e) + 2)
                update(5, 0, 1, 1)
                update(5, RV, 1, CTX_TILE).then_inc(u_full, 1)

            def outputs(i, e):
                head = 2 * i + e
                pe.wait_ge(s_done, 6 * head + 6)
                pe.wait_ge(so_done, 2 * head + 2)
                pe.wait_ge(qdec_done, 4 * head + 4)
                for tile in range(NT):
                    out = ps[:, 5 + tile // 2, (tile % 2) * RV:(tile % 2 + 1) * RV]
                    cs = slice(tile * P, (tile + 1) * P)
                    ctx_ = tile == CTX_TILE
                    last = nc.tensor.matmul(out, prob[:, cs], v_nat[:, tile, :], start=True, stop=ctx_)
                    if not ctx_:
                        n = LAT_TILES.index(tile)
                        for r in range(2):
                            last = nc.tensor.matmul(out, qdec[:, r, cs], S[:, r, n, :], start=False, stop=(r == 1))
                    if tile in (1, 3, 4):
                        last.then_inc(o_full, 1)

            with pe.Fori(0, 2) as i:
                at = 0
                for b in range(6):
                    t = T_HEADS + 6 * i + b
                    hooks = ada_hooks(24 + 12 * i + 2 * b, lambda a, b=b: 16 * (5 + 6 * i + b))
                    free = lambda n, at=at: pe.wait_ge(act_free, A_HEADS + G_PAIR * i + at + n - 3)
                    if b == 0:
                        free0 = free

                        def free(n, free0=free0):
                            if n < 4:
                                pe.wait_ge(dve_free, V_WR - 3 + n)
                            free0(n)
                    if b < 2:
                        tile_t(t, b % 2, hH, hL, free, None, hooks)
                        at += 4
                        continue
                    e = (b - 2) // 2
                    if b % 2 == 0:
                        hooks[0].append(lambda e=e: scores(i, e))
                    else:
                        hooks[0].append(lambda e=e: updates_1(i, e))
                        hooks[1].append(lambda e=e: updates_2(i, e))
                        hooks[2].append(lambda e=e: outputs(i, e))
                    tile_n(t, b % 2, free, [(at + n) % 4 for n in range(NT)], None, hooks)
                    at += 5

            def turn_retention(n):
                pe.wait_ge(ret_done, n % 8 // 2 + 1)
                if n >= 4:
                    pe.wait_ge(rtl_done, n - 3)
                elif n == 0:
                    pe.wait_ge(mod_done, MOD1 - N_PRE)
                    pe.wait_ge(act_free, A_MLP0)
                turn_half(4 + n % 4, ret, (n % 8) * P, n // 8, rt_full)

            for n in range(8):
                turn_retention(n)

            def channel_stat(which):
                pe.wait_ge(cstat_in, which + 1)
                nc.tensor.matmul(ps[:, 5, 0:LAT], ones[:], cst[:, which, 0:LAT], start=True, stop=True)
                nc.tensor.matmul(ps[:, 6, 0:CTX], ones[:], cst[:, which, LAT:T], start=True,
                                 stop=True).then_inc(cstat_full, 1)

            for t in range(4):
                def free(n, t=t):
                    if t == 0 and n < 4:
                        pe.wait_ge(act_free, A_MLP0 - 3 + n)
                    else:
                        pe.wait_ge(dve_free, V_WR + 4 * t + n - 3)
                tile_t(T_WR + t, t % 2, hH, hL, free,
                       (lambda half, k: pe.wait_ge(rtl_done, 8 * half + k + 1)) if t == 0 else None,
                       {0: {0: [lambda n=n: turn_retention(n) for n in range(8, 16)], 2: [lambda: channel_stat(0)]},
                        1: {2: [lambda: channel_stat(1)]}}.get(t))
            pe.wait_ge(cl_done, 2 * CC)
            for t in range(2):
                tile_t(T_WC + t, t % 2, cH, cL, lambda n, t=t: pe.wait_ge(dve_free, V_WC + 8 * t + n - 3),
                       nk=CC, nm=4, hooks={6: [lambda: stat(1, 0, SUM_AT["wc"][5])]} if t else None)
            stat(1, 1, SUM_AT["wc"][7])

            def mlp_group(g, layer, norm, last):
                t0, a0, v0, f0 = ((T_MLP0, A_MLP0, V_MLP0, 0), (T_MLP1, A_MLP1, V_MLP1, 64))[layer]
                for b in range(4):
                    hooks = None
                    if layer == 0:
                        hooks = ada_hooks(MOD1 + 12 * g + 2 * b, lambda a, b=b: 16 * (17 + 6 * g + b))
                    tile_t(t0 + 8 * g + b, b % 2, hH, hL,
                           lambda n, b=b: (pe.wait_ge(dve_free, v0 + 16 * g - 3 + n) if b == 0
                                           else pe.wait_ge(act_free, a0 + 16 * g + 4 * b + n - 3)),
                           h_wait(norm) if b == 0 else None, hooks)
                for b in range(4):
                    hooks = {}
                    if layer == 0:
                        n_ = MOD1 + 12 * g + 8 + b
                        hooks = {0: [lambda n_=n_, b=b: strips(n_, b % 2, 16 * (21 + 6 * g + b // 2))],
                                 1: [lambda n_=n_: finish(n_)]}
                    if last and b == 3:
                        hooks.setdefault(2, []).append(lambda: stat(norm + 1, 0, SUM_AT["tile"][6]))
                    tile_t(t0 + 8 * g + 4 + b, b % 2, fH, fL,
                           lambda n, b=b: (pe.wait_ge(act_free, a0 + 16 * g + 13 + n) if b == 0
                                           else pe.wait_ge(dve_free, v0 + 16 * g + 4 * b + n - 3)),
                           (lambda half, k: pe.wait_ge(f_ready, f0 + 16 * g + 4 * (k // 2) + 2 * half + k % 2 + 1))
                           if b == 0 else None, hooks)
                if last:
                    stat(norm + 1, 1, SUM_AT["tile"][7])

            with pe.Fori(0, FG - 1) as g:
                mlp_group(g, 0, 1, False)
            mlp_group(FG - 1, 0, 1, True)

            def turn_keys():
                pe.wait_ge(ro_done, 2)
                pe.wait_ge(att_in, 16 * 5)
                for h in range(KVH):
                    cs = slice(h * P, (h + 1) * P)
                    for n, tile in enumerate(LAT_TILES):
                        last = nc.tensor.transpose(ps[:, 4 + h, n * P:(n + 1) * P], kro[:, tile, cs], ident)
                    last.then_inc(tr_full, 1)
                    nc.tensor.transpose(ps[:, 6, 2 * h * P:(2 * h + 1) * P], kro[:, CTX_TILE, cs], ident)
                    last = nc.tensor.transpose(ps[:, 6, (2 * h + 1) * P:(2 * h + 2) * P], kc_nat[:, cs], ident)
                last.then_inc(tr_full, 1)

            def turn_queries(r):
                pe.wait_ge(ro_done, 2 * r + 4)
                pe.wait_ge(tr_out, 3 * (r + 1))
                for h in range(2):
                    cs = slice(h * P, (h + 1) * P)
                    for n, tile in enumerate(LAT_TILES):
                        last = nc.tensor.transpose(ps[:, 4 + h, n * P:(n + 1) * P], qro[:, tile, cs], ident)
                    last.then_inc(tr_full, 1)
                    last = nc.tensor.transpose(ps[:, 6, h * P:(h + 1) * P], qro[:, CTX_TILE, cs], ident)
                last.then_inc(tr_full, 1)

            for t in range(6):
                def free(n, t=t):
                    if t == 0:
                        if n < 4:
                            pe.wait_ge(dve_free, V_WO - 3 + n)
                    else:
                        pe.wait_ge(act_free, A_QKV + 5 * (t - 1) + n + 1)
                tile_n(T_QKV + t, t % 2, free, NAT_BANKS, h_wait(2) if t == 0 else None)
                if t == 1:
                    turn_keys()
                elif t > 1:
                    turn_queries(t - 2)

            def att_scores(n):
                if n >= 2:
                    pe.wait_ge(ex_done, n - 1)
                if n >= KVH:
                    h, i = (n - KVH) // 4, (n - KVH) % 4
                    for j in range(2):
                        last = nc.tensor.matmul(ps[:, 2 * (n % 2) + j, 0:HALF], qTa[:, h, i * P:(i + 1) * P],
                                                kTa[:, h // GRP, P + j * HALF:P + (j + 1) * HALF], start=True, stop=True)
                else:
                    for j in range(GRP):
                        last = nc.tensor.matmul(ps[:, 2 * (n % 2), j * P:(j + 1) * P], qTa[:, GRP * n + j, LAT:T],
                                                kTa[:, n, 0:P], start=True, stop=True)
                last.then_inc(sc_full, 1)

            def att_turn(n):
                pe.wait_ge(pn_done, n + 1)
                if n >= 2:
                    pe.wait_ge(pt_act, n - 1)
                bank = 4 if n % 2 == 0 else 7
                for j in range(4):
                    last = nc.tensor.transpose(ps[:, bank, j * P:(j + 1) * P], pr[:, n % 2, j * P:(j + 1) * P], ident)
                if n >= KVH:
                    if n > KVH:
                        pe.wait_ge(pt_dve, n - KVH)
                    last = nc.tensor.transpose(ps[:, 5, 0:P], pr[:, n % 2, 4 * P:5 * P], ident)
                last.then_inc(pt_full, 1)

            def att_values(v):
                if v >= 1:
                    pe.wait_ge(attn_ready, v)
                if v < KVH:
                    pe.wait_ge(pt_act, v + 1)
                    last = nc.tensor.matmul(ps[:, 6, :], va[:, CTX_TILE, v * P:(v + 1) * P], pT[:, 1, v, :],
                                            start=True, stop=True)
                else:
                    h = v - KVH
                    pe.wait_ge(pt_act, KVH + 4 * h + 4)
                    pe.wait_ge(pt_dve, 4 * h + 4)
                    kv = h // GRP
                    for n, vt in enumerate((NT,) + LAT_TILES):
                        last = nc.tensor.matmul(ps[:, 6, :], va[:, vt, kv * P:(kv + 1) * P], pT[:, h % 2, n, :],
                                                start=(n == 0), stop=(n == 4))
                last.then_inc(pv_full, 1)

            pe.wait_ge(tr_out, 15)
            pe.wait_ge(act_free, A_QKV + 30)
            att_scores(0)
            att_scores(1)
            for n in range(N_ATT):
                if n + 2 < N_ATT:
                    att_scores(n + 2)
                att_turn(n)
                if n in VALUES_AT:
                    att_values(VALUES_AT[n])
            att_values(KVH + QH - 1)

            for t in range(4):
                tile_t(T_WO + t, t % 2, hH, hL,
                       lambda n, t=t: (None if t == 0 else pe.wait_ge(dve_free, V_WO + 4 * t + n - 3)),
                       (lambda half, k: pe.wait_ge(attn_ready, KVH + k + 1)) if t == 0 else None,
                       hooks={2: [lambda: stat(3, 0, SUM_AT["tile"][6])]} if t == 3 else None)
            stat(3, 1, SUM_AT["tile"][7])

            with pe.Fori(0, FG - 1) as g:
                mlp_group(g, 1, 3, False)
            mlp_group(FG - 1, 1, 3, True)

            for tile in range(NT):
                pe.wait_ge(y_done, 8 if tile < 2 else 16)
                for kq in range(2):
                    n = 2 * tile + kq
                    if n >= 4:
                        pe.wait_ge(y_dve if kq else y_act, tile - 1)
                    for j in range(4):
                        last = nc.tensor.transpose(ps[:, n % 4, j * P:(j + 1) * P],
                                                   xT[:, 4 * kq + j, tile * P:(tile + 1) * P], ident)
                    last.then_inc(y_full, 1)


        @block.scalar
        def _(act):
            def seg(x, half, s):
                c0, n, which = SEGS[half][s]
                return x[..., c0:c0 + n], which

            def split(t, slot, start=None):
                if start is not None:
                    act.wait_ge(acc_full, start)
                for j in range(2):
                    act.wait_ge(raw_in[j], 16 * (t + 1))
                    nc.scalar.activation(wH[:, slot, j * 1024:(j + 1) * 1024], raw[:, j, :], ACT.Copy).then_inc(wh_done, 1)

            def strips_out(n):
                act.wait_ge(ada_strips, n - N_PRE + 1)
                nc.scalar.activation(ada_sb[:], ps[:, B_ADA, 0:P], ACT.Copy).then_inc(ada_ev, 1)

            def add_bias(n):
                act.wait_ge(ada_fin, n - N_PRE + 1)
                act.wait_ge(vec_in, 16)
                nc.scalar.activation(modT[:, bass.ds(n, 1), :].rearrange("p a c -> p (a c)"), ps[:, B_ADA, 256:258],
                                     ACT.Identity, bias=vecT[:, 1, bass.ds(n, 1)]).then_inc(mod_done, 1)

            def square(norm, s, v0, order):
                half, p_ = PAIRS[order][s // 2]
                k = 2 * p_ + s % 2
                act.wait_ge(dve_free, v0 + s + 1)
                if s >= 2:
                    act.wait_ge(sum_done, SUMS * norm + SUM_AT[order][s // 2 - 1])
                nc.scalar.activation(sqb[:, s % 2, :], xT[:, k, half * HALF:(half + 1) * HALF], ACT.Square).then_inc(sq_done, 1)

            def std(norm, half):
                act.wait_ge(stat_full, 2 * norm + half + 1)
                nc.scalar.activation(rstd[:, half, :], ps[:, 5 + half, 0:HALF], ACT.Sqrt, bias=eps[:],
                                     scale=1.0 / D).then_inc(std_done, 1)

            def hi(norm, half, ks=range(KC)):
                for k in ks:
                    act.wait_ge(t_done, 16 * norm + 8 * half + k + 1)
                    nc.scalar.activation(hH[:, k, half * HALF:(half + 1) * HALF], tb[:, k % 2, :],
                                         ACT.Copy).then_inc(hh_done, 1)

            def h_hi(norm):
                for half in range(2):
                    std(norm, half)
                    hi(norm, half)

            def last_tile(norm, v0):
                square(norm, 12, v0, "tile")
                square(norm, 13, v0, "tile")
                std(norm, 0)
                square(norm, 14, v0, "tile")
                hi(norm, 0, range(0, 4))
                square(norm, 15, v0, "tile")
                hi(norm, 0, range(4, 8))
                std(norm, 1)
                hi(norm, 1)

            act.dma_start(lg[:].rearrange("p a b -> p (a b)"),
                          ret_log_decay.rearrange("a b c -> (a b c)").partition_broadcast(P)).then_inc(act_dma, 16)
            act.wait_ge(vec_in, 16)
            act.wait_ge(set_up, 3)
            nc.scalar.activation(siluc[:, :, 0:2].rearrange("p k c -> p c k"),
                                 vecT[:, 0, R_C:R_C + 16].rearrange("p (c k) -> p c k", c=2), ACT.Silu).then_inc(siluc_ready, 1)
            act.wait_ge(act_dma, 16)
            nc.scalar.activation(lg[:], lg[:], ACT.Exp).then_inc(lg_raw, 1)
            act.wait_ge(lg_done, 1)
            act.wait_ge(const_in, 16)
            for r in range(2):
                nc.scalar.activation(kdec[:, r, :], lg[:, r, :], ACT.Exp, scale=const[:, C_KP + r:C_KP + r + 1]).then_inc(dec_done, 1)
            nc.scalar.activation(cdec[:], lg[:], ACT.Exp, scale=float(P)).then_inc(dec_done, 1)

            def pre_out(j):
                act.wait_ge(pre_strips, j + 1)
                if j >= 2:
                    act.wait_ge(pre_fin, j - 1)
                nc.scalar.activation(pre_sb[:, j % 2, :], ps[:, B_ADA, :], ACT.Copy).then_inc(pre_ev, 1)

            for j, (s0, s1) in enumerate(((0, 4), (4, 8), (8, 12), (12, 16))):
                for s in range(s0, s1):
                    square(0, s, 0, "half")
                if j == 3:
                    std(0, 0)
                    std(0, 1)
                    split(0, 0)
                pre_out(j)
            hi(0, 0)
            hi(0, 1)

            for t in range(4):
                split(t + 1, (t + 1) % 2, 16 + 4 * t if t else None)
                for n in range(4):
                    g = G_GATE + 4 * t + n
                    if t < 2:
                        act.wait_ge(acc_full, g + 1)
                        nc.scalar.activation(sgate[:, 2 * t + n % 2, (n // 2) * HALF:(n // 2 + 1) * HALF],
                                             ps[:, n, 0:HALF], ACT.Sigmoid).then_inc(act_free, 1)
                    (strips_out if n % 2 == 0 else add_bias)(16 + 2 * t + n // 2)

            def decay_tables(head, e):
                act.wait_ge(dec_done, 3)
                for r, col in enumerate((C_PF, C_PB)):
                    nc.scalar.activation(dmat[:, r, :], const[:, col:col + P], ACT.Exp,
                                         scale=lg[:, r, bass.ds(head, 1)]).then_inc(dexp_done, 1)
                for r, col in enumerate((C_QF, C_QB)):
                    nc.scalar.activation(qtab[:, r, :], const[:, col:col + P], ACT.Exp,
                                         scale=lg[:, r, bass.ds(head, 1)]).then_inc(dexp_done, 1)

            def decayed_keys(head):
                act.wait_ge(st_full, 3 * head + 3)
                act.wait_ge(prob_done, 2 * head + 2)
                act.wait_ge(dec_done, 2)
                for r in range(2):
                    sc = kdec[:, r, bass.ds(head, 1)]
                    for a_, b_ in ((0, 0), (3, 2)):
                        nc.scalar.activation(kd_nat[:, r, a_:a_ + 2, :],
                                             ps[:, 6, b_ * P:(b_ + 2) * P].rearrange("p (a b) -> p a b", a=2),
                                             ACT.Copy, scale=sc)
                    nc.scalar.activation(kd_nat[:, r, CTX_TILE, :], ps[:, 7, P:2 * P], ACT.Copy, scale=sc).then_inc(kd_done, 2)

            def ret_std(head):
                act.wait_ge(bn_done, 10 * head + 10)
                nc.scalar.activation(brs[:, :, 0], bmv[:, :, 1], ACT.Sqrt, bias=eps[:]).then_inc(bstd_done, 1)

            with act.Fori(0, 2) as i:
                at = 0
                for b in range(6):
                    e = (b - 2) // 2
                    head = 2 * i + e
                    split(T_HEADS + 6 * i + b + 1, (b + 1) % 2, G_HEADS + G_PAIR * i + at)
                    if b == 0:
                        decay_tables(2 * i, 0)
                    if b == 3:
                        decay_tables(2 * i + 1, 1)
                    for n in range(4 if b < 2 else NT):
                        act.wait_ge(acc_full, G_HEADS + G_PAIR * i + at + n + 1)
                        bank = (at + n) % 4
                        if b < 2:
                            dst, src = (qT, kT)[b][:, n % 2, (n // 2) * HALF:(n // 2 + 1) * HALF], ps[:, bank, 0:HALF]
                        else:
                            dst, src = (v_nat, gate)[b % 2][:, n, :], ps[:, bank, 0:RV]
                        nc.scalar.activation(dst, src, ACT.Silu if b in (3, 5) else ACT.Copy).then_inc(act_free, 1)
                        m = 24 + 12 * i + 2 * b + n // 2
                        if n < 4:
                            (strips_out if n % 2 == 0 else add_bias)(m)
                        if b in (2, 4) and n == 1:
                            decayed_keys(head)
                        if b == 4 and n == 0:
                            ret_std(2 * i)
                        if b == 4 and n == 2:
                            act.wait_ge(so_done, 2 * (2 * i) + 2)
                            act.dma_start(new_state[0, 0, :, bass.ds(2 * i, 1)].rearrange("r a d e -> d (r a) e"),
                                          state_out[:]).then_inc(act_dma, 16)
                        if b in (3, 5) and n == 3:
                            for q in range(3):
                                act.wait_ge(o_full, 3 * head + q + 1)
                                act.wait_ge(dve_free, V_WR)
                                w_ = 2 if q < 2 else 1
                                nc.scalar.activation(ret[:, 2 * q:2 * q + w_, bass.ds(512 * i + 256 * e, RV)],
                                                     ps[:, 5 + q, 0:w_ * RV].rearrange("p (a b) -> p a b", a=w_),
                                                     ACT.Copy).then_inc(o_out, 1)
                    at += 4 if b < 2 else NT
                ret_std(2 * i + 1)
                act.wait_ge(so_done, 2 * (2 * i + 1) + 2)
                act.dma_start(new_state[0, 0, :, bass.ds(2 * i + 1, 1)].rearrange("r a d e -> d (r a) e"),
                              state_out[:]).then_inc(act_dma, 16)

            for n in range(16):
                act.wait_ge(rt_full, n + 1)
                nc.scalar.activation(hH[:, n % 8, (n // 8) * HALF:(n // 8 + 1) * HALF], ps[:, 4 + n % 4, 0:HALF],
                                     ACT.Copy).then_inc(rth_done, 1)

            split(T_WR + 1, 1, G_WR)
            for ch in range(CC):
                act.wait_ge(cx_done, ch + 1)
                if ch >= 2:
                    act.wait_ge(csum_done, ch - 1)
                nc.scalar.activation(cmp_[:, ch % 2, 0:LAT], cacc[:, ch, 0:LAT], ACT.Square)
                nc.scalar.activation(cmp_[:, ch % 2, LAT:T], cacc[:, ch, LAT + PAD:CW], ACT.Square).then_inc(csq_done, 1)
            split(T_WR + 2, 0, G_WR + 4)
            split(T_WR + 3, 1, G_WR + 8)
            act.wait_ge(cstat_full, 2)
            nc.scalar.activation(cmp_[:, 0, 0:LAT], ps[:, 5, 0:LAT], ACT.Sqrt, bias=eps[:], scale=1.0 / CONV)
            nc.scalar.activation(cmp_[:, 0, LAT:T], ps[:, 6, 0:CTX], ACT.Sqrt, bias=eps[:], scale=1.0 / CONV).then_inc(cstd_done, 1)
            for ch in range(CC):
                act.wait_ge(cn_done, ch + 1)
                nc.scalar.activation(cacc[:, ch, :], cacc[:, ch, :], ACT.Silu, scale=vecT[:, 0, R_LG + ch:R_LG + ch + 1],
                                     bias=vecT[:, 0, R_LB + ch:R_LB + ch + 1]).then_inc(csilu_done, 1)
            for ch in range(CC):
                act.wait_ge(csilu_done, ch + 1)
                for a_, b_, n_ in CONV_MAP:
                    last = nc.scalar.activation(cH[:, ch, b_:b_ + n_], cacc[:, ch, a_:a_ + n_], ACT.Copy)
                last.then_inc(ch_done, 1)
            split(T_WC, 0, G_WR + 12)
            split(T_WC + 1, 1, G_WC)
            for s in range(8):
                square(1, s, V_WC, "wc")
            split(T_MLP0, 0, G_WC + 8)
            for s in range(8, 16):
                square(1, s, V_WC, "wc")
            act.wait_ge(act_dma, 16 * (RH + 1))
            h_hi(1)

            def mlp_group(g, layer, last):
                t0, g0, a0, v0, f0, norm = ((T_MLP0, G_MLP0, A_MLP0, V_MLP0, 0, 1),
                                            (T_MLP1, G_MLP1, A_MLP1, V_MLP1, 64, 3))[layer]

                def hidden_hi(n):
                    act.wait_ge(fs_done, f0 + 16 * g + n + 1)
                    k, half = 2 * (n // 4) + n % 2, n // 2 % 2
                    nc.scalar.activation(fH[:, k, half * HALF:(half + 1) * HALF], fs[:, n % 2, :], ACT.Copy).then_inc(fh_done, 1)

                for b in range(8):
                    if not (last and layer == 1 and b == 7):
                        split(t0 + 8 * g + b + 1, (b + 1) % 2, g0 + 32 * g + 4 * b)
                    if b < 4:
                        for n in range(4):
                            j = 4 * b + n
                            act.wait_ge(acc_full, g0 + 32 * g + j + 1)
                            if j >= 2:
                                act.wait_ge(fs_done, f0 + 16 * g + j - 1)
                            nc.scalar.activation(fr[:, j % 2, :], ps[:, n, 0:HALF], ACT.Relu).then_inc(act_free, 1)
                            if j:
                                hidden_hi(j - 1)
                            if layer == 0:
                                (strips_out if n % 2 == 0 else add_bias)(MOD1 + 12 * g + 2 * b + n // 2)
                        if b == 3:
                            hidden_hi(15)
                    else:
                        if layer == 0:
                            strips_out(MOD1 + 12 * g + 4 + b)
                            add_bias(MOD1 + 12 * g + 4 + b)
                        if last and b == 7 and layer == 0:
                            last_tile(2, v0 + 16 * g)
                        elif last:
                            for s in range(4 * (b - 4), 4 * (b - 3)):
                                square(norm + 1, s, v0 + 16 * g, "tile")

            with act.Fori(0, FG - 1) as g:
                mlp_group(g, 0, False)
            mlp_group(FG - 1, 0, True)

            def rope_std(r):
                act.wait_ge(rss_done, r + 1)
                nc.scalar.activation(rss[:], rss[:], ACT.Sqrt, bias=eps[:], scale=1.0 / P).then_inc(rstd2, 1)

            def turned_out(r):
                for h in range(2):
                    act.wait_ge(tr_full, 3 * r + h + 1)
                    dst = kTa[:, h, 2 * P:] if r == 0 else qTa[:, 2 * (r - 1) + h, 0:LAT]
                    nc.scalar.activation(dst, ps[:, 4 + h, :], ACT.Copy).then_inc(tr_out, 1)
                act.wait_ge(tr_full, 3 * r + 3)
                if r == 0:
                    nc.scalar.activation(kTa[:, :, 0:2 * P], ps[:, 6, :].rearrange("p (h n) -> p h n", h=2),
                                         ACT.Copy).then_inc(tr_out, 1)
                else:
                    nc.scalar.activation(qTa[:, 2 * (r - 1):2 * r, LAT:T], ps[:, 6, 0:2 * P].rearrange("p (h n) -> p h n", h=2),
                                         ACT.Copy).then_inc(tr_out, 1)

            for t in range(6):
                split(T_QKV + t + 1, (t + 1) % 2, G_QKV + 5 * t)
                for n in range(NT):
                    act.wait_ge(acc_full, G_QKV + 5 * t + n + 1)
                    if t == 0:
                        dst = k_nat[:, n, :]
                    elif t < 5:
                        if t > 2:
                            act.wait_ge(rn_done, t - 1)
                        dst = q_nat[:, (t - 1) % 2, n, :]
                    else:
                        dst = va[:, n, :]
                    nc.scalar.activation(dst, ps[:, NAT_BANKS[n], 0:RV], ACT.Copy).then_inc(act_free, 1)
                    if n == 1 and t:
                        rope_std(t - 1)
                    if n == 1 and t > 1:
                        turned_out(t - 2)
            turned_out(4)

            def att_exp(n):
                act.wait_ge(nmx_done, n + 1)
                if n >= 2:
                    act.wait_ge(pt_full, n - 1)
                if n >= KVH:
                    last = nc.scalar.activation(pr[:, n % 2, :].rearrange("p (a b) -> p a b", a=2),
                                                ps[:, 2 * (n % 2):2 * (n % 2) + 2, 0:HALF], ACT.Exp,
                                                bias=amx[:, n % 2, 0:1], scale=ATT_SCALE, accum_out=asum[:, n % 2, 0:1])
                else:
                    for j in range(GRP):
                        last = nc.scalar.activation(pr[:, n % 2, j * P:(j + 1) * P], ps[:, 2 * (n % 2), j * P:(j + 1) * P],
                                                    ACT.Exp, bias=amx[:, n % 2, j:j + 1], scale=ATT_SCALE,
                                                    accum_out=asum[:, n % 2, j:j + 1])
                last.then_inc(ex_done, 1)

            def att_turned(n):
                act.wait_ge(pt_full, n + 1)
                bank = ps[:, 4 if n % 2 == 0 else 7, :]
                if n == 0:
                    act.wait_ge(k_st, 16)
                m = n - KVH
                if m >= 0:
                    if m >= 4 and m % 4 == 0:
                        act.wait_ge(pv_full, m // 4 + 1)
                    nc.scalar.activation(pT[:, m // 4 % 2, 0:4, (m % 4) * P:(m % 4 + 1) * P],
                                         bank.rearrange("p (a b) -> p a b", a=4), ACT.Copy).then_inc(pt_act, 1)
                else:
                    nc.scalar.activation(pT[:, 1, n, :], bank, ACT.Copy).then_inc(pt_act, 1)

            def att_hi(v):
                act.wait_ge(pv_full, v + 1)
                if v >= KVH:
                    h = v - KVH
                    nc.scalar.activation(hH[:, h, 0:256], ps[:, 6, 0:256], ACT.Copy)
                    nc.scalar.activation(hH[:, h, 384:640], ps[:, 6, 256:512], ACT.Copy).then_inc(ah_done, 1)
                else:
                    nc.scalar.activation(hH[:, GRP * v:GRP * (v + 1), 256:384],
                                         ps[:, 6, :].rearrange("p (a b) -> p a b", a=GRP), ACT.Copy).then_inc(ah_done, 1)

            att_exp(0)
            att_exp(1)
            for n in range(N_ATT):
                att_turned(n)
                if n + 2 < N_ATT:
                    att_exp(n + 2)
                if n - 1 in VALUES_AT:
                    att_hi(VALUES_AT[n - 1])
            att_hi(KVH + QH - 1)

            for t in range(4):
                split(T_WO + t + 1, (t + 1) % 2, G_WO + 4 * t)
                if t < 3:
                    for s in range(4 * t, 4 * t + 4):
                        square(3, s, V_WO, "tile")
            last_tile(3, V_WO)
            with act.Fori(0, FG - 1) as g:
                mlp_group(g, 1, False)
            mlp_group(FG - 1, 1, True)
            std(4, 0)
            std(4, 1)
            for tile in range(NT):
                act.wait_ge(y_full, 2 * tile + 1)
                nc.scalar.activation(y_nat[:, tile, 0:512], ps[:, (2 * tile) % 4, :], ACT.Copy).then_inc(y_act, 1)

        @block.gpsimd
        def _(pool):
            def lo(t, slot):
                for j in range(2):
                    pool.wait_ge(wh_done, 2 * t + j + 1)
                    cs = slice(j * 1024, (j + 1) * 1024)
                    nc.gpsimd.tensor_tensor(wL[:, slot, cs], raw[:, j, :], wH[:, slot, cs].bitcast(F32),
                                            ALU.subtract).then_inc(wl_done, 1)

            def h_lo(norm):
                for half in range(2):
                    for k in range(KC):
                        pool.wait_ge(hh_done, 16 * norm + 8 * half + k + 1)
                        cs = slice(half * HALF, (half + 1) * HALF)
                        nc.gpsimd.tensor_tensor(hL[:, k, cs], tb[:, k % 2, :], hH[:, k, cs].bitcast(F32),
                                                ALU.subtract).then_inc(h_ready, 1)

            lo(0, 0)
            h_lo(0)
            for t in range(4):
                lo(t + 1, (t + 1) % 2)
            with pool.Fori(0, 2) as i:
                for b in range(6):
                    lo(T_HEADS + 6 * i + b + 1, (b + 1) % 2)
            for t in range(T_WR + 1, T_MLP0 + 1):
                lo(t, t % 2)
            for norm, first, n_tiles in ((1, T_MLP0, 8 * FG), (2, T_QKV, 6 + 4), (3, T_MLP1, 8 * FG - 1)):
                h_lo(norm)
                with pool.Fori(0, n_tiles // 2) as i:
                    for j in range(2):
                        lo(first + 2 * i + j + 1, (j + 1) % 2)
            lo(N_TILES - 1, 1)

        @block.vector
        def _(dve):
            def halfcols(half):
                return slice(half * HALF, (half + 1) * HALF)

            def residual(g, v0, n, half, k, gate_at):
                dve.wait_ge(acc_full, g + n + 1)
                for c0, w_, which in SEGS[half]:
                    x = xT[:, k, c0:c0 + w_]
                    last = nc.vector.scalar_tensor_tensor(out=x, in0=ps[:, n % 4, c0 - half * HALF:c0 - half * HALF + w_],
                                                          scalar=modT[:, gate_at + k, which:which + 1], in1=x,
                                                          op0=ALU.mult, op1=ALU.add)
                last.then_inc(dve_free, 1)

            def add_squares(norm, q, order):
                half, p_ = PAIRS[order][q]
                base = SUMS * norm
                dve.wait_ge(sq_done, 16 * norm + 2 * q + 2)
                out = ssum[:, half, :]
                if p_ == 0:
                    nc.vector.tensor_tensor(out, sqb[:, 0, :], sqb[:, 1, :], ALU.add).then_inc(sum_done, 1)
                else:
                    before = base + SUM_AT[order][q] - 2
                    dve.wait_ge(sum_done, before)
                    nc.vector.tensor_tensor(out, out, sqb[:, 0, :], ALU.add).then_inc(sum_done, 1)
                    dve.wait_ge(sum_done, before + 1)
                    nc.vector.tensor_tensor(out, out, sqb[:, 1, :], ALU.add).then_inc(sum_done, 1)

            def reciprocal_std(norm, half):
                dve.wait_ge(std_done, 2 * norm + half + 1)
                nc.vector.reciprocal(rstd[:, half, :], rstd[:, half, :]).then_inc(rstd_done, 1)
                dve.wait_ge(rstd_done, 2 * norm + half + 1)

            def h_values(norm, half, ks):
                shift_at = (SH1, SH2, MOD1 + SH1, MOD1 + SH2)[norm]
                i0 = 16 * norm + 8 * half

                def normed(k):
                    if i0 + k >= 2:
                        dve.wait_ge(t_done, i0 + k - 1)
                    nc.vector.tensor_tensor(ub[:, k % 2, :], xT[:, k, halfcols(half)], rstd[:, half, :],
                                            ALU.mult).then_inc(u_done, 1)
                normed(ks[0])
                for k in ks:
                    if k != ks[-1]:
                        normed(k + 1)
                    dve.wait_ge(u_done, i0 + k + 1)
                    if i0 + k >= 2:
                        dve.wait_ge(h_ready, i0 + k - 1)
                    for c0, w_, which in SEGS[half]:
                        a_ = c0 - half * HALF
                        last = nc.vector.tensor_scalar(tb[:, k % 2, a_:a_ + w_], ub[:, k % 2, a_:a_ + w_],
                                                       coef[:, norm, k, which:which + 1],
                                                       modT[:, shift_at + k, which:which + 1], ALU.mult, ALU.add)
                    last.then_inc(t_done, 1)

            def coefficients(norm):
                scale_at = (SC1, SC2, MOD1 + SC1, MOD1 + SC2)[norm]
                dve.wait_ge(mod_done, scale_at + KC - N_PRE) if norm else dve.wait_ge(pre_mod, 4)
                g = vecT[:, 0, R_NORM + KC * norm:R_NORM + KC * (norm + 1)]
                nc.vector.scalar_tensor_tensor(out=coef[:, norm], in0=modT[:, scale_at:scale_at + KC, :], scalar=1.0,
                                               in1=g[:, :, None].to_broadcast([P, KC, 2]), op0=ALU.add,
                                               op1=ALU.mult).then_inc(coef_done, 1)
                dve.wait_ge(coef_done, norm + 1)

            nc.vector.memset(ones[:], 1.0).then_inc(set_up, 1)
            nc.vector.memset(eps[:], EPS).then_inc(set_up, 1)
            nc.vector.memset(siluc[:], 0.0).then_inc(set_up, 1)
            dve.wait_ge(lg_raw, 1)
            nc.vector.tensor_scalar(lg[:], lg[:], -1.0, None, ALU.mult).then_inc(lg_done, 1)

            def pre_bias(j):
                dve.wait_ge(pre_fin, j + 1)
                nc.vector.tensor_tensor(modT[:, 4 * j:4 * (j + 1), :],
                                        ps[:, 6 + j % 2, 0:8].rearrange("p (a b) -> p a b", a=4),
                                        vecT[:, 1, 4 * j:4 * (j + 1), None].to_broadcast([P, 4, 2]), ALU.add).then_inc(pre_mod, 1)

            dve.wait_ge(vec_in, 16)
            for n in range(16):
                dve.wait_ge(acc_full, n + 1)
                nc.vector.tensor_copy(xT[:, n % 8, halfcols(n // 8)], ps[:, n % 4, 0:HALF]).then_inc(dve_free, 1)
                if n % 2 == 1 and n > 1:
                    add_squares(0, n // 2 - 1, "half")
                if n in (9, 13):
                    pre_bias(n // 4 - 2)
            add_squares(0, 7, "half")
            pre_bias(2)
            reciprocal_std(0, 0)
            reciprocal_std(0, 1)
            pre_bias(3)
            for a_, b_ in ((0, PAD), (PAD + LAT, 2 * PAD + LAT), (ZW - PAD, ZW)):
                last = nc.vector.memset(zp[:, :, a_:b_], 0.0)
            last.then_inc(set_up, 1)
            coefficients(0)
            for half in range(2):
                h_values(0, half, range(KC))

            dve.wait_ge(act_free, 8)
            for t in range(2):
                for n in range(4):
                    half, ch = n // 2, 2 * t + n % 2
                    dve.wait_ge(acc_full, G_VAL + 4 * t + n + 1)
                    for c0, w_, which in SEGS[half]:
                        a_ = c0 - half * HALF
                        z0 = (2 * PAD + LAT + c0 - 256) if which else (PAD + c0 - (P if half else 0))
                        last = nc.vector.tensor_tensor(zp[:, ch, z0:z0 + w_], ps[:, n, a_:a_ + w_],
                                                       sgate[:, ch, c0:c0 + w_], ALU.mult)
                    last.then_inc(dve_free, 1)

            dve.wait_ge(set_up, 4)
            dve.wait_ge(dve_free, V_WR)
            with dve.Fori(0, 2) as i:
                def taps(w0, w1):
                    for w in range(w0, w1):
                        for ch in range(2):
                            src = zp[:, bass.ds(2 * i + ch, 1), w:w + CW].rearrange("p a n -> p (a n)")
                            acc = cacc[:, bass.ds(2 * i + ch, 1), :].rearrange("p a n -> p (a n)")
                            wt = vecT[:, 2, bass.ds(2 * i + 4 * w + ch, 1)]
                            if w == 0:
                                nc.vector.tensor_scalar(acc, src, wt, vecT[:, 0, bass.ds(R_CB + 2 * i + ch, 1)],
                                                        ALU.mult, ALU.add).then_inc(conv_done, 1)
                            else:
                                dve.wait_ge(conv_done, 2 * WIDTH * i + 2 * w + ch - 1)
                                nc.vector.scalar_tensor_tensor(out=acc, in0=src, scalar=wt, in1=acc, op0=ALU.mult,
                                                               op1=ALU.add).then_inc(conv_done, 1)

                for e in range(2):
                    head = 2 * i + e
                    cuts = ((0, 13, 19, 20, 21, 22), (22, 22, 28, 30, 31, 31))[e]
                    taps(*cuts[0:2])
                    dve.wait_ge(dexp_done, 4 * head + 4)
                    nc.vector.tensor_tensor(dmat[:, 0, :], dmat[:, 0, :], dmat[:, 1, :], ALU.mult).then_inc(dm_done, 1)
                    dve.wait_ge(act_free, A_HEADS + G_PAIR * i + 4)
                    for r in range(2):
                        for c0 in (0, 384):
                            nc.vector.scalar_tensor_tensor(
                                out=qdec[:, r, c0:c0 + 256].rearrange("p (a b) -> p a b", a=2),
                                in0=qT[:, e, c0:c0 + 256].rearrange("p (a b) -> p a b", a=2), scalar=RET_SCALE,
                                in1=qtab[:, r, None, :].to_broadcast([P, 2, P]), op0=ALU.mult,
                                op1=ALU.mult).then_inc(qdec_done, 1)
                    dve.wait_ge(dm_done, 2 * head + 1)
                    nc.vector.tensor_tensor(dmat[:, 0, :], dmat[:, 0, :], ident, ALU.add).then_inc(dm_done, 1)
                    dve.wait_ge(dm_done, 2 * head + 2)
                    dve.wait_ge(st_full, 3 * head + 2)
                    for a_, b_ in ((0, 0), (3, 2)):
                        last = nc.vector.scalar_tensor_tensor(
                            out=prob[:, a_ * P:(a_ + 2) * P].rearrange("p (a b) -> p a b", a=2),
                            in0=ps[:, 5, b_ * P:(b_ + 2) * P].rearrange("p (a b) -> p a b", a=2), scalar=RET_SCALE,
                            in1=dmat[:, 0, None, :].to_broadcast([P, 2, P]), op0=ALU.mult, op1=ALU.mult)
                    last.then_inc(prob_done, 1)
                    nc.vector.scalar_tensor_tensor(out=prob[:, 2 * P:3 * P], in0=ps[:, 7, 0:P], scalar=RET_SCALE,
                                                   in1=dmat[:, 0, :], op0=ALU.mult, op1=ALU.mult).then_inc(prob_done, 1)
                    taps(*cuts[1:3])
                    dve.wait_ge(s0_in, 32 * (head + 1))
                    dve.wait_ge(dec_done, 3)

                    def advance(r, n, to, bank, at, count):
                        if count:
                            dve.wait_ge(s_done, 6 * head + count)
                        nc.vector.scalar_tensor_tensor(out=S[:, r, to, :], in0=S[:, r, n, :],
                                                       scalar=cdec[:, r, bass.ds(head, 1)], in1=ps[:, bank, at:at + RV],
                                                       op0=ALU.mult, op1=ALU.add).then_inc(s_done, 1)

                    dve.wait_ge(u_full, 4 * head + 1)
                    advance(0, 0, 1, 5, 0, 0)
                    advance(0, 1, 2, 5, RV, 1)
                    dve.wait_ge(u_full, 4 * head + 2)
                    advance(0, 2, 3, 6, 0, 2)
                    dve.wait_ge(act_dma, 16 * (head + 1))
                    nc.vector.tensor_copy(state_out[:, 0, :], ps[:, 6, RV:2 * RV]).then_inc(so_done, 1)
                    dve.wait_ge(u_full, 4 * head + 3)
                    advance(1, 3, 2, 7, 0, 3)
                    advance(1, 2, 1, 7, RV, 4)
                    dve.wait_ge(u_full, 4 * head + 4)
                    advance(1, 1, 0, 5, 0, 5)
                    nc.vector.tensor_copy(state_out[:, 1, :], ps[:, 5, RV:2 * RV]).then_inc(so_done, 1)
                    taps(*cuts[2:4])
                    hc = bass.ds(512 * i + 256 * e, RV)
                    for n in range(NT):
                        dve.wait_ge(o_out, 3 * head + n // 2 + 1)
                        nc.vector.bn_stats(bst[:, n, :], ret[:, n, hc]).then_inc(bn_done, 1)
                    dve.wait_ge(bn_done, 10 * head + 5)
                    taps(*cuts[3:5])
                    for n in range(NT):
                        nc.vector.bn_aggr(bmv[:, n, :], bst[:, n, :]).then_inc(bn_done, 1)
                    taps(*cuts[4:6])
                    dve.wait_ge(bstd_done, head + 1)
                    nc.vector.reciprocal(brs[:, :, 0], brs[:, :, 0]).then_inc(brs_done, 1)
                    dve.wait_ge(brs_done, head + 1)
                    for n in range(NT):
                        nc.vector.tensor_scalar(ret[:, n, hc], ret[:, n, hc], bmv[:, n, 0:1], brs[:, n, 0:1],
                                                ALU.subtract, ALU.mult).then_inc(on_done, 1)
                    dve.wait_ge(act_free, A_HEADS + G_PAIR * i + 18 + 10 * e)
                    for n in range(NT):
                        dve.wait_ge(on_done, NT * head + n + 1)
                        last = nc.vector.tensor_tensor(ret[:, n, hc], ret[:, n, hc], gate[:, n, :], ALU.mult)
                    last.then_inc(ret_done, 1)

            def compact(ch):
                return ((cacc[:, ch, 0:LAT], slice(0, LAT)), (cacc[:, ch, LAT + PAD:CW], slice(LAT, T)))

            for n in range(16):
                dve.wait_ge(rth_done, n + 1)
                cs = halfcols(n // 8)
                nc.vector.tensor_tensor(hL[:, n % 8, cs], ps[:, 4 + n % 4, 0:HALF], hH[:, n % 8, cs].bitcast(F32),
                                        ALU.subtract).then_inc(rtl_done, 1)

            dve.wait_ge(conv_done, 4 * WIDTH)
            for src, cs in compact(0):
                other = dict((c.start, s) for s, c in compact(1))[cs.start]
                last = nc.vector.tensor_tensor(cst[:, 0, cs], src, other, ALU.add)
            last.then_inc(cn_sum, 1)
            for ch in (2, 3):
                dve.wait_ge(cn_sum, ch - 1)
                for src, cs in compact(ch):
                    last = nc.vector.tensor_tensor(cst[:, 0, cs], cst[:, 0, cs], src, ALU.add)
                last.then_inc(cn_sum, 1)
            dve.wait_ge(cn_sum, 3)
            nc.vector.tensor_scalar(cst[:, 0, :], cst[:, 0, :], 1.0 / CONV, None, ALU.mult).then_inc(cstat_in, 1)

            def wr(n):
                t, m = n // 4, n % 4
                residual(G_WR, V_WR, n, m // 2, 2 * t + m % 2, G1)

            dve.wait_ge(mod_done, MOD1 - N_PRE)
            wr(0)
            wr(1)
            dve.wait_ge(cstat_full, 1)
            for ch in range(CC):
                for (src, cs), bank in zip(compact(ch), (5, 6)):
                    last = nc.vector.tensor_tensor(src, src, ps[:, bank, 0:cs.stop - cs.start], ALU.subtract)
                last.then_inc(cx_done, 1)
            for n in range(2, 5):
                wr(n)
            dve.wait_ge(csq_done, 2)
            nc.vector.tensor_tensor(cst[:, 1, :], cmp_[:, 0, :], cmp_[:, 1, :], ALU.add).then_inc(csum_done, 2)
            for ch in (2, 3):
                dve.wait_ge(csq_done, ch + 1)
                dve.wait_ge(csum_done, ch)
                nc.vector.tensor_tensor(cst[:, 1, :], cst[:, 1, :], cmp_[:, ch % 2, :], ALU.add).then_inc(
                    csum_done if ch == 2 else cstat_in, 1)
            for n in range(5, 10):
                wr(n)
            dve.wait_ge(cstd_done, 1)
            nc.vector.reciprocal(cmp_[:, 0, :], cmp_[:, 0, :]).then_inc(crec_done, 1)
            dve.wait_ge(crec_done, 1)
            for ch in range(CC):
                dve.wait_ge(cx_done, ch + 1)
                for src, cs in compact(ch):
                    last = nc.vector.tensor_tensor(src, src, cmp_[:, 0, cs], ALU.mult)
                last.then_inc(cn_done, 1)
            for n in range(10, 16):
                wr(n)
            for ch in range(CC):
                dve.wait_ge(ch_done, ch + 1)
                for a_, b_, n_ in CONV_MAP:
                    last = nc.vector.tensor_tensor(cL[:, ch, b_:b_ + n_], cacc[:, ch, a_:a_ + n_],
                                                   cH[:, ch, b_:b_ + n_].bitcast(F32), ALU.subtract)
                last.then_inc(cl_done, 2)
            coefficients(1)

            def last_tile(norm, order, update, first):
                update(first)
                update(first + 1)
                add_squares(norm, first // 2, order)
                update(first + 2)
                reciprocal_std(norm, 0)
                h_values(norm, 0, range(0, 4))
                update(first + 3)
                add_squares(norm, first // 2 + 1, order)
                h_values(norm, 0, range(4, 8))
                reciprocal_std(norm, 1)
                h_values(norm, 1, range(KC))

            def wc(n):
                t, m = n // 8, n % 8
                residual(G_WC, V_WC, n, m // 4, 4 * t + m % 4, G1)

            for n in range(13):
                wc(n)
                if n % 2 == 1:
                    add_squares(1, n // 2, "wc")
            wc(13)
            add_squares(1, 6, "wc")
            wc(14)
            wc(15)
            add_squares(1, 7, "wc")
            for half in range(2):
                reciprocal_std(1, half)
                h_values(1, half, range(KC))

            def mlp_group(g, layer, last):
                g0, a0, v0, f0, norm, gate_at = ((G_MLP0, A_MLP0, V_MLP0, 0, 1, G2),
                                                 (G_MLP1, A_MLP1, V_MLP1, 64, 3, MOD1 + G2))[layer]

                def hidden_lo(n):
                    dve.wait_ge(fh_done, f0 + 16 * g + n + 1)
                    k, half = 2 * (n // 4) + n % 2, n // 2 % 2
                    nc.vector.tensor_tensor(fL[:, k, halfcols(half)], fs[:, n % 2, :], fH[:, k, halfcols(half)].bitcast(F32),
                                            ALU.subtract).then_inc(f_ready, 1)

                for n in range(16):
                    dve.wait_ge(act_free, a0 + 16 * g + n + 1)
                    if n >= 2:
                        dve.wait_ge(f_ready, f0 + 16 * g + n - 1)
                    nc.vector.tensor_tensor(fs[:, n % 2, :], fr[:, n % 2, :], fr[:, n % 2, :], ALU.mult).then_inc(fs_done, 1)
                    if n:
                        hidden_lo(n - 1)
                hidden_lo(15)

                def update(n):
                    b, m = n // 4, n % 4
                    residual(g0 + 32 * g + 16, v0, n, m // 2, 2 * b + m % 2, gate_at)

                for n in range(12 if last else 16):
                    update(n)
                    if last and n % 2 == 1:
                        add_squares(norm + 1, n // 2, "tile")
                return update

            with dve.Fori(0, FG - 1) as g:
                mlp_group(g, 0, False)
            update = mlp_group(FG - 1, 0, True)
            dve.wait_ge(mod_done, N_MOD - N_PRE)
            coefficients(2)
            last_tile(2, "tile", update, 12)
            coefficients(3)

            dve.wait_ge(att_in, 16 * 3)
            for qk in range(2):
                for j, (cs_, par) in enumerate(((0, 0), (1, 1), (1, 0), (0, 1))):
                    last = nc.vector.tensor_tensor(tabs[:, qk, j], rope_sb[:, cs_],
                                                   gqk[:, qk, None, par::2].to_broadcast([P, NT, 64]), ALU.mult)
            last.then_inc(tab_done, 1)
            dve.wait_ge(tab_done, 1)

            def rope(r):
                src = k_nat[:] if r == 0 else q_nat[:, (r - 1) % 2]
                out = kro if r == 0 else qro
                tab = tabs[:, 1 if r == 0 else 0]
                dve.wait_ge(act_free, A_QKV + 5 * r + 5)
                nc.vector.tensor_tensor(rn[:], src, src, ALU.mult).then_inc(rsq_done, 1)
                dve.wait_ge(rsq_done, r + 1)
                nc.vector.tensor_reduce(rss[:], rn[:].rearrange("p n (h d) -> p (n h) d", h=2), AX_X,
                                        ALU.add).then_inc(rss_done, 1)
                dve.wait_ge(rstd2, r + 1)
                nc.vector.reciprocal(rss[:], rss[:]).then_inc(rrec, 1)
                dve.wait_ge(rrec, r + 1)
                nc.vector.tensor_tensor(rn[:].rearrange("p n (h d) -> p (n h) d", h=2),
                                        src.rearrange("p n (h d) -> p (n h) d", h=2),
                                        rss[:, :, None].to_broadcast([P, 2 * NT, P]), ALU.mult).then_inc(rn_done, 1)
                dve.wait_ge(rn_done, r + 1)
                if r > 1:
                    dve.wait_ge(tr_full, 3 * r)
                x = [rn[:].rearrange("p n (h d) -> p n h d", h=2)[..., par::2] for par in range(2)]
                y = [out[:].rearrange("p n (h d) -> p n h d", h=2)[..., par::2] for par in range(2)]
                for j, (dst, a_) in enumerate(((y[0], 0), (rtmp[:, 0], 1), (y[1], 0), (rtmp[:, 1], 1))):
                    nc.vector.tensor_tensor(dst, x[a_], tab[:, j, :, None, :].to_broadcast([P, NT, 2, 64]),
                                            ALU.mult).then_inc(rm_done, 1)
                for j in range(2):
                    dve.wait_ge(rm_done, 4 * r + 2 * j + 2)
                    nc.vector.tensor_tensor(y[j], y[j], rtmp[:, j], ALU.add if j else ALU.subtract).then_inc(ro_done, 1)

            for r in range(5):
                rope(r)

            def att_max(n):
                dve.wait_ge(sc_full, n + 1)
                if n >= 2:
                    dve.wait_ge(ex_done, n - 1)
                if n >= KVH:
                    m = amx[:, n % 2, 0:1]
                    nc.vector.tensor_reduce(m, ps[:, 2 * (n % 2):2 * (n % 2) + 2, 0:HALF], mybir.AxisListType.XY,
                                            ALU.max).then_inc(mx_done, 1)
                else:
                    m = amx[:, n % 2, :]
                    nc.vector.tensor_reduce(m, ps[:, 2 * (n % 2), :].rearrange("p (a b) -> p a b", a=GRP), AX_X,
                                            ALU.max).then_inc(mx_done, 1)
                dve.wait_ge(mx_done, n + 1)
                nc.vector.tensor_scalar(m, m, -ATT_SCALE, None, ALU.mult).then_inc(nmx_done, 1)

            def att_normalise(n):
                dve.wait_ge(ex_done, n + 1)
                w_ = 1 if n >= KVH else GRP
                s = asum[:, n % 2, 0:w_]
                nc.vector.reciprocal(s, s).then_inc(rc_done, 1)
                dve.wait_ge(rc_done, n + 1)
                if w_ == 1:
                    nc.vector.tensor_scalar(pr[:, n % 2, :], pr[:, n % 2, :], s, None, ALU.mult).then_inc(pn_done, 1)
                else:
                    p_ = pr[:, n % 2, 0:512].rearrange("p (a b) -> p a b", a=GRP)
                    nc.vector.tensor_tensor(p_, p_, s[:, :, None].to_broadcast([P, GRP, P]), ALU.mult).then_inc(pn_done, 1)

            def att_lo(v):
                dve.wait_ge(ah_done, v + 1)
                if v >= KVH:
                    h = v - KVH
                    for a_, b_ in ((0, 0), (384, 256)):
                        last = nc.vector.tensor_tensor(hL[:, h, a_:a_ + 256], ps[:, 6, b_:b_ + 256],
                                                       hH[:, h, a_:a_ + 256].bitcast(F32), ALU.subtract)
                else:
                    hs = slice(GRP * v, GRP * (v + 1))
                    last = nc.vector.tensor_tensor(hL[:, hs, 256:384], ps[:, 6, :].rearrange("p (a b) -> p a b", a=GRP),
                                                   hH[:, hs, 256:384].bitcast(F32), ALU.subtract)
                last.then_inc(attn_ready, 1)

            def att_last_out(m):
                dve.wait_ge(pt_full, KVH + m + 1)
                if m >= 4 and m % 4 == 0:
                    dve.wait_ge(pv_full, m // 4 + 1)
                nc.vector.tensor_copy(pT[:, m // 4 % 2, 4, (m % 4) * P:(m % 4 + 1) * P], ps[:, 5, 0:P]).then_inc(pt_dve, 1)

            att_max(0)
            att_max(1)
            for n in range(N_ATT):
                att_normalise(n)
                if n > KVH:
                    att_last_out(n - KVH - 1)
                if n + 2 < N_ATT:
                    att_max(n + 2)
                if n - 2 in VALUES_AT:
                    att_lo(VALUES_AT[n - 2])
            att_last_out(4 * QH - 1)
            att_lo(KVH + QH - 1)

            def wo(n):
                t, m = n // 4, n % 4
                residual(G_WO, V_WO, n, m // 2, 2 * t + m % 2, MOD1 + G1)

            for n in range(12):
                wo(n)
                if n % 2 == 1:
                    add_squares(3, n // 2, "tile")
            last_tile(3, "tile", wo, 12)

            with dve.Fori(0, FG - 1) as g:
                mlp_group(g, 1, False)
            update = mlp_group(FG - 1, 1, True)
            for n in range(12, 16):
                update(n)
                if n % 2 == 1:
                    add_squares(4, n // 2, "tile")
            for half in range(2):
                reciprocal_std(4, half)
                for k in range(KC):
                    x = xT[:, k, halfcols(half)]
                    nc.vector.scalar_tensor_tensor(out=x, in0=x, scalar=vecT[:, 0, R_FINAL + k:R_FINAL + k + 1],
                                                   in1=rstd[:, half, :], op0=ALU.mult, op1=ALU.mult).then_inc(y_done, 1)
            for tile in range(NT):
                dve.wait_ge(y_full, 2 * tile + 2)
                nc.vector.tensor_copy(y_nat[:, tile, 512:1024], ps[:, (2 * tile + 1) % 4, :]).then_inc(y_dve, 1)


_INS = ["x_prompt", "x_sample", "state_ret", "cache_k", "cache_v", "ada_w", "even_w_in", "even_w_out",
        "ret_log_decay", "odd_w_qkv", "odd_q_g", "odd_k_g", "odd_w_o", "mlp_w1", "mlp_w2"]
_OUTS = [("y_prompt", (1, CTX, D)), ("y_sample", (1, LAT, D)), ("new_state", (1, 1, 2, RH, P, RV)),
         ("new_k", (1, 1, CTX, KVH, P)), ("new_v", (1, 1, CTX, KVH, P))]


def kernel(**inputs):
    import concourse.bacc as bacc
    from concourse.bass_utils import run_bass_kernel_spmd

    nc = bacc.Bacc("TRN2", target_bir_lowering=False, num_devices=1)
    shape_const, rope_const = shape_constants()
    arrays, args = {}, []
    given = [(name, inputs[name]) for name in _INS] + [("feature_vectors", by_feature_chunk(inputs)),
                                                       ("shape_const", shape_const), ("rope_const", rope_const)]
    for name, a in given:
        a = np.ascontiguousarray(a)
        arrays[f"in_{name}"] = a
        args.append(nc.dram_tensor(f"in_{name}", a.shape, mybir.dt.from_np(a.dtype), kind="ExternalInput").ap())
    for name, shape in _OUTS:
        args.append(nc.dram_tensor(f"out_{name}", shape, F32, kind="ExternalOutput").ap())
    hybrid_step(nc, *args)
    r = run_bass_kernel_spmd(nc, [arrays], core_ids=[0])
    return tuple(r.results[0][f"out_{name}"] for name, _ in _OUTS)
```

```python
from contextlib import ExitStack

import numpy as np

import concourse.bass as bass
from concourse import mybir

F32, F32R = mybir.dt.float32, mybir.dt.float32r
ALU, ACT = mybir.AluOpType, mybir.ActivationFunctionType
AX_X = mybir.AxisListType.X

P = 128
D = 1024
KC = D // P
LAT, CTX = 512, 128
T = LAT + CTX
HALF = T // 2
NT = T // P
CTX_TILE = 2
LAT_TILES = (0, 1, 3, 4)
EPS = 1e-6
CONV, WIDTH = 512, 31
CC = CONV // P
PAD = WIDTH // 2
ZW = PAD + LAT + PAD + CTX + PAD
CW = LAT + PAD + CTX
RH, RV = 4, 256
QH, KVH = 8, 2
GRP = QH // KVH
FF = 4 * D
FG = FF // D
GRID_W = 64
ATT_SCALE = float(P) ** -0.5
RET_SCALE = float(P) ** -0.5
KEYS = P + LAT

PAIRS = {"half": [(h, p) for h in range(2) for p in range(4)],
         "tile": [(h, p) for p in range(4) for h in range(2)],
         "wc": [(h, 2 * t + p) for t in range(2) for h in range(2) for p in range(2)]}
SUM_AT = {k: [sum(1 if p == 0 else 2 for _, p in v[:n + 1]) for n in range(8)] for k, v in PAIRS.items()}
SUMS = 14
CONV_MAP = ((0, 0, 256), (LAT + PAD, 256, CTX), (256, 384, 256))

SEGS = (((0, 256, 0), (256, 64, 1)), ((320, 64, 1), (384, 256, 0)))

T_GATE, T_VAL, T_HEADS = 0, 2, 4
T_WR = T_HEADS + 12
T_WC = T_WR + 4
T_MLP0 = T_WC + 2
T_QKV = T_MLP0 + 8 * FG
T_WO = T_QKV + 6
T_MLP1 = T_WO + 4
N_TILES = T_MLP1 + 8 * FG

G_X = 0
G_GATE = 16
G_VAL = G_GATE + 8
G_HEADS = G_VAL + 8
G_PAIR = 28
G_WR = G_HEADS + 2 * G_PAIR
G_WC = G_WR + 16
G_MLP0 = G_WC + 16
G_QKV = G_MLP0 + 32 * FG
G_WO = G_QKV + 30
G_MLP1 = G_WO + 16
A_HEADS, A_MLP0 = 8, 8 + 2 * G_PAIR
A_QKV = A_MLP0 + 16 * FG
A_MLP1 = A_QKV + 30
V_VAL, V_WR, V_WC, V_MLP0 = 16, 24, 40, 56
V_WO = V_MLP0 + 16 * FG
V_MLP1 = V_WO + 16
N_ATT = KVH + 4 * QH
VALUES_AT = {2: 0, 4: 1, **{KVH + 4 * h + 4: KVH + h for h in range(QH - 1)}}
NAT_BANKS = (0, 1, 2, 3, 7)

PRE_ORDER = (2, 3, 0, 1)
N_PRE = 16
Y_BANKS = ((4, 5), (6, 7), (4, 5), (6, 7), (2, 3))
Y_TILES = ((0, 1), (2, 3, 4))
N_MOD = 96
SH1, SC1, G1, SH2, SC2, G2 = (8 * s for s in range(6))
MOD1 = 48
M_HEADS, M_MLP = 4, (MOD1 - N_PRE) // 2
MLP_PAIR = {0: 0, 1: 1, 2: 2, 3: 3, 4: 4, 6: 5}
ADA_STEP = {0: 0, 2: 1}
SHIFT_AT = (SH1, SH2, MOD1 + SH1, MOD1 + SH2)
SCALE_AT = (SC1, SC2, MOD1 + SC1, MOD1 + SC2)

R_C, R_NORM, R_CB, R_LG, R_LB = 0, 16, 48, 52, 56

C_ID, C_PF, C_PB, C_QF, C_QB, C_KP, C_SEL = 0, 128, 256, 384, 512, 640, 642
C_END = 644


def shape_constants():
    c = np.zeros((P, C_END), np.float32)
    i, j = np.arange(P)[None, :], np.arange(P)[:, None]
    c[:, C_ID:C_ID + P] = np.eye(P)
    c[:, C_PF:C_PF + P] = np.maximum(i - j, 0)
    c[:, C_PB:C_PB + P] = np.maximum(j - i, 0)
    c[:, C_QF:C_QF + P] = i + 1
    c[:, C_QB:C_QB + P] = P - i
    c[:, C_KP] = P - 1 - np.arange(P)
    c[:, C_KP + 1] = np.arange(P)
    for s in range(4):
        c[32 * s, C_SEL] = c[32 * s + 1, C_SEL + 1] = 1
    half = P // 2
    pos = np.arange(LAT)
    inv = (np.float32(10000.0) ** (-np.arange(0, half, 2, dtype=np.float32) / half)).astype(np.float32)
    ang = np.concatenate([(pos // GRID_W).astype(np.float32)[:, None] * inv,
                          (pos % GRID_W).astype(np.float32)[:, None] * inv], axis=1)
    rope = np.zeros((P, 2, NT, half), np.float32)
    rope[:, 0, CTX_TILE] = 1.0
    for n, tile in enumerate(LAT_TILES):
        rope[:, 0, tile] = np.cos(ang[n * P:(n + 1) * P].astype(np.float64))
        rope[:, 1, tile] = np.sin(ang[n * P:(n + 1) * P].astype(np.float64))
    return c, rope


def by_feature_chunk(inputs):
    out = np.zeros((P, 3, P), np.float32)
    for b, at, names in ((0, R_C, ("c", "c_ctx", "norm_g", "conv_dw_b", "conv_ln_g", "conv_ln_b")),
                         (1, 0, ("ada_b",)), (2, 0, ("conv_dw_w",))):
        for name in names:
            a = np.asarray(inputs[name]).reshape(-1, P)
            out[:, b, at:at + len(a)] = a.T
            at += len(a)
    return out


def hybrid_step(nc, x_prompt, x_sample, state_ret, cache_k, cache_v, ada_w, even_w_in, even_w_out, final_g,
                ret_log_decay, odd_w_qkv, odd_q_g, odd_k_g, odd_w_o, mlp_w1, mlp_w2, feature_vectors,
                shape_const, rope_const, y_prompt, y_sample, new_state, new_k, new_v):
    ctx = ExitStack()
    with ctx:
        here = [(nc.sbuf_base + 31) // 32 * 32]

        def place(name, shape, dt=F32):
            at = here[0]
            here[0] += (int(np.prod(shape[1:])) * 4 + 31) // 32 * 32
            return nc.alloc_sbuf_tensor_at(name, shape, dt, offset=at)

        xT = place("xT", [P, KC, T])
        h_at = here[0]
        hH = place("hH", [P, KC, T], F32R)
        hL = place("hL", [P, KC, T], F32R)
        raw = place("raw", [P, 2, 1024])
        wH = place("wH", [P, 2, 2048], F32R)
        wL = place("wL", [P, 2, 2048], F32R)
        ada = place("ada", [P, KC, 256])
        const = place("const", [P, C_END])
        ones = place("ones", [P, P])
        eps = place("eps", [P, 1])
        vecT = place("vecT", [P, 3, P])
        siluc = place("siluc", [P, KC, 32])
        ada_sb = place("ada_sb", [P, 256])
        modT = place("modT", [P, N_MOD, 2])
        coef = place("coef", [P, 4, KC, 2])
        norm_buffers = here[0]
        ssum = place("ssum", [P, 2, HALF])
        rstd = place("rstd", [P, 2, HALF])
        vb = place("vb", [P, 4, HALF])
        sqb = place("sqb", [P, 2, HALF])
        lg = place("lg", [P, 2, RH])
        kdec = place("kdec", [P, 2, RH])
        cdec = place("cdec", [P, 2, RH])
        arena = here[0]

        x_nat = place("x_nat", [P, NT, D])
        pre_over_h = nc.alloc_sbuf_tensor_at("pre_over_h", [P, 2, KC, 4 * P], F32, offset=h_at)
        pre_sb = nc.alloc_sbuf_tensor_at("pre_sb", [P, 2, 4 * P], F32, offset=h_at + 2 * KC * 4 * P * 4)
        pre_arena = place("pre_arena", [P, 2, KC, 4 * P])
        here[0] = arena
        ret = place("ret", [P, NT, RH * RV])
        zp = place("zp", [P, CC, ZW])
        cacc = place("cacc", [P, CC, CW])
        head_arena = here[0]
        qT = place("qT", [P, 2, T])
        kT = place("kT", [P, 2, T])
        v_nat = place("v_nat", [P, NT, RV])
        gate = place("gate", [P, NT, RV])
        qdec = place("qdec", [P, 2, T])
        kd_nat = place("kd_nat", [P, 2, NT, P])
        S = place("S", [P, 2, 4, RV])
        here[0] = norm_buffers
        dmat = place("dmat", [P, 2, P])
        qtab = place("qtab", [P, 2, P])
        here[0] = norm_buffers + 4 * T
        state_out = place("state_out", [P, 2, RV])
        bst = place("bst", [P, NT, 6])
        bmv = place("bmv", [P, NT, 2])
        brs = place("brs", [P, NT, 1])
        here[0] = norm_buffers + 8 * T
        prob = place("prob", [P, T])
        sgate = nc.alloc_sbuf_tensor_at("sgate", [P, CC, T], F32, offset=arena)
        here[0] = head_arena
        cH = place("cH", [P, CC, T], F32R)
        cL = place("cL", [P, CC, T], F32R)
        cst = place("cst", [P, 2, T])
        cmp_ = place("cmp", [P, 2, T])
        here[0] = arena
        fH = place("fH", [P, KC, T], F32R)
        fL = place("fL", [P, KC, T], F32R)
        fr = place("fr", [P, 2, HALF])
        fs = place("fs", [P, 2, HALF])
        mlp_end = here[0]
        here[0] = arena
        q_nat = place("q_nat", [P, 2, NT, RV])
        k_nat = place("k_nat", [P, NT, RV])
        va = place("va", [P, NT + 1, RV])
        kc_nat = place("kc_nat", [P, RV])
        behind_values = here[0]
        kro = place("kro", [P, NT, RV])
        qro = place("qro", [P, NT, RV])
        rtmp = place("rtmp", [P, 2, NT, 2, 64])
        rn = place("rn", [P, NT, RV])
        rss = place("rss", [P, NT * 2])
        tabs = place("tabs", [P, 2, 4, NT, 64])
        rope_sb = nc.alloc_sbuf_tensor_at("rope_sb", [P, 2, NT, 64], F32, offset=here[0])
        gqk = nc.alloc_sbuf_tensor_at("gqk", [P, 2, P], F32, offset=here[0] + 2 * NT * 64 * 4)
        kTa = place("kTa", [P, KVH, P + KEYS])
        qTa = place("qTa", [P, QH, T])
        here[0] = arena
        pr = place("pr", [P, 2, KEYS])
        pT = nc.alloc_sbuf_tensor_at("pT", [P, 2, NT, LAT], F32, offset=behind_values)
        amx = place("amx", [P, 2, 4])
        asum = place("asum", [P, 2, 4])
        here[0] = mlp_end
        y_nat = place("y_nat", [P, NT, D])
        gfin = place("gfin", [P, D])
        yr = place("yr", [P, NT])

        ident = const[:, C_ID:C_ID + P]
        sel = const[:, C_SEL:C_SEL + 2]

        ps = ctx.enter_context(nc.psum_tensor("ps", [P, 8, 512], F32))
        B_ADA = 4

        def sem(name):
            return ctx.enter_context(nc.semaphore(name))

        vec_in, const_in = sem("vec_in"), sem("const_in")
        x_in = [sem("x_in0"), sem("x_in1")]
        pre_in = [sem(f"pre_in{j}") for j in range(N_PRE // 4)]
        raw_in = [sem("raw_in0"), sem("raw_in1")]
        ada_in = sem("ada_in")
        s0_in, att_in, store = sem("s0_in"), sem("att_in"), sem("store")
        act_dma, k_st, v_st = sem("act_dma"), sem("k_st"), sem("v_st")
        wh_done, wl_done = sem("wh_done"), sem("wl_done")
        acc_full, act_free, dve_free = sem("acc_full"), sem("act_free"), sem("dve_free")
        set_up, siluc_ready = sem("set_up"), sem("siluc_ready")
        pre_strips, pre_ev, pre_fin, pre_mod = sem("pre_strips"), sem("pre_ev"), sem("pre_fin"), sem("pre_mod")
        ada_strips, ada_ev, ada_fin, mod_done = sem("ada_strips"), sem("ada_ev"), sem("ada_fin"), sem("mod_done")
        coef_done = sem("coef_done")
        sq_done, sum_done, stat_full, std_done = sem("sq_done"), sem("sum_done"), sem("stat_full"), sem("std_done")
        rstd_done, u_done, v_done = sem("rstd_done"), sem("u_done"), sem("v_done")
        w_done, hh_done = sem("w_done"), sem("hh_done")
        h_ready = sem("h_ready")
        conv_done, cn_sum, csum_done, crec_done = sem("conv_done"), sem("cn_sum"), sem("csum_done"), sem("crec_done")
        cstat_in, cstat_full, csq_done, cstd_done = sem("cstat_in"), sem("cstat_full"), sem("csq_done"), sem("cstd_done")
        cx_done, cn_done, csilu_done, ch_done, cl_done = (sem("cx_done"), sem("cn_done"), sem("csilu_done"),
                                                          sem("ch_done"), sem("cl_done"))
        lg_raw, lg_done, dec_done = sem("lg_raw"), sem("lg_done"), sem("dec_done")
        dexp_done, dm_done = sem("dexp_done"), sem("dm_done")
        st_full, prob_done, qdec_done, kd_done = sem("st_full"), sem("prob_done"), sem("qdec_done"), sem("kd_done")
        u_full, s_done, so_done, o_full, o_out = sem("u_full"), sem("s_done"), sem("so_done"), sem("o_full"), sem("o_out")
        bn_done, bstd_done, brs_done, on_done, ret_done = (sem("bn_done"), sem("bstd_done"), sem("brs_done"),
                                                           sem("on_done"), sem("ret_done"))
        rt_full, rth_done, rtl_done = sem("rt_full"), sem("rth_done"), sem("rtl_done")
        fr_done, fs_done, fh_done, f_ready = sem("fr_done"), sem("fs_done"), sem("fh_done"), sem("f_ready")
        tab_done, rsq_done, rss_done, rstd2, rrec = sem("tab_done"), sem("rsq_done"), sem("rss_done"), sem("rstd2"), sem("rrec")
        rn_done, rm_done, ro_done = sem("rn_done"), sem("rm_done"), sem("ro_done")
        tr_full, tr_out = sem("tr_full"), sem("tr_out")
        sc_full, mx_done, nmx_done, ex_done = sem("sc_full"), sem("mx_done"), sem("nmx_done"), sem("ex_done")
        rc_done, pn_done, pt_full, pt_act, pt_dve = (sem("rc_done"), sem("pn_done"), sem("pt_full"),
                                                     sem("pt_act"), sem("pt_dve"))
        pv_full, ah_done, attn_ready = sem("pv_full"), sem("ah_done"), sem("attn_ready")
        g_in, y_full, y_act, y_dve, y_pool = sem("g_in"), sem("y_full"), sem("y_act"), sem("y_dve"), sem("y_pool")

        pre_w = [pre_over_h[:, 0], pre_over_h[:, 1], pre_arena[:, 0], pre_arena[:, 1]]

        block = ctx.enter_context(nc.Block())

        @block.sync
        def _(sp):
            def cols(w, k0, nk, c0, n):
                return w[k0 * P:(k0 + nk) * P, bass.ds(c0, n)].rearrange("(k p) n -> p k n", p=P)

            def load_tile(t, halves, first=False):
                for j, src in enumerate(halves):
                    if not first:
                        sp.wait_ge(wl_done, 2 * t - 1 + j)
                    n = src.shape[2]
                    sp.dma_start(raw[:, j, :].rearrange("p (k n) -> p k n", n=n), src).then_inc(raw_in[j], 16)

            def k8(w, c0, row0=0):
                return [w[row0 + 512 * j:row0 + 512 * (j + 1), bass.ds(c0, 256)]
                        .rearrange("(k p) n -> p k n", p=P) for j in range(2)]

            def load_ada(p, layer, col, first=False):
                if not first:
                    sp.wait_ge(ada_strips, p)
                sp.dma_start(ada[:], ada_w[layer, :, bass.ds(col, 256)]
                             .rearrange("(k p) n -> p k n", p=P)).then_inc(ada_in, 16)

            sp.dma_start(vecT[:], feature_vectors).then_inc(vec_in, 16)
            sp.dma_start(const[:], shape_const).then_inc(const_in, 16)

            def load_x(half, tiles):
                for tile in tiles:
                    src = x_prompt[0] if tile == CTX_TILE else x_sample[0, LAT_TILES.index(tile) * P:][:P]
                    sp.dma_start(x_nat[:, tile, :], src).then_inc(x_in[half], 16)

            def load_pre(j):
                c0 = 4 * PRE_ORDER[j] * P
                sp.dma_start(pre_w[j], ada_w[0, :, c0:c0 + 4 * P].rearrange("(k p) n -> p k n", p=P)).then_inc(pre_in[j], 16)

            load_x(0, (0, 1, CTX_TILE))
            load_pre(0)
            load_x(1, (3, 4))
            load_pre(1)
            load_pre(2)
            load_tile(0, k8(even_w_in[0], CONV), first=True)
            load_pre(3)
            for t in range(4):
                if t:
                    load_tile(t, k8(even_w_in[0], (CONV, CONV + 256, 0, 256)[t]))
                load_ada(t, 0, N_PRE * P + 256 * t, first=(t == 0))
            with sp.Fori(0, 2) as i:
                for b in range(6):
                    col = (1024 + 256 * i, 1536 + 256 * i, 2048 + 512 * i, 3072 + 512 * i,
                           2304 + 512 * i, 3328 + 512 * i)[b]
                    load_tile(T_HEADS + 6 * i + b, k8(even_w_in[0], col))
                    p = M_HEADS + 6 * i + b
                    load_ada(p, 0, N_PRE * P + 256 * p)
                    if b in (2, 5):
                        head = 2 * i + (b == 5)
                        sp.wait_ge(acc_full, G_HEADS + G_PAIR * i + (17 if b == 5 else -1))
                        for r in range(2):
                            sp.dma_start(S[:, r, 3 * r, :], state_ret[0, 0, r, bass.ds(head, 1)]
                                         .rearrange("a d e -> (a d) e")).then_inc(s0_in, 16)
            for t in range(4):
                load_tile(T_WR + t, k8(even_w_out[0], 256 * t, CONV))
            for t in range(2):
                load_tile(T_WC + t, [even_w_out[0, 256 * j:256 * (j + 1), 512 * t:512 * (t + 1)]
                                     .rearrange("(k p) n -> p k n", p=P) for j in range(2)])

            def load_mlp(layer, first_tile):
                with sp.Fori(0, FG) as g:
                    for b in range(8):
                        if b < 4:
                            halves = k8(mlp_w1[layer], 1024 * g + 256 * b)
                        else:
                            halves = [mlp_w2[layer, bass.ds(1024 * g + 512 * j, 512), 256 * (b - 4):256 * (b - 3)]
                                      .rearrange("(k p) n -> p k n", p=P) for j in range(2)]
                        load_tile(first_tile + 8 * g + b, halves)
                        if layer == 0 and b in MLP_PAIR:
                            load_ada(M_MLP + 6 * g + MLP_PAIR[b], 1, 256 * (6 * g + MLP_PAIR[b]))

            load_mlp(0, T_MLP0)
            sp.dma_start(rope_sb[:], rope_const).then_inc(att_in, 16)
            sp.dma_start(gqk[:, 0, :], odd_q_g[0].partition_broadcast(P)).then_inc(att_in, 16)
            sp.dma_start(gqk[:, 1, :], odd_k_g[0].partition_broadcast(P)).then_inc(att_in, 16)
            load_tile(T_QKV, k8(odd_w_qkv[0], 1024))
            load_tile(T_QKV + 1, k8(odd_w_qkv[0], 0))
            sp.wait_ge(acc_full, G_QKV)
            sp.dma_start(kc_nat[:], cache_k[0, 0].rearrange("t h d -> t (h d)")).then_inc(att_in, 16)
            sp.dma_start(va[:, NT, :], cache_v[0, 0].rearrange("t h d -> t (h d)")).then_inc(att_in, 16)
            for t in range(2, 6):
                load_tile(T_QKV + t, k8(odd_w_qkv[0], (256, 512, 768, 1280)[t - 2]))
            for t in range(2):
                load_tile(T_WO + t, k8(odd_w_o[0], 256 * t))
            sp.wait_ge(ro_done, 2)
            sp.dma_start(new_k[0, 0].rearrange("t h d -> t (h d)"), kro[:, CTX_TILE, :]).then_inc(k_st, 16)
            sp.wait_ge(act_free, A_QKV + 30)
            sp.dma_start(new_v[0, 0].rearrange("t h d -> t (h d)"), va[:, CTX_TILE, :]).then_inc(v_st, 16)
            for t in range(2, 4):
                load_tile(T_WO + t, k8(odd_w_o[0], 256 * t))
            sp.wait_ge(acc_full, G_WO + 1)
            sp.dma_start(gfin[:], final_g.partition_broadcast(P)).then_inc(g_in, 16)
            load_mlp(1, T_MLP1)
            for tile in range(NT):
                sp.wait_ge(y_pool, tile + 1)
                sp.wait_ge(y_dve, tile + 1)
                if tile == CTX_TILE:
                    dst = y_prompt[0]
                else:
                    n = LAT_TILES.index(tile)
                    dst = y_sample[0, n * P:(n + 1) * P, :]
                sp.dma_start(dst, y_nat[:, tile, :]).then_inc(store, 16)
            sp.wait_ge(store, 16 * NT)
            sp.wait_ge(k_st, 16)
            sp.wait_ge(v_st, 16)
            sp.wait_ge(act_dma, 16 * (RH + 1))

        @block.tensor
        def _(pe):
            def product(groups, nk, waits, width):
                for k in range(nk):
                    waits(k)
                    for bank, lhs, rhs in groups:
                        (aH, aL), (bH, bL) = lhs(k), rhs(k)
                        for p_, (a_, b_) in enumerate(((aH, bH), (aH, bL), (aL, bH))):
                            last = nc.tensor.matmul(ps[:, bank, 0:width], a_, b_, start=(k == 0 and p_ == 0),
                                                    stop=(k == nk - 1 and p_ == 2))
                        if k == nk - 1:
                            last.then_inc(acc_full, 1)

            def w_wait(t, k, nk):
                if k == 0:
                    pe.wait_ge(wl_done, 2 * t + 1)
                elif k == nk // 2:
                    pe.wait_ge(wl_done, 2 * t + 2)

            def tile_t(t, slot, xH, xL, free, x_wait=None, hooks=None, nk=KC, nm=2, bank0=0, inside=None, pairs=False):
                wv = [w[:, slot, :].rearrange("p (k n) -> p k n", k=nk) for w in (wH, wL)]

                def group(n):
                    half, m = n // nm, n % nm
                    return ((bank0 + n) % 4, lambda k: [w[:, k, m * P:(m + 1) * P] for w in wv],
                            lambda k: [x[:, k, half * HALF:(half + 1) * HALF] for x in (xH, xL)])

                together = 2 if pairs else 1
                for n in range(0, 2 * nm, together):
                    for q in range(n, n + together):
                        free(q)

                    def waits(k, n=n):
                        if n == 0:
                            w_wait(t, k, nk)
                        if inside and inside[:2] == (n, k):
                            inside[2]()
                        if x_wait and n % nm == 0:
                            x_wait(n // nm, k)
                    product([group(q) for q in range(n, n + together)], nk, waits, HALF)
                    for q in (n,) if not pairs else (0,) if n == 0 else (1, 2, 3):
                        for hook in (hooks or {}).get(q, ()):
                            hook()

            def tile_n(t, slot, free, banks, x_wait=None, hooks=None, inside=None):
                wv = [w[:, slot, :].rearrange("p (k n) -> p k n", k=KC) for w in (wH, wL)]

                def group(n):
                    return (banks[n], lambda k: [x[:, k, n * P:(n + 1) * P] for x in (hH, hL)],
                            lambda k: [w[:, k, :] for w in wv])

                for ns in (((0, 1), (2, 3), (4,)) if x_wait else [(n,) for n in range(NT)]):
                    for q in ns:
                        free(q)

                    def waits(k, n=ns[0]):
                        if n == 0:
                            w_wait(t, k, KC)
                        if inside and inside[:2] == (n, k):
                            inside[2]()
                        if x_wait and n in (0, 2):
                            x_wait(n // 2, k)
                    product([group(q) for q in ns], KC, waits, 256)
                    for q in ns:
                        for hook in (hooks or {}).get(q, ()):
                            hook()

            def strips(p):
                pe.wait_ge(ada_in, 16 * (p + 1))
                if not (isinstance(p, int) and p == 0):
                    pe.wait_ge(mod_done, p)
                for k in range(KC):
                    j = k % 4
                    last = nc.tensor.matmul(ps[32 * j:32 * j + 32, B_ADA, 0:256], siluc[:, k, :], ada[:, k, :],
                                            start=(k < 4), stop=(k >= 4), tile_position=(0, 32 * j))
                last.then_inc(ada_strips, 1)

            def finish(p):
                pe.wait_ge(ada_ev, p + 1)
                for a in range(2):
                    last = nc.tensor.matmul(ps[:, B_ADA, 256 + 2 * a:258 + 2 * a], ada_sb[:, a * P:(a + 1) * P], sel,
                                            start=True, stop=True)
                last.then_inc(ada_fin, 1)

            def ada_hooks(p):
                return {0: [lambda: strips(p)], 1: [lambda: finish(p)]}

            def stat(norm, half, count):
                pe.wait_ge(sum_done, SUMS * norm + count)
                nc.tensor.matmul(ps[:, 5 + half, 0:HALF], ones[:], ssum[:, half, :], start=True,
                                 stop=True).then_inc(stat_full, 1)

            def h_wait(norm):
                return lambda half, k: pe.wait_ge(h_ready, 16 * norm + 8 * half + k + 1)

            def turn(bank, src, col0):
                def one(tile, p0, np_, at, last=False):
                    return nc.tensor.transpose(ps[:, bank, at:at + np_], src[p0:p0 + np_, tile, col0:col0 + P],
                                               ident[p0:p0 + np_, p0:p0 + np_])
                return one

            def turn_half(bank, src, col0, half, full):
                one = turn(bank, src, col0)
                if half == 0:
                    one(0, 0, P, 0)
                    one(1, 0, P, P)
                    last = one(CTX_TILE, 0, 64, 256)
                else:
                    one(CTX_TILE, 64, 64, 0)
                    one(3, 0, P, 64)
                    last = one(4, 0, P, 192)
                last.then_inc(full, 1)

            pe.wait_ge(const_in, 16)

            def x_group(n):
                if n == 0:
                    pe.wait_ge(x_in[0], 3 * 16)
                elif n == 8:
                    pe.wait_ge(x_in[1], 2 * 16)
                if n >= 4:
                    pe.wait_ge(dve_free, n - 3)
                turn_half(n % 4, x_nat, (n % 8) * P, n // 8, acc_full)

            def pre_strip(j):
                pe.wait_ge(pre_in[j], 16)
                if j:
                    pe.wait_ge(pre_ev, j)
                for k in range(KC):
                    q = k % 4
                    last = nc.tensor.matmul(ps[32 * q:32 * q + 32, B_ADA, :], siluc[:, k, :], pre_w[j][:, k, :],
                                            start=(k < 4), stop=(k >= 4), tile_position=(0, 32 * q))
                last.then_inc(pre_strips, 1)

            def pre_finish(j):
                pe.wait_ge(pre_ev, j + 1)
                if j >= 2:
                    pe.wait_ge(pre_mod, j - 1)
                for q in range(4):
                    last = nc.tensor.matmul(ps[:, 6 + j % 2, 2 * q:2 * q + 2], pre_sb[:, j % 2, q * P:(q + 1) * P], sel,
                                            start=True, stop=True)
                last.then_inc(pre_fin, 1)

            for n in range(6):
                x_group(n)
            pe.wait_ge(siluc_ready, 1)
            for j, (n0, n1) in enumerate(((6, 9), (9, 13), (13, 16), (16, 16))):
                if j == 3:
                    stat(0, 0, SUM_AT["half"][3])
                    pe.wait_ge(pre_mod, 3)
                    stat(0, 1, SUM_AT["half"][7])
                pre_strip(j)
                for n in range(n0, n1):
                    x_group(n)
                pre_finish(j)

            for t in range(4):
                if t < 2:
                    free = lambda n, t=t: (pe.wait_ge(dve_free, 13 + n) if t == 0 else pe.wait_ge(act_free, n + 1))
                else:
                    free = lambda n, t=t: (pe.wait_ge(act_free, 5 + n) if t == 2
                                           else pe.wait_ge(dve_free, V_VAL + n + 1))
                tile_t(t, t % 2, hH, hL, free, h_wait(0) if t == 0 else None,
                       ada_hooks(t), pairs=(t == 0))

            def scores(i, e):
                pe.wait_ge(act_free, A_HEADS + G_PAIR * i + (18 if e else 8))
                k_of = lambda tile: kT[:, e, tile * P:(tile + 1) * P]
                q_of = lambda tile: qT[:, e, tile * P:(tile + 1) * P]
                for n, tile in enumerate(LAT_TILES):
                    last = nc.tensor.matmul(ps[:, 5, n * P:(n + 1) * P], k_of(tile), q_of(tile), start=True, stop=True)
                last.then_inc(st_full, 1)
                nc.tensor.matmul(ps[:, 7, 0:P], k_of(CTX_TILE), q_of(CTX_TILE), start=True, stop=True)
                nc.tensor.transpose(ps[:, 7, P:2 * P], k_of(CTX_TILE), ident).then_inc(st_full, 1)
                for n, tile in enumerate(LAT_TILES):
                    last = nc.tensor.transpose(ps[:, 6, n * P:(n + 1) * P], k_of(tile), ident)
                last.then_inc(st_full, 1)

            def update(bank, at, r, tile):
                return nc.tensor.matmul(ps[:, bank, at:at + RV], kd_nat[:, r, tile, :], v_nat[:, tile, :],
                                        start=True, stop=True)

            def updates_1(i, e):
                head = 2 * i + e
                pe.wait_ge(kd_done, 4 * head + 4)
                pe.wait_ge(prob_done, 2 * head + 2)
                pe.wait_ge(act_free, A_HEADS + G_PAIR * i + 13 + 10 * e)
                for bank, (a_, b_) in ((5, ((0, 0), (0, 1))), (6, ((0, 3), (0, CTX_TILE))), (7, ((1, 4), (1, 3)))):
                    update(bank, 0, *a_)
                    update(bank, RV, *b_).then_inc(u_full, 1)

            def updates_2(i, e):
                pe.wait_ge(s_done, 6 * (2 * i + e) + 2)
                update(5, 0, 1, 1)
                update(5, RV, 1, CTX_TILE).then_inc(u_full, 1)

            def outputs(i, e):
                head = 2 * i + e
                pe.wait_ge(s_done, 6 * head + 6)
                pe.wait_ge(so_done, 2 * head + 2)
                pe.wait_ge(qdec_done, 4 * head + 4)
                for tile in range(NT):
                    out = ps[:, 5 + tile // 2, (tile % 2) * RV:(tile % 2 + 1) * RV]
                    cs = slice(tile * P, (tile + 1) * P)
                    ctx_ = tile == CTX_TILE
                    last = nc.tensor.matmul(out, prob[:, cs], v_nat[:, tile, :], start=True, stop=ctx_)
                    if not ctx_:
                        n = LAT_TILES.index(tile)
                        for r in range(2):
                            last = nc.tensor.matmul(out, qdec[:, r, cs], S[:, r, n, :], start=False, stop=(r == 1))
                    if tile in (1, 3, 4):
                        last.then_inc(o_full, 1)

            with pe.Fori(0, 2) as i:
                at = 0
                for b in range(6):
                    t = T_HEADS + 6 * i + b
                    hooks = ada_hooks(M_HEADS + 6 * i + b)
                    free = lambda n, at=at: pe.wait_ge(act_free, A_HEADS + G_PAIR * i + at + n - 3)
                    if b == 0:
                        free0 = free

                        def free(n, free0=free0):
                            if n < 4:
                                pe.wait_ge(dve_free, V_WR - 3 + n)
                            free0(n)
                    if b < 2:
                        tile_t(t, b % 2, hH, hL, free, None, hooks)
                        at += 4
                        continue
                    e = (b - 2) // 2
                    if b % 2 == 0:
                        hooks[0].append(lambda e=e: scores(i, e))
                    else:
                        hooks[0].append(lambda e=e: updates_1(i, e))
                        hooks[1].append(lambda e=e: updates_2(i, e))
                        hooks[2] = [lambda e=e: outputs(i, e)]
                    tile_n(t, b % 2, free, [(at + n) % 4 for n in range(NT)], None, hooks)
                    at += 5

            def turn_retention(n):
                pe.wait_ge(ret_done, n % 8 // 2 + 1)
                if n >= 4:
                    pe.wait_ge(rtl_done, n - 3)
                elif n == 0:
                    pe.wait_ge(mod_done, M_MLP)
                    pe.wait_ge(act_free, A_MLP0)
                turn_half(4 + n % 4, ret, (n % 8) * P, n // 8, rt_full)

            for n in range(8):
                turn_retention(n)

            def channel_stat(which):
                pe.wait_ge(cstat_in, which + 1)
                nc.tensor.matmul(ps[:, 5, 0:LAT], ones[:], cst[:, which, 0:LAT], start=True, stop=True)
                nc.tensor.matmul(ps[:, 6, 0:CTX], ones[:], cst[:, which, LAT:T], start=True,
                                 stop=True).then_inc(cstat_full, 1)

            for t in range(4):
                def free(n, t=t):
                    if t == 0 and n < 4:
                        pe.wait_ge(act_free, A_MLP0 - 3 + n)
                    else:
                        pe.wait_ge(dve_free, V_WR + 4 * t + n - 3)
                tile_t(T_WR + t, t % 2, hH, hL, free,
                       (lambda half, k: pe.wait_ge(rtl_done, 8 * half + k + 1)) if t == 0 else None,
                       {0: {2: [lambda: channel_stat(0)]}, 1: {2: [lambda: channel_stat(1)]}}.get(t),
                       inside=(0, 7, lambda: [turn_retention(n) for n in range(8, 16)]) if t == 0 else None,
                       pairs=(t == 0))
            pe.wait_ge(cl_done, 2 * CC)
            for t in range(2):
                tile_t(T_WC + t, t % 2, cH, cL, lambda n, t=t: pe.wait_ge(dve_free, V_WC + 8 * t + n - 3),
                       nk=CC, nm=4, inside=(5, 1, lambda: stat(1, 0, SUM_AT["wc"][5])) if t else None)
            V_LAST = V_MLP1 + 16 * (FG - 1)

            def turn_output(tile):
                pe.wait_ge(dve_free, V_LAST + (14 if tile < 2 else 16))
                if tile in (2, 3):
                    pe.wait_ge(y_dve, tile - 1)
                    pe.wait_ge(y_act, tile - 1)
                for kq in range(2):
                    for j in range(4):
                        last = nc.tensor.transpose(ps[:, Y_BANKS[tile][kq], j * P:(j + 1) * P],
                                                   xT[:, 4 * kq + j, tile * P:(tile + 1) * P], ident)
                    last.then_inc(y_full, 1)

            def token_sums(part, count):
                pe.wait_ge(sum_done, 4 * SUMS + count)
                flat = ssum[:].rearrange("p a n -> p (a n)")
                for j, tile in enumerate(Y_TILES[part]):
                    last = nc.tensor.matmul(ps[:, part, j:j + 1], flat[:, tile * P:(tile + 1) * P], ones[:, 0:1],
                                            start=True, stop=True)
                last.then_inc(stat_full, 1)

            def mlp_tile(g, b, layer, norm, first=False, last=False):
                t0, a0, v0, f0 = ((T_MLP0, A_MLP0, V_MLP0, 0), (T_MLP1, A_MLP1, V_MLP1, 64))[layer]
                c, hooks, x_wait, inside = b % 4, {}, None, None
                if layer == 0 and b in MLP_PAIR:
                    hooks = ada_hooks(M_MLP + 6 * g + MLP_PAIR[b])
                if b < 4:
                    if b == 0:
                        x_wait = h_wait(norm)
                    if first:
                        inside = (0, 4, lambda: stat(norm, 1, SUMS))

                    def free(n):
                        if b == 0:
                            pe.wait_ge(dve_free, v0 + 16 * g - 3 + n)
                        else:
                            pe.wait_ge(act_free, a0 + 16 * g + 4 * b + n - 3)
                    tile_t(t0 + 8 * g + b, b % 2, hH, hL, free, x_wait, hooks, inside=inside, pairs=first)
                else:
                    if last and layer == 0:
                        inside = (2, 6, lambda: stat(norm + 1, 0, SUM_AT["tile"][6]))
                    elif last:
                        hooks[2] = [lambda: (turn_output(0), turn_output(1), token_sums(0, SUM_AT["tile"][6]))]

                    def free(n):
                        if c == 0:
                            pe.wait_ge(act_free, a0 + 16 * g + 13 + n)
                        else:
                            pe.wait_ge(dve_free, v0 + 16 * g + 4 * c + n - 3)
                    if c == 0:
                        x_wait = lambda half, k: pe.wait_ge(f_ready, f0 + 16 * g + 4 * (k // 2) + 2 * half + k % 2 + 1)
                    tile_t(t0 + 8 * g + b, b % 2, fH, fL, free, x_wait, hooks, inside=inside)

            def mlp(layer, norm):
                mlp_tile(0, 0, layer, norm, first=True)
                with pe.Fori(0, FG - 1) as g:
                    for b in range(1, 9):
                        mlp_tile(g + b // 8, b % 8, layer, norm)
                for b in range(1, 8):
                    mlp_tile(FG - 1, b, layer, norm, last=(b == 7))

            mlp(0, 1)

            def turn_keys():
                pe.wait_ge(ro_done, 2)
                pe.wait_ge(att_in, 16 * 5)
                for h in range(KVH):
                    cs = slice(h * P, (h + 1) * P)
                    for n, tile in enumerate(LAT_TILES):
                        last = nc.tensor.transpose(ps[:, 4 + h, n * P:(n + 1) * P], kro[:, tile, cs], ident)
                    last.then_inc(tr_full, 1)
                    nc.tensor.transpose(ps[:, 6, 2 * h * P:(2 * h + 1) * P], kro[:, CTX_TILE, cs], ident)
                    last = nc.tensor.transpose(ps[:, 6, (2 * h + 1) * P:(2 * h + 2) * P], kc_nat[:, cs], ident)
                last.then_inc(tr_full, 1)

            def turn_queries(r):
                pe.wait_ge(ro_done, 2 * r + 4)
                pe.wait_ge(tr_out, 3 * (r + 1))
                for h in range(2):
                    cs = slice(h * P, (h + 1) * P)
                    for n, tile in enumerate(LAT_TILES):
                        last = nc.tensor.transpose(ps[:, 4 + h, n * P:(n + 1) * P], qro[:, tile, cs], ident)
                    last.then_inc(tr_full, 1)
                    last = nc.tensor.transpose(ps[:, 6, h * P:(h + 1) * P], qro[:, CTX_TILE, cs], ident)
                last.then_inc(tr_full, 1)

            for t in range(6):
                def free(n, t=t):
                    if t == 0:
                        if n < 4:
                            pe.wait_ge(dve_free, V_WO - 3 + n)
                    else:
                        pe.wait_ge(act_free, A_QKV + 5 * (t - 1) + n + 1)
                tile_n(T_QKV + t, t % 2, free, NAT_BANKS, h_wait(2) if t == 0 else None,
                       inside=(0, 4, lambda: stat(2, 1, SUMS)) if t == 0 else None)
                if t == 1:
                    turn_keys()
                elif t > 1:
                    turn_queries(t - 2)

            def att_scores(n):
                if n >= 2:
                    pe.wait_ge(ex_done, n - 1)
                if n >= KVH:
                    h, i = (n - KVH) // 4, (n - KVH) % 4
                    for j in range(2):
                        last = nc.tensor.matmul(ps[:, 2 * (n % 2) + j, 0:HALF], qTa[:, h, i * P:(i + 1) * P],
                                                kTa[:, h // GRP, P + j * HALF:P + (j + 1) * HALF], start=True, stop=True)
                else:
                    for j in range(GRP):
                        last = nc.tensor.matmul(ps[:, 2 * (n % 2), j * P:(j + 1) * P], qTa[:, GRP * n + j, LAT:T],
                                                kTa[:, n, 0:P], start=True, stop=True)
                last.then_inc(sc_full, 1)

            def att_turn(n):
                pe.wait_ge(pn_done, n + 1)
                if n >= 2:
                    pe.wait_ge(pt_act, n - 1)
                bank = 4 if n % 2 == 0 else 7
                for j in range(4):
                    last = nc.tensor.transpose(ps[:, bank, j * P:(j + 1) * P], pr[:, n % 2, j * P:(j + 1) * P], ident)
                if n >= KVH:
                    if n > KVH:
                        pe.wait_ge(pt_dve, n - KVH)
                    last = nc.tensor.transpose(ps[:, 5, 0:P], pr[:, n % 2, 4 * P:5 * P], ident)
                last.then_inc(pt_full, 1)

            def att_values(v):
                if v >= 1:
                    pe.wait_ge(attn_ready, v)
                if v < KVH:
                    pe.wait_ge(pt_act, v + 1)
                    last = nc.tensor.matmul(ps[:, 6, :], va[:, CTX_TILE, v * P:(v + 1) * P], pT[:, 1, v, :],
                                            start=True, stop=True)
                else:
                    h = v - KVH
                    pe.wait_ge(pt_act, KVH + 4 * h + 4)
                    pe.wait_ge(pt_dve, 4 * h + 4)
                    kv = h // GRP
                    for n, vt in enumerate((NT,) + LAT_TILES):
                        last = nc.tensor.matmul(ps[:, 6, :], va[:, vt, kv * P:(kv + 1) * P], pT[:, h % 2, n, :],
                                                start=(n == 0), stop=(n == 4))
                last.then_inc(pv_full, 1)

            pe.wait_ge(tr_out, 15)
            pe.wait_ge(act_free, A_QKV + 30)
            att_scores(0)
            att_scores(1)
            for n in range(N_ATT):
                if n + 2 < N_ATT:
                    att_scores(n + 2)
                att_turn(n)
                if n in VALUES_AT:
                    att_values(VALUES_AT[n])
            att_values(KVH + QH - 1)

            for t in range(4):
                tile_t(T_WO + t, t % 2, hH, hL,
                       lambda n, t=t: (None if t == 0 else pe.wait_ge(dve_free, V_WO + 4 * t + n - 3)),
                       (lambda half, k: pe.wait_ge(attn_ready, KVH + k + 1)) if t == 0 else None,
                       inside=(2, 6, lambda: stat(3, 0, SUM_AT["tile"][6])) if t == 3 else None)

            mlp(1, 3)
            turn_output(2)
            token_sums(1, SUMS)
            turn_output(3)
            turn_output(4)

        @block.scalar
        def _(act):
            def seg(x, half, s):
                c0, n, which = SEGS[half][s]
                return x[..., c0:c0 + n], which

            def split(t, slot, start=None):
                if start is not None:
                    act.wait_ge(acc_full, start)
                for j in range(2):
                    act.wait_ge(raw_in[j], 16 * (t + 1))
                    nc.scalar.activation(wH[:, slot, j * 1024:(j + 1) * 1024], raw[:, j, :], ACT.Copy).then_inc(wh_done, 1)

            def strips_out(p):
                act.wait_ge(ada_strips, p + 1)
                nc.scalar.activation(ada_sb[:], ps[:, B_ADA, 0:256], ACT.Copy).then_inc(ada_ev, 1)

            def add_bias(p):
                act.wait_ge(ada_fin, p + 1)
                act.wait_ge(vec_in, 16)
                for a in range(2):
                    n = N_PRE + 2 * p + a
                    last = nc.scalar.activation(modT[:, bass.ds(n, 1), :].rearrange("p a c -> p (a c)"),
                                                ps[:, B_ADA, 256 + 2 * a:258 + 2 * a],
                                                ACT.Identity, bias=vecT[:, 1, bass.ds(n, 1)])
                last.then_inc(mod_done, 1)

            def square(norm, s, v0, order):
                half, p_ = PAIRS[order][s // 2]
                k = 2 * p_ + s % 2
                act.wait_ge(dve_free, v0 + s + 1)
                if s >= 2:
                    act.wait_ge(sum_done, SUMS * norm + SUM_AT[order][s // 2 - 1])
                nc.scalar.activation(sqb[:, s % 2, :], xT[:, k, half * HALF:(half + 1) * HALF], ACT.Square).then_inc(sq_done, 1)

            def std(norm, half):
                act.wait_ge(stat_full, 2 * norm + half + 1)
                nc.scalar.activation(rstd[:, half, :], ps[:, 5 + half, 0:HALF], ACT.Sqrt, bias=eps[:],
                                     scale=1.0 / D).then_inc(std_done, 1)

            def hi(norm, half, ks=range(KC)):
                for k in ks:
                    n = 16 * norm + 8 * half + k
                    act.wait_ge(v_done, n + 1)
                    if k % 2:
                        for c0, w_, which in SEGS[half]:
                            v = vb[:, k % 4, c0 - half * HALF:c0 - half * HALF + w_]
                            last = nc.scalar.activation(v, v, ACT.Identity,
                                                        bias=modT[:, SHIFT_AT[norm] + k, which:which + 1])
                        last.then_inc(w_done, 1)
                        act.wait_ge(w_done, (n + 1) // 2)
                    nc.scalar.activation(hH[:, k, half * HALF:(half + 1) * HALF], vb[:, k % 4, :],
                                         ACT.Copy).then_inc(hh_done, 1)

            def h_hi(norm):
                for half in range(2):
                    std(norm, half)
                    hi(norm, half)

            def last_tile(norm, v0, t, slot, start):
                square(norm, 12, v0, "tile")
                square(norm, 13, v0, "tile")
                std(norm, 0)
                hi(norm, 0, range(0, 2))
                square(norm, 14, v0, "tile")
                hi(norm, 0, range(2, 4))
                square(norm, 15, v0, "tile")
                hi(norm, 0, range(4, 6))
                std(norm, 1)
                hi(norm, 0, range(6, 8))
                split(t, slot, start)
                hi(norm, 1)

            act.dma_start(lg[:].rearrange("p a b -> p (a b)"),
                          ret_log_decay.rearrange("a b c -> (a b c)").partition_broadcast(P)).then_inc(act_dma, 16)
            act.wait_ge(vec_in, 16)
            act.wait_ge(set_up, 3)
            nc.scalar.activation(siluc[:, :, 0:2].rearrange("p k c -> p c k"),
                                 vecT[:, 0, R_C:R_C + 16].rearrange("p (c k) -> p c k", c=2), ACT.Silu).then_inc(siluc_ready, 1)
            act.wait_ge(act_dma, 16)
            nc.scalar.activation(lg[:], lg[:], ACT.Exp).then_inc(lg_raw, 1)
            act.wait_ge(lg_done, 1)
            act.wait_ge(const_in, 16)
            for r in range(2):
                nc.scalar.activation(kdec[:, r, :], lg[:, r, :], ACT.Exp, scale=const[:, C_KP + r:C_KP + r + 1]).then_inc(dec_done, 1)
            nc.scalar.activation(cdec[:], lg[:], ACT.Exp, scale=float(P)).then_inc(dec_done, 1)

            def pre_out(j):
                act.wait_ge(pre_strips, j + 1)
                if j >= 2:
                    act.wait_ge(pre_fin, j - 1)
                nc.scalar.activation(pre_sb[:, j % 2, :], ps[:, B_ADA, :], ACT.Copy).then_inc(pre_ev, 1)

            for j, (s0, s1) in enumerate(((0, 4), (4, 8), (8, 12), (12, 16))):
                for s in range(s0, s1):
                    square(0, s, 0, "half")
                if j == 3:
                    std(0, 0)
                    std(0, 1)
                    split(0, 0)
                pre_out(j)
            hi(0, 0)
            hi(0, 1)

            for t in range(4):
                split(t + 1, (t + 1) % 2, 16 + 4 * t if t else None)
                for n in range(4):
                    g = G_GATE + 4 * t + n
                    if t < 2:
                        act.wait_ge(acc_full, g + 1)
                        nc.scalar.activation(sgate[:, 2 * t + n % 2, (n // 2) * HALF:(n // 2 + 1) * HALF],
                                             ps[:, n, 0:HALF], ACT.Sigmoid).then_inc(act_free, 1)
                    if n in ADA_STEP:
                        (strips_out, add_bias)[ADA_STEP[n]](t)

            def decay_tables(head, e):
                act.wait_ge(dec_done, 3)
                for r, col in enumerate((C_PF, C_PB)):
                    nc.scalar.activation(dmat[:, r, :], const[:, col:col + P], ACT.Exp,
                                         scale=lg[:, r, bass.ds(head, 1)]).then_inc(dexp_done, 1)
                for r, col in enumerate((C_QF, C_QB)):
                    nc.scalar.activation(qtab[:, r, :], const[:, col:col + P], ACT.Exp,
                                         scale=lg[:, r, bass.ds(head, 1)]).then_inc(dexp_done, 1)

            def decayed_keys(head):
                act.wait_ge(st_full, 3 * head + 3)
                act.wait_ge(prob_done, 2 * head + 2)
                act.wait_ge(dec_done, 2)
                for r in range(2):
                    sc = kdec[:, r, bass.ds(head, 1)]
                    for a_, b_ in ((0, 0), (3, 2)):
                        nc.scalar.activation(kd_nat[:, r, a_:a_ + 2, :],
                                             ps[:, 6, b_ * P:(b_ + 2) * P].rearrange("p (a b) -> p a b", a=2),
                                             ACT.Copy, scale=sc)
                    nc.scalar.activation(kd_nat[:, r, CTX_TILE, :], ps[:, 7, P:2 * P], ACT.Copy, scale=sc).then_inc(kd_done, 2)

            def ret_std(head):
                act.wait_ge(bn_done, 10 * head + 10)
                nc.scalar.activation(brs[:, :, 0], bmv[:, :, 1], ACT.Sqrt, bias=eps[:]).then_inc(bstd_done, 1)

            with act.Fori(0, 2) as i:
                at = 0
                for b in range(6):
                    e = (b - 2) // 2
                    head = 2 * i + e
                    split(T_HEADS + 6 * i + b + 1, (b + 1) % 2, G_HEADS + G_PAIR * i + at)
                    if b == 0:
                        decay_tables(2 * i, 0)
                    if b == 3:
                        decay_tables(2 * i + 1, 1)
                    for n in range(4 if b < 2 else NT):
                        act.wait_ge(acc_full, G_HEADS + G_PAIR * i + at + n + 1)
                        bank = (at + n) % 4
                        if b < 2:
                            dst, src = (qT, kT)[b][:, n % 2, (n // 2) * HALF:(n // 2 + 1) * HALF], ps[:, bank, 0:HALF]
                        else:
                            dst, src = (v_nat, gate)[b % 2][:, n, :], ps[:, bank, 0:RV]
                        nc.scalar.activation(dst, src, ACT.Silu if b in (3, 5) else ACT.Copy).then_inc(act_free, 1)
                        if n in ADA_STEP:
                            (strips_out, add_bias)[ADA_STEP[n]](M_HEADS + 6 * i + b)
                        if b in (2, 4) and n == 1:
                            decayed_keys(head)
                        if b == 4 and n == 0:
                            ret_std(2 * i)
                        if b == 4 and n == 2:
                            act.wait_ge(so_done, 2 * (2 * i) + 2)
                            act.dma_start(new_state[0, 0, :, bass.ds(2 * i, 1)].rearrange("r a d e -> d (r a) e"),
                                          state_out[:]).then_inc(act_dma, 16)
                        if b in (3, 5) and n == 3:
                            for q in range(3):
                                act.wait_ge(o_full, 3 * head + q + 1)
                                act.wait_ge(dve_free, V_WR)
                                w_ = 2 if q < 2 else 1
                                nc.scalar.activation(ret[:, 2 * q:2 * q + w_, bass.ds(512 * i + 256 * e, RV)],
                                                     ps[:, 5 + q, 0:w_ * RV].rearrange("p (a b) -> p a b", a=w_),
                                                     ACT.Copy).then_inc(o_out, 1)
                    at += 4 if b < 2 else NT
                ret_std(2 * i + 1)
                act.wait_ge(so_done, 2 * (2 * i + 1) + 2)
                act.dma_start(new_state[0, 0, :, bass.ds(2 * i + 1, 1)].rearrange("r a d e -> d (r a) e"),
                              state_out[:]).then_inc(act_dma, 16)

            for n in range(16):
                act.wait_ge(rt_full, n + 1)
                nc.scalar.activation(hH[:, n % 8, (n // 8) * HALF:(n // 8 + 1) * HALF], ps[:, 4 + n % 4, 0:HALF],
                                     ACT.Copy).then_inc(rth_done, 1)

            split(T_WR + 1, 1, G_WR)
            for ch in range(CC):
                act.wait_ge(cx_done, ch + 1)
                if ch >= 2:
                    act.wait_ge(csum_done, ch - 1)
                nc.scalar.activation(cmp_[:, ch % 2, 0:LAT], cacc[:, ch, 0:LAT], ACT.Square)
                nc.scalar.activation(cmp_[:, ch % 2, LAT:T], cacc[:, ch, LAT + PAD:CW], ACT.Square).then_inc(csq_done, 1)
            split(T_WR + 2, 0, G_WR + 4)
            split(T_WR + 3, 1, G_WR + 8)
            act.wait_ge(cstat_full, 2)
            nc.scalar.activation(cmp_[:, 0, 0:LAT], ps[:, 5, 0:LAT], ACT.Sqrt, bias=eps[:], scale=1.0 / CONV)
            nc.scalar.activation(cmp_[:, 0, LAT:T], ps[:, 6, 0:CTX], ACT.Sqrt, bias=eps[:], scale=1.0 / CONV).then_inc(cstd_done, 1)
            for ch in range(CC):
                act.wait_ge(cn_done, ch + 1)
                nc.scalar.activation(cacc[:, ch, :], cacc[:, ch, :], ACT.Silu, scale=vecT[:, 0, R_LG + ch:R_LG + ch + 1],
                                     bias=vecT[:, 0, R_LB + ch:R_LB + ch + 1]).then_inc(csilu_done, 1)
            for ch in range(CC):
                act.wait_ge(csilu_done, ch + 1)
                for a_, b_, n_ in CONV_MAP:
                    last = nc.scalar.activation(cH[:, ch, b_:b_ + n_], cacc[:, ch, a_:a_ + n_], ACT.Copy)
                last.then_inc(ch_done, 1)
            split(T_WC, 0, G_WR + 12)
            split(T_WC + 1, 1, G_WC)
            for n in range(8):
                square(1, n, V_WC, "wc")
            split(T_MLP0, 0, G_WC + 8)
            for n in range(8, 12):
                square(1, n, V_WC, "wc")
            act.wait_ge(act_dma, 16 * (RH + 1))
            std(1, 0)
            square(1, 12, V_WC, "wc")
            square(1, 13, V_WC, "wc")
            hi(1, 0, range(0, 4))
            square(1, 14, V_WC, "wc")
            square(1, 15, V_WC, "wc")
            hi(1, 0, range(4, 6))
            std(1, 1)
            hi(1, 0, range(6, 8))
            split(T_MLP0 + 1, 1, G_MLP0)
            hi(1, 1)

            def token_std(part):
                act.wait_ge(stat_full, 8 + part + 1)
                t0_, n_ = Y_TILES[part][0], len(Y_TILES[part])
                nc.scalar.activation(yr[:, t0_:t0_ + n_], ps[:, part, 0:n_], ACT.Sqrt, bias=eps[:],
                                     scale=1.0 / D).then_inc(std_done, 1)
                act.wait_ge(rstd_done, 8 + part + 1)

            def output(tile):
                act.wait_ge(y_full, 2 * tile + 2)
                nc.scalar.activation(y_nat[:, tile, 512:], ps[:, Y_BANKS[tile][1], :], ACT.Copy,
                                     scale=yr[:, tile:tile + 1]).then_inc(y_act, 1)

            def outputs(v0):
                for n in (12, 13, 14):
                    square(4, n, v0, "tile")
                token_std(0)
                output(0)
                output(1)
                square(4, 15, v0, "tile")
                token_std(1)
                for tile in (2, 3, 4):
                    output(tile)

            def mlp_group(g, layer, last):
                t0, g0, a0, v0, f0, norm = ((T_MLP0, G_MLP0, A_MLP0, V_MLP0, 0, 1),
                                            (T_MLP1, G_MLP1, A_MLP1, V_MLP1, 64, 3))[layer]

                def hidden_hi(n):
                    act.wait_ge(fs_done, f0 + 16 * g + n + 1)
                    k, half = 2 * (n // 4) + n % 2, n // 2 % 2
                    nc.scalar.activation(fH[:, k, half * HALF:(half + 1) * HALF], fs[:, n % 2, :], ACT.Copy).then_inc(fh_done, 1)

                for b in range(8):
                    if b < 4:
                        for n in range(4):
                            j = 4 * b + n
                            act.wait_ge(acc_full, g0 + 32 * g + j + 1)
                            if j >= 2:
                                act.wait_ge(fs_done, f0 + 16 * g + j - 1)
                            nc.scalar.activation(fr[:, j % 2, :], ps[:, n, 0:HALF], ACT.Relu).then_inc(act_free, 1)
                            if j:
                                hidden_hi(j - 1)
                            if layer == 0 and n in ADA_STEP:
                                (strips_out, add_bias)[ADA_STEP[n]](M_MLP + 6 * g + b)
                        if b == 3:
                            hidden_hi(15)
                    else:
                        if layer == 0 and b in MLP_PAIR:
                            strips_out(M_MLP + 6 * g + MLP_PAIR[b])
                            add_bias(M_MLP + 6 * g + MLP_PAIR[b])
                        if last and b == 7 and layer == 0:
                            last_tile(2, v0 + 16 * g, T_QKV + 1, 1, G_QKV)
                        elif last and b == 7:
                            outputs(v0 + 16 * g)
                        elif last:
                            for s in range(4 * (b - 4), 4 * (b - 3)):
                                square(norm + 1, s, v0 + 16 * g, "tile")
                    if not (last and (b == 7 or layer == 1 and b == 6)):
                        split(t0 + 8 * g + b + 2, b % 2, g0 + 32 * g + 4 * (b + 1))

            with act.Fori(0, FG - 1) as g:
                mlp_group(g, 0, False)
            mlp_group(FG - 1, 0, True)

            def rope_std(r):
                act.wait_ge(rss_done, r + 1)
                nc.scalar.activation(rss[:], rss[:], ACT.Sqrt, bias=eps[:], scale=1.0 / P).then_inc(rstd2, 1)

            def turned_out(r):
                for h in range(2):
                    act.wait_ge(tr_full, 3 * r + h + 1)
                    dst = kTa[:, h, 2 * P:] if r == 0 else qTa[:, 2 * (r - 1) + h, 0:LAT]
                    nc.scalar.activation(dst, ps[:, 4 + h, :], ACT.Copy).then_inc(tr_out, 1)
                act.wait_ge(tr_full, 3 * r + 3)
                if r == 0:
                    nc.scalar.activation(kTa[:, :, 0:2 * P], ps[:, 6, :].rearrange("p (h n) -> p h n", h=2),
                                         ACT.Copy).then_inc(tr_out, 1)
                else:
                    nc.scalar.activation(qTa[:, 2 * (r - 1):2 * r, LAT:T], ps[:, 6, 0:2 * P].rearrange("p (h n) -> p h n", h=2),
                                         ACT.Copy).then_inc(tr_out, 1)

            for t in range(6):
                for n in range(NT):
                    act.wait_ge(acc_full, G_QKV + 5 * t + n + 1)
                    if t == 0:
                        dst = k_nat[:, n, :]
                    elif t < 5:
                        if t > 2:
                            act.wait_ge(rn_done, t - 1)
                        dst = q_nat[:, (t - 1) % 2, n, :]
                    else:
                        dst = va[:, n, :]
                    nc.scalar.activation(dst, ps[:, NAT_BANKS[n], 0:RV], ACT.Copy).then_inc(act_free, 1)
                    if n == 1 and t:
                        rope_std(t - 1)
                    if n == 1 and t > 1:
                        turned_out(t - 2)
                split(T_QKV + t + 2, t % 2, G_QKV + 5 * (t + 1))
            turned_out(4)

            def att_exp(n):
                act.wait_ge(nmx_done, n + 1)
                if n >= 2:
                    act.wait_ge(pt_full, n - 1)
                if n >= KVH:
                    last = nc.scalar.activation(pr[:, n % 2, :].rearrange("p (a b) -> p a b", a=2),
                                                ps[:, 2 * (n % 2):2 * (n % 2) + 2, 0:HALF], ACT.Exp,
                                                bias=amx[:, n % 2, 0:1], scale=ATT_SCALE, accum_out=asum[:, n % 2, 0:1])
                else:
                    for j in range(GRP):
                        last = nc.scalar.activation(pr[:, n % 2, j * P:(j + 1) * P], ps[:, 2 * (n % 2), j * P:(j + 1) * P],
                                                    ACT.Exp, bias=amx[:, n % 2, j:j + 1], scale=ATT_SCALE,
                                                    accum_out=asum[:, n % 2, j:j + 1])
                last.then_inc(ex_done, 1)

            def att_turned(n):
                act.wait_ge(pt_full, n + 1)
                bank = ps[:, 4 if n % 2 == 0 else 7, :]
                if n == 0:
                    act.wait_ge(k_st, 16)
                m = n - KVH
                if m >= 0:
                    if m >= 4 and m % 4 == 0:
                        act.wait_ge(pv_full, m // 4 + 1)
                    nc.scalar.activation(pT[:, m // 4 % 2, 0:4, (m % 4) * P:(m % 4 + 1) * P],
                                         bank.rearrange("p (a b) -> p a b", a=4), ACT.Copy).then_inc(pt_act, 1)
                else:
                    nc.scalar.activation(pT[:, 1, n, :], bank, ACT.Copy).then_inc(pt_act, 1)

            def att_hi(v):
                act.wait_ge(pv_full, v + 1)
                if v >= KVH:
                    h = v - KVH
                    nc.scalar.activation(hH[:, h, 0:256], ps[:, 6, 0:256], ACT.Copy)
                    nc.scalar.activation(hH[:, h, 384:640], ps[:, 6, 256:512], ACT.Copy).then_inc(ah_done, 1)
                else:
                    nc.scalar.activation(hH[:, GRP * v:GRP * (v + 1), 256:384],
                                         ps[:, 6, :].rearrange("p (a b) -> p a b", a=GRP), ACT.Copy).then_inc(ah_done, 1)

            att_exp(0)
            att_exp(1)
            for n in range(N_ATT):
                att_turned(n)
                if n + 2 < N_ATT:
                    att_exp(n + 2)
                if n - 1 in VALUES_AT:
                    att_hi(VALUES_AT[n - 1])
            att_hi(KVH + QH - 1)

            for t in range(4):
                if t < 3:
                    for s in range(4 * t, 4 * t + 4):
                        square(3, s, V_WO, "tile")
                    split(T_WO + t + 2, t % 2, G_WO + 4 * (t + 1))
            last_tile(3, V_WO, T_MLP1 + 1, 1, G_MLP1)
            with act.Fori(0, FG - 1) as g:
                mlp_group(g, 1, False)
            mlp_group(FG - 1, 1, True)
        @block.gpsimd
        def _(pool):
            def lo(t, slot):
                for j in range(2):
                    pool.wait_ge(wh_done, 2 * t + j + 1)
                    cs = slice(j * 1024, (j + 1) * 1024)
                    nc.gpsimd.tensor_tensor(wL[:, slot, cs], raw[:, j, :], wH[:, slot, cs].bitcast(F32),
                                            ALU.subtract).then_inc(wl_done, 1)

            def h_lo(norm):
                for half in range(2):
                    for k in range(KC):
                        pool.wait_ge(hh_done, 16 * norm + 8 * half + k + 1)
                        cs = slice(half * HALF, (half + 1) * HALF)
                        nc.gpsimd.tensor_tensor(hL[:, k, cs], vb[:, k % 4, :], hH[:, k, cs].bitcast(F32),
                                                ALU.subtract).then_inc(h_ready, 1)

            lo(0, 0)
            h_lo(0)
            for t in range(4):
                lo(t + 1, (t + 1) % 2)
            with pool.Fori(0, 2) as i:
                for b in range(6):
                    lo(T_HEADS + 6 * i + b + 1, (b + 1) % 2)
            for t in range(T_WR + 1, T_MLP0 + 1):
                lo(t, t % 2)
            for norm, first, n_tiles in ((1, T_MLP0, 8 * FG), (2, T_QKV, 6 + 4), (3, T_MLP1, 8 * FG - 1)):
                h_lo(norm)
                with pool.Fori(0, n_tiles // 2) as i:
                    for j in range(2):
                        lo(first + 2 * i + j + 1, (j + 1) % 2)
            lo(N_TILES - 1, 1)
            pool.wait_ge(g_in, 16)
            for tile in range(NT):
                pool.wait_ge(y_act, tile + 1)
                nc.gpsimd.tensor_tensor(y_nat[:, tile, 512:], y_nat[:, tile, 512:], gfin[:, 512:], ALU.mult).then_inc(y_pool, 1)

        @block.vector
        def _(dve):
            def halfcols(half):
                return slice(half * HALF, (half + 1) * HALF)

            def residual(g, v0, n, half, k, gate_at):
                dve.wait_ge(acc_full, g + n + 1)
                for c0, w_, which in SEGS[half]:
                    x = xT[:, k, c0:c0 + w_]
                    last = nc.vector.scalar_tensor_tensor(out=x, in0=ps[:, n % 4, c0 - half * HALF:c0 - half * HALF + w_],
                                                          scalar=modT[:, gate_at + k, which:which + 1], in1=x,
                                                          op0=ALU.mult, op1=ALU.add)
                last.then_inc(dve_free, 1)

            def add_squares(norm, q, order):
                half, p_ = PAIRS[order][q]
                base = SUMS * norm
                dve.wait_ge(sq_done, 16 * norm + 2 * q + 2)
                out = ssum[:, half, :]
                if p_ == 0:
                    nc.vector.tensor_tensor(out, sqb[:, 0, :], sqb[:, 1, :], ALU.add).then_inc(sum_done, 1)
                else:
                    before = base + SUM_AT[order][q] - 2
                    dve.wait_ge(sum_done, before)
                    nc.vector.tensor_tensor(out, out, sqb[:, 0, :], ALU.add).then_inc(sum_done, 1)
                    dve.wait_ge(sum_done, before + 1)
                    nc.vector.tensor_tensor(out, out, sqb[:, 1, :], ALU.add).then_inc(sum_done, 1)

            def reciprocal_std(norm, half):
                dve.wait_ge(std_done, 2 * norm + half + 1)
                nc.vector.reciprocal(rstd[:, half, :], rstd[:, half, :]).then_inc(rstd_done, 1)
                dve.wait_ge(rstd_done, 2 * norm + half + 1)

            def h_values(norm, half, ks):
                i0 = 16 * norm + 8 * half

                def free(k):
                    if i0 + k >= 4:
                        dve.wait_ge(h_ready, i0 + k - 3)

                for k in ks:
                    free(k)
                    if k % 2 == 0:
                        nc.vector.tensor_tensor(vb[:, k % 4, :], xT[:, k, halfcols(half)], rstd[:, half, :],
                                                ALU.mult).then_inc(u_done, 1)
                        dve.wait_ge(u_done, (i0 + k) // 2 + 1)
                    for c0, w_, which in SEGS[half]:
                        a_ = c0 - half * HALF
                        v = vb[:, k % 4, a_:a_ + w_]
                        if k % 2 == 0:
                            last = nc.vector.tensor_scalar(v, v, coef[:, norm, k, which:which + 1],
                                                           modT[:, SHIFT_AT[norm] + k, which:which + 1], ALU.mult, ALU.add)
                        else:
                            last = nc.vector.scalar_tensor_tensor(out=v, in0=xT[:, k, c0:c0 + w_],
                                                                  scalar=coef[:, norm, k, which:which + 1],
                                                                  in1=rstd[:, half, a_:a_ + w_], op0=ALU.mult,
                                                                  op1=ALU.mult)
                    last.then_inc(v_done, 1)

            def coefficients(norm):
                scale_at = SCALE_AT[norm]
                dve.wait_ge(mod_done, (scale_at + KC - N_PRE) // 2) if norm else dve.wait_ge(pre_mod, 2)
                g = vecT[:, 0, R_NORM + KC * norm:R_NORM + KC * (norm + 1)]
                nc.vector.scalar_tensor_tensor(out=coef[:, norm], in0=modT[:, scale_at:scale_at + KC, :], scalar=1.0,
                                               in1=g[:, :, None].to_broadcast([P, KC, 2]), op0=ALU.add,
                                               op1=ALU.mult).then_inc(coef_done, 1)
                dve.wait_ge(coef_done, norm + 1)

            nc.vector.memset(ones[:], 1.0).then_inc(set_up, 1)
            nc.vector.memset(eps[:], EPS).then_inc(set_up, 1)
            nc.vector.memset(siluc[:], 0.0).then_inc(set_up, 1)
            dve.wait_ge(lg_raw, 1)
            nc.vector.tensor_scalar(lg[:], lg[:], -1.0, None, ALU.mult).then_inc(lg_done, 1)

            def pre_bias(j):
                dve.wait_ge(pre_fin, j + 1)
                m0 = 4 * PRE_ORDER[j]
                nc.vector.tensor_tensor(modT[:, m0:m0 + 4, :], ps[:, 6 + j % 2, 0:8].rearrange("p (a b) -> p a b", a=4),
                                        vecT[:, 1, m0:m0 + 4, None].to_broadcast([P, 4, 2]), ALU.add).then_inc(pre_mod, 1)

            dve.wait_ge(vec_in, 16)
            for n in range(16):
                dve.wait_ge(acc_full, n + 1)
                nc.vector.tensor_copy(xT[:, n % 8, halfcols(n // 8)], ps[:, n % 4, 0:HALF]).then_inc(dve_free, 1)
                if n % 2 == 1 and n > 1:
                    add_squares(0, n // 2 - 1, "half")
                if n in (9, 13):
                    pre_bias(n // 4 - 2)
            add_squares(0, 7, "half")
            pre_bias(2)
            for a_, b_ in ((0, PAD), (PAD + LAT, 2 * PAD + LAT), (ZW - PAD, ZW)):
                last = nc.vector.memset(zp[:, :, a_:b_], 0.0)
            last.then_inc(set_up, 1)
            coefficients(0)
            reciprocal_std(0, 0)
            pre_bias(3)
            dve.wait_ge(pre_mod, 4)
            h_values(0, 0, range(KC))
            reciprocal_std(0, 1)
            h_values(0, 1, range(KC))

            dve.wait_ge(act_free, 8)
            for t in range(2):
                for n in range(4):
                    half, ch = n // 2, 2 * t + n % 2
                    dve.wait_ge(acc_full, G_VAL + 4 * t + n + 1)
                    for c0, w_, which in SEGS[half]:
                        a_ = c0 - half * HALF
                        z0 = (2 * PAD + LAT + c0 - 256) if which else (PAD + c0 - (P if half else 0))
                        last = nc.vector.tensor_tensor(zp[:, ch, z0:z0 + w_], ps[:, n, a_:a_ + w_],
                                                       sgate[:, ch, c0:c0 + w_], ALU.mult)
                    last.then_inc(dve_free, 1)

            dve.wait_ge(set_up, 4)
            dve.wait_ge(dve_free, V_WR)
            with dve.Fori(0, 2) as i:
                def taps(w0, w1, chs=(0, 1)):
                    for w in range(w0, w1):
                        for ch in chs:
                            src = zp[:, bass.ds(2 * i + ch, 1), w:w + CW].rearrange("p a n -> p (a n)")
                            acc = cacc[:, bass.ds(2 * i + ch, 1), :].rearrange("p a n -> p (a n)")
                            wt = vecT[:, 2, bass.ds(2 * i + 4 * w + ch, 1)]
                            if w == 0:
                                nc.vector.tensor_scalar(acc, src, wt, vecT[:, 0, bass.ds(R_CB + 2 * i + ch, 1)],
                                                        ALU.mult, ALU.add).then_inc(conv_done, 1)
                            else:
                                dve.wait_ge(conv_done, 2 * WIDTH * i + 2 * w + ch - 1)
                                nc.vector.scalar_tensor_tensor(out=acc, in0=src, scalar=wt, in1=acc, op0=ALU.mult,
                                                               op1=ALU.add).then_inc(conv_done, 1)

                for e in range(2):
                    head = 2 * i + e
                    cuts = ((0, 13, 19, 21), (22, 22, 28, 30))[e]
                    taps(*cuts[0:2])
                    dve.wait_ge(dexp_done, 4 * head + 4)
                    nc.vector.tensor_tensor(dmat[:, 0, :], dmat[:, 0, :], dmat[:, 1, :], ALU.mult).then_inc(dm_done, 1)
                    dve.wait_ge(act_free, A_HEADS + G_PAIR * i + 4)
                    for r in range(2):
                        for c0 in (0, 384):
                            nc.vector.scalar_tensor_tensor(
                                out=qdec[:, r, c0:c0 + 256].rearrange("p (a b) -> p a b", a=2),
                                in0=qT[:, e, c0:c0 + 256].rearrange("p (a b) -> p a b", a=2), scalar=RET_SCALE,
                                in1=qtab[:, r, None, :].to_broadcast([P, 2, P]), op0=ALU.mult,
                                op1=ALU.mult).then_inc(qdec_done, 1)
                    dve.wait_ge(dm_done, 2 * head + 1)
                    nc.vector.tensor_tensor(dmat[:, 0, :], dmat[:, 0, :], ident, ALU.add).then_inc(dm_done, 1)
                    dve.wait_ge(dm_done, 2 * head + 2)
                    dve.wait_ge(st_full, 3 * head + 2)
                    for a_, b_ in ((0, 0), (3, 2)):
                        last = nc.vector.scalar_tensor_tensor(
                            out=prob[:, a_ * P:(a_ + 2) * P].rearrange("p (a b) -> p a b", a=2),
                            in0=ps[:, 5, b_ * P:(b_ + 2) * P].rearrange("p (a b) -> p a b", a=2), scalar=RET_SCALE,
                            in1=dmat[:, 0, None, :].to_broadcast([P, 2, P]), op0=ALU.mult, op1=ALU.mult)
                    last.then_inc(prob_done, 1)
                    nc.vector.scalar_tensor_tensor(out=prob[:, 2 * P:3 * P], in0=ps[:, 7, 0:P], scalar=RET_SCALE,
                                                   in1=dmat[:, 0, :], op0=ALU.mult, op1=ALU.mult).then_inc(prob_done, 1)
                    taps(*cuts[1:3])
                    dve.wait_ge(s0_in, 32 * (head + 1))
                    dve.wait_ge(dec_done, 3)

                    def advance(r, n, to, bank, at, count):
                        if count:
                            dve.wait_ge(s_done, 6 * head + count)
                        nc.vector.scalar_tensor_tensor(out=S[:, r, to, :], in0=S[:, r, n, :],
                                                       scalar=cdec[:, r, bass.ds(head, 1)], in1=ps[:, bank, at:at + RV],
                                                       op0=ALU.mult, op1=ALU.add).then_inc(s_done, 1)

                    dve.wait_ge(u_full, 4 * head + 1)
                    advance(0, 0, 1, 5, 0, 0)
                    advance(0, 1, 2, 5, RV, 1)
                    dve.wait_ge(u_full, 4 * head + 2)
                    advance(0, 2, 3, 6, 0, 2)
                    dve.wait_ge(act_dma, 16 * (head + 1))
                    nc.vector.tensor_copy(state_out[:, 0, :], ps[:, 6, RV:2 * RV]).then_inc(so_done, 1)
                    dve.wait_ge(u_full, 4 * head + 3)
                    advance(1, 3, 2, 7, 0, 3)
                    advance(1, 2, 1, 7, RV, 4)
                    dve.wait_ge(u_full, 4 * head + 4)
                    advance(1, 1, 0, 5, 0, 5)
                    nc.vector.tensor_copy(state_out[:, 1, :], ps[:, 5, RV:2 * RV]).then_inc(so_done, 1)
                    taps(*cuts[2:4])
                    hc = bass.ds(512 * i + 256 * e, RV)
                    for n in range(NT):
                        dve.wait_ge(o_out, 3 * head + n // 2 + 1)
                        nc.vector.bn_stats(bst[:, n, :], ret[:, n, hc]).then_inc(bn_done, 1)
                    dve.wait_ge(bn_done, 10 * head + 5)
                    taps(cuts[3], cuts[3] + 1, (0,))
                    for n in range(NT):
                        nc.vector.bn_aggr(bmv[:, n, :], bst[:, n, :]).then_inc(bn_done, 1)
                    taps(cuts[3], cuts[3] + 1, (1,))
                    dve.wait_ge(bstd_done, head + 1)
                    nc.vector.reciprocal(brs[:, :, 0], brs[:, :, 0]).then_inc(brs_done, 1)
                    dve.wait_ge(brs_done, head + 1)
                    for n in range(NT):
                        nc.vector.tensor_scalar(ret[:, n, hc], ret[:, n, hc], bmv[:, n, 0:1], brs[:, n, 0:1],
                                                ALU.subtract, ALU.mult).then_inc(on_done, 1)
                    dve.wait_ge(act_free, A_HEADS + G_PAIR * i + 18 + 10 * e)
                    for n in range(NT):
                        dve.wait_ge(on_done, NT * head + n + 1)
                        last = nc.vector.tensor_tensor(ret[:, n, hc], ret[:, n, hc], gate[:, n, :], ALU.mult)
                    last.then_inc(ret_done, 1)

            def compact(ch):
                return ((cacc[:, ch, 0:LAT], slice(0, LAT)), (cacc[:, ch, LAT + PAD:CW], slice(LAT, T)))

            for n in range(16):
                dve.wait_ge(rth_done, n + 1)
                cs = halfcols(n // 8)
                nc.vector.tensor_tensor(hL[:, n % 8, cs], ps[:, 4 + n % 4, 0:HALF], hH[:, n % 8, cs].bitcast(F32),
                                        ALU.subtract).then_inc(rtl_done, 1)

            dve.wait_ge(conv_done, 4 * WIDTH)
            for src, cs in compact(0):
                other = dict((c.start, s) for s, c in compact(1))[cs.start]
                last = nc.vector.tensor_tensor(cst[:, 0, cs], src, other, ALU.add)
            last.then_inc(cn_sum, 1)
            for ch in (2, 3):
                dve.wait_ge(cn_sum, ch - 1)
                for src, cs in compact(ch):
                    last = nc.vector.tensor_tensor(cst[:, 0, cs], cst[:, 0, cs], src, ALU.add)
                last.then_inc(cn_sum, 1)
            dve.wait_ge(cn_sum, 3)
            nc.vector.tensor_scalar(cst[:, 0, :], cst[:, 0, :], 1.0 / CONV, None, ALU.mult).then_inc(cstat_in, 1)

            def wr(n):
                t, m = n // 4, n % 4
                residual(G_WR, V_WR, n, m // 2, 2 * t + m % 2, G1)

            dve.wait_ge(mod_done, M_MLP)
            wr(0)
            wr(1)
            dve.wait_ge(cstat_full, 1)
            for ch in range(CC):
                for (src, cs), bank in zip(compact(ch), (5, 6)):
                    last = nc.vector.tensor_tensor(src, src, ps[:, bank, 0:cs.stop - cs.start], ALU.subtract)
                last.then_inc(cx_done, 1)
            for n in range(2, 5):
                wr(n)
            dve.wait_ge(csq_done, 2)
            nc.vector.tensor_tensor(cst[:, 1, :], cmp_[:, 0, :], cmp_[:, 1, :], ALU.add).then_inc(csum_done, 2)
            for ch in (2, 3):
                dve.wait_ge(csq_done, ch + 1)
                dve.wait_ge(csum_done, ch)
                nc.vector.tensor_tensor(cst[:, 1, :], cst[:, 1, :], cmp_[:, ch % 2, :], ALU.add).then_inc(
                    csum_done if ch == 2 else cstat_in, 1)
            for n in range(5, 10):
                wr(n)
            dve.wait_ge(cstd_done, 1)
            nc.vector.reciprocal(cmp_[:, 0, :], cmp_[:, 0, :]).then_inc(crec_done, 1)
            dve.wait_ge(crec_done, 1)
            for ch in range(CC):
                dve.wait_ge(cx_done, ch + 1)
                for src, cs in compact(ch):
                    last = nc.vector.tensor_tensor(src, src, cmp_[:, 0, cs], ALU.mult)
                last.then_inc(cn_done, 1)
            for n in range(10, 13):
                wr(n)
            for ch in range(CC):
                dve.wait_ge(ch_done, ch + 1)
                for a_, b_, n_ in CONV_MAP:
                    last = nc.vector.tensor_tensor(cL[:, ch, b_:b_ + n_], cacc[:, ch, a_:a_ + n_],
                                                   cH[:, ch, b_:b_ + n_].bitcast(F32), ALU.subtract)
                last.then_inc(cl_done, 2)
            for n in range(13, 16):
                wr(n)
            coefficients(1)

            def last_tile(norm, order, update, first):
                update(first)
                update(first + 1)
                add_squares(norm, first // 2, order)
                reciprocal_std(norm, 0)
                h_values(norm, 0, range(0, 2))
                update(first + 2)
                h_values(norm, 0, range(2, 4))
                update(first + 3)
                add_squares(norm, first // 2 + 1, order)
                h_values(norm, 0, range(4, 8))
                reciprocal_std(norm, 1)
                h_values(norm, 1, range(KC))

            def wc(n):
                t, m = n // 8, n % 8
                residual(G_WC, V_WC, n, m // 4, 4 * t + m % 4, G1)

            for n in range(12):
                wc(n)
                if n % 2 == 1:
                    add_squares(1, n // 2, "wc")
            wc(12)
            wc(13)
            reciprocal_std(1, 0)
            h_values(1, 0, range(0, 4))
            add_squares(1, 6, "wc")
            wc(14)
            wc(15)
            h_values(1, 0, range(4, 6))
            add_squares(1, 7, "wc")
            h_values(1, 0, range(6, 8))
            reciprocal_std(1, 1)
            h_values(1, 1, range(KC))

            def mlp_group(g, layer, last):
                g0, a0, v0, f0, norm, gate_at = ((G_MLP0, A_MLP0, V_MLP0, 0, 1, G2),
                                                 (G_MLP1, A_MLP1, V_MLP1, 64, 3, MOD1 + G2))[layer]

                def hidden_lo(n):
                    dve.wait_ge(fh_done, f0 + 16 * g + n + 1)
                    k, half = 2 * (n // 4) + n % 2, n // 2 % 2
                    nc.vector.tensor_tensor(fL[:, k, halfcols(half)], fs[:, n % 2, :], fH[:, k, halfcols(half)].bitcast(F32),
                                            ALU.subtract).then_inc(f_ready, 1)

                for n in range(16):
                    dve.wait_ge(act_free, a0 + 16 * g + n + 1)
                    if n >= 2:
                        dve.wait_ge(f_ready, f0 + 16 * g + n - 1)
                    nc.vector.tensor_tensor(fs[:, n % 2, :], fr[:, n % 2, :], fr[:, n % 2, :], ALU.mult).then_inc(fs_done, 1)
                    if n:
                        hidden_lo(n - 1)
                hidden_lo(15)

                def update(n):
                    b, m = n // 4, n % 4
                    residual(g0 + 32 * g + 16, v0, n, m // 2, 2 * b + m % 2, gate_at)

                for n in range(12 if last else 16):
                    update(n)
                    if last and n % 2 == 1:
                        add_squares(norm + 1, n // 2, "tile")
                return update

            with dve.Fori(0, FG - 1) as g:
                mlp_group(g, 0, False)
            update = mlp_group(FG - 1, 0, True)
            dve.wait_ge(mod_done, M_MLP + 6 * FG)
            coefficients(2)
            last_tile(2, "tile", update, 12)
            coefficients(3)

            dve.wait_ge(att_in, 16 * 3)
            for qk in range(2):
                for j, (cs_, par) in enumerate(((0, 0), (1, 1), (1, 0), (0, 1))):
                    last = nc.vector.tensor_tensor(tabs[:, qk, j], rope_sb[:, cs_],
                                                   gqk[:, qk, None, par::2].to_broadcast([P, NT, 64]), ALU.mult)
            last.then_inc(tab_done, 1)
            dve.wait_ge(tab_done, 1)

            def rope(r):
                src = k_nat[:] if r == 0 else q_nat[:, (r - 1) % 2]
                out = kro if r == 0 else qro
                tab = tabs[:, 1 if r == 0 else 0]
                dve.wait_ge(act_free, A_QKV + 5 * r + 5)
                nc.vector.tensor_tensor(rn[:], src, src, ALU.mult).then_inc(rsq_done, 1)
                dve.wait_ge(rsq_done, r + 1)
                nc.vector.tensor_reduce(rss[:], rn[:].rearrange("p n (h d) -> p (n h) d", h=2), AX_X,
                                        ALU.add).then_inc(rss_done, 1)
                dve.wait_ge(rstd2, r + 1)
                nc.vector.reciprocal(rss[:], rss[:]).then_inc(rrec, 1)
                dve.wait_ge(rrec, r + 1)
                nc.vector.tensor_tensor(rn[:].rearrange("p n (h d) -> p (n h) d", h=2),
                                        src.rearrange("p n (h d) -> p (n h) d", h=2),
                                        rss[:, :, None].to_broadcast([P, 2 * NT, P]), ALU.mult).then_inc(rn_done, 1)
                dve.wait_ge(rn_done, r + 1)
                if r > 1:
                    dve.wait_ge(tr_full, 3 * r)
                x = [rn[:].rearrange("p n (h d) -> p n h d", h=2)[..., par::2] for par in range(2)]
                y = [out[:].rearrange("p n (h d) -> p n h d", h=2)[..., par::2] for par in range(2)]
                for j, (dst, a_) in enumerate(((y[0], 0), (rtmp[:, 0], 1), (y[1], 0), (rtmp[:, 1], 1))):
                    nc.vector.tensor_tensor(dst, x[a_], tab[:, j, :, None, :].to_broadcast([P, NT, 2, 64]),
                                            ALU.mult).then_inc(rm_done, 1)
                for j in range(2):
                    dve.wait_ge(rm_done, 4 * r + 2 * j + 2)
                    nc.vector.tensor_tensor(y[j], y[j], rtmp[:, j], ALU.add if j else ALU.subtract).then_inc(ro_done, 1)

            for r in range(5):
                rope(r)

            def att_max(n):
                dve.wait_ge(sc_full, n + 1)
                if n >= 2:
                    dve.wait_ge(ex_done, n - 1)
                if n >= KVH:
                    m = amx[:, n % 2, 0:1]
                    nc.vector.tensor_reduce(m, ps[:, 2 * (n % 2):2 * (n % 2) + 2, 0:HALF], mybir.AxisListType.XY,
                                            ALU.max).then_inc(mx_done, 1)
                else:
                    m = amx[:, n % 2, :]
                    nc.vector.tensor_reduce(m, ps[:, 2 * (n % 2), :].rearrange("p (a b) -> p a b", a=GRP), AX_X,
                                            ALU.max).then_inc(mx_done, 1)
                dve.wait_ge(mx_done, n + 1)
                nc.vector.tensor_scalar(m, m, -ATT_SCALE, None, ALU.mult).then_inc(nmx_done, 1)

            def att_normalise(n):
                dve.wait_ge(ex_done, n + 1)
                w_ = 1 if n >= KVH else GRP
                s = asum[:, n % 2, 0:w_]
                nc.vector.reciprocal(s, s).then_inc(rc_done, 1)
                dve.wait_ge(rc_done, n + 1)
                if w_ == 1:
                    nc.vector.tensor_scalar(pr[:, n % 2, :], pr[:, n % 2, :], s, None, ALU.mult).then_inc(pn_done, 1)
                else:
                    p_ = pr[:, n % 2, 0:512].rearrange("p (a b) -> p a b", a=GRP)
                    nc.vector.tensor_tensor(p_, p_, s[:, :, None].to_broadcast([P, GRP, P]), ALU.mult).then_inc(pn_done, 1)

            def att_lo(v):
                dve.wait_ge(ah_done, v + 1)
                if v >= KVH:
                    h = v - KVH
                    for a_, b_ in ((0, 0), (384, 256)):
                        last = nc.vector.tensor_tensor(hL[:, h, a_:a_ + 256], ps[:, 6, b_:b_ + 256],
                                                       hH[:, h, a_:a_ + 256].bitcast(F32), ALU.subtract)
                else:
                    hs = slice(GRP * v, GRP * (v + 1))
                    last = nc.vector.tensor_tensor(hL[:, hs, 256:384], ps[:, 6, :].rearrange("p (a b) -> p a b", a=GRP),
                                                   hH[:, hs, 256:384].bitcast(F32), ALU.subtract)
                last.then_inc(attn_ready, 1)

            def att_last_out(m):
                dve.wait_ge(pt_full, KVH + m + 1)
                if m >= 4 and m % 4 == 0:
                    dve.wait_ge(pv_full, m // 4 + 1)
                nc.vector.tensor_copy(pT[:, m // 4 % 2, 4, (m % 4) * P:(m % 4 + 1) * P], ps[:, 5, 0:P]).then_inc(pt_dve, 1)

            att_max(0)
            att_max(1)
            for n in range(N_ATT):
                att_normalise(n)
                if n > KVH:
                    att_last_out(n - KVH - 1)
                if n + 2 < N_ATT:
                    att_max(n + 2)
                if n - 2 in VALUES_AT:
                    att_lo(VALUES_AT[n - 2])
            att_last_out(4 * QH - 1)
            att_lo(KVH + QH - 1)

            def wo(n):
                t, m = n // 4, n % 4
                residual(G_WO, V_WO, n, m // 2, 2 * t + m % 2, MOD1 + G1)

            for n in range(12):
                wo(n)
                if n % 2 == 1:
                    add_squares(3, n // 2, "tile")
            last_tile(3, "tile", wo, 12)

            with dve.Fori(0, FG - 1) as g:
                mlp_group(g, 1, False)
            update = mlp_group(FG - 1, 1, True)

            def token_rstd(part):
                dve.wait_ge(std_done, 8 + part + 1)
                rs = yr[:, Y_TILES[part][0]:Y_TILES[part][-1] + 1]
                nc.vector.reciprocal(rs, rs).then_inc(rstd_done, 1)
                dve.wait_ge(rstd_done, 8 + part + 1)

            def output(tile):
                dve.wait_ge(y_full, 2 * tile + 1)
                nc.vector.scalar_tensor_tensor(out=y_nat[:, tile, 0:512], in0=ps[:, Y_BANKS[tile][0], :],
                                               scalar=yr[:, tile:tile + 1], in1=gfin[:, 0:512], op0=ALU.mult,
                                               op1=ALU.mult).then_inc(y_dve, 1)

            update(12)
            update(13)
            add_squares(4, 6, "tile")
            update(14)
            dve.wait_ge(g_in, 16)
            token_rstd(0)
            output(0)
            output(1)
            update(15)
            add_squares(4, 7, "tile")
            token_rstd(1)
            for tile in (2, 3, 4):
                output(tile)


_INS = ["x_prompt", "x_sample", "state_ret", "cache_k", "cache_v", "ada_w", "even_w_in", "even_w_out", "final_g",
        "ret_log_decay", "odd_w_qkv", "odd_q_g", "odd_k_g", "odd_w_o", "mlp_w1", "mlp_w2"]
_OUTS = [("y_prompt", (1, CTX, D)), ("y_sample", (1, LAT, D)), ("new_state", (1, 1, 2, RH, P, RV)),
         ("new_k", (1, 1, CTX, KVH, P)), ("new_v", (1, 1, CTX, KVH, P))]


def kernel(**inputs):
    import concourse.bacc as bacc
    from concourse.bass_utils import run_bass_kernel_spmd

    nc = bacc.Bacc("TRN2", target_bir_lowering=False, num_devices=1)
    shape_const, rope_const = shape_constants()
    arrays, args = {}, []
    given = [(name, inputs[name]) for name in _INS] + [("feature_vectors", by_feature_chunk(inputs)),
                                                       ("shape_const", shape_const), ("rope_const", rope_const)]
    for name, a in given:
        a = np.ascontiguousarray(a)
        arrays[f"in_{name}"] = a
        args.append(nc.dram_tensor(f"in_{name}", a.shape, mybir.dt.from_np(a.dtype), kind="ExternalInput").ap())
    for name, shape in _OUTS:
        args.append(nc.dram_tensor(f"out_{name}", shape, F32, kind="ExternalOutput").ap())
    hybrid_step(nc, *args)
    r = run_bass_kernel_spmd(nc, [arrays], core_ids=[0])
    return tuple(r.results[0][f"out_{name}"] for name, _ in _OUTS)
```
